# Optimizing a Trainium2 kernel written in Bass

```python
import jax, jax.numpy as jnp
from jax import lax
import numpy as np
import math

D_MODEL = 1024
BATCH = 1
SEQ = 512
DEPTH = 2

EPS_RMS = 1e-6
EPS_LN = 1e-5
W_CONV = D_MODEL
CONV_K = 31
W_POOL = D_MODEL
POOL_WINDOWS = (2, 4, 8, 16)
POOL_GROUPS = len(POOL_WINDOWS)
POOL_GW = W_POOL // POOL_GROUPS
W_EVEN_IN = 3 * W_CONV + 2 * W_POOL
W_EVEN_MIX = W_CONV + W_POOL
LRU_HEADS = 12
LRU_HD = 128
W_LRU = LRU_HEADS * LRU_HD
LRU_CONV_K = 4
LRU_C = 8.0
N_EVEN = (DEPTH + 1) // 2
N_ODD = DEPTH // 2


def rmsnorm(x, g):
    xf = x.astype(jnp.float32)
    y = xf * lax.rsqrt(jnp.mean(xf * xf, axis=-1, keepdims=True) + EPS_RMS)
    return (y * g.astype(jnp.float32)).astype(x.dtype)

def layernorm(x, g, b):
    xf = x.astype(jnp.float32)
    mu = jnp.mean(xf, axis=-1, keepdims=True)
    var = jnp.mean(jnp.square(xf - mu), axis=-1, keepdims=True)
    y = (xf - mu) * lax.rsqrt(var + EPS_LN)
    return (y * g.astype(jnp.float32) + b.astype(jnp.float32)).astype(x.dtype)

def causal_depthwise_conv(x, w, b):
    k = w.shape[0]
    y = lax.conv_general_dilated(
        x, w[:, None, :].astype(x.dtype), window_strides=(1,), padding=[(k - 1, 0)],
        dimension_numbers=("NWC", "WIO", "NWC"), feature_group_count=x.shape[-1])
    return y + b.astype(x.dtype)

def multiscale_pool_diff(v):
    bsz, t, _ = v.shape
    vf = v.astype(jnp.float32)
    cs_pad = jnp.pad(jnp.cumsum(vf, axis=1), ((0, 0), (1, 0), (0, 0)))
    pos = jnp.arange(1, t + 1, dtype=jnp.float32)
    outs = []
    for g, w in enumerate(POOL_WINDOWS):
        seg = cs_pad[:, :, g * POOL_GW:(g + 1) * POOL_GW]
        upper = seg[:, 1:]
        lower = jnp.pad(seg[:, :t - w + 1], ((0, 0), (w - 1, 0), (0, 0)))
        cnt = jnp.minimum(pos, jnp.float32(w))[None, :, None]
        outs.append((upper - lower) / cnt)
    return jnp.concatenate(outs, axis=-1) - vf

def even_mixer(h, w_in, conv_w, conv_b, ln_g, ln_b, pool_w, pool_b, pool_scale, w_out):
    bsz, t, _ = h.shape
    p = jnp.einsum("btd,dn->btn", h, w_in)
    a_val, a_glu, a_gate, b_val, b_gate = jnp.split(
        p, [W_CONV, 2 * W_CONV, 3 * W_CONV, 3 * W_CONV + W_POOL], axis=-1)
    u = a_val * jax.nn.sigmoid(a_glu)
    u = causal_depthwise_conv(u, conv_w, conv_b)
    u = jax.nn.silu(layernorm(u, ln_g, ln_b))
    ya = u * jax.nn.silu(a_gate)
    d = multiscale_pool_diff(b_val).reshape(bsz, t, POOL_GROUPS, POOL_GW)
    d = jnp.einsum("btgc,gce->btge", d, pool_w.astype(jnp.float32)) + pool_b.astype(jnp.float32)
    yb = (d.reshape(bsz, t, W_POOL) * pool_scale.astype(jnp.float32)).astype(h.dtype)
    yb = yb * jax.nn.silu(b_gate)
    y = jnp.concatenate([ya, yb], axis=-1)
    return jnp.einsum("btn,nd->btd", y, w_out)

def _lin_combine(c1, c2):
    a1, b1 = c1
    a2, b2 = c2
    return a1 * a2, a2 * b1 + b2

def odd_mixer(h, w_in, conv_w, conv_b, w_rg, b_rg, w_ig, b_ig, lam, w_out):
    bsz, t, _ = h.shape
    p = jnp.einsum("btd,dn->btn", h, w_in)
    xr, gate = jnp.split(p, [W_LRU], axis=-1)
    xc = causal_depthwise_conv(xr, conv_w, conv_b)
    xh = xc.reshape(bsz, t, LRU_HEADS, LRU_HD)
    r = jax.nn.sigmoid(jnp.einsum("bthi,hij->bthj", xh, w_rg).reshape(bsz, t, W_LRU).astype(jnp.float32)
                       + b_rg.astype(jnp.float32))
    i = jax.nn.sigmoid(jnp.einsum("bthi,hij->bthj", xh, w_ig).reshape(bsz, t, W_LRU).astype(jnp.float32)
                       + b_ig.astype(jnp.float32))
    log_a = -LRU_C * r * jax.nn.softplus(-lam.astype(jnp.float32))
    a = jnp.exp(log_a)
    mult = jnp.sqrt(-jnp.expm1(2.0 * log_a))
    bterm = mult * (i * xc.astype(jnp.float32))
    _, hs = lax.associative_scan(_lin_combine, (a, bterm), axis=1)
    y = hs.astype(h.dtype) * jax.nn.silu(gate)
    return jnp.einsum("btn,nd->btd", y, w_out)

def first_inputs(seed: int = 0) -> dict:
    key = jax.random.key(seed)
    ks = iter(jax.random.split(key, 32))
    f32 = jnp.float32

    def nrm(shape, scale):
        return jax.random.normal(next(ks), shape, f32) * scale

    x = jax.random.normal(next(ks), (BATCH, SEQ, D_MODEL), f32)
    a0 = jax.random.uniform(next(ks), (N_ODD, W_LRU), f32, 0.9, 0.999)
    s = a0 ** (1.0 / LRU_C)
    lru_lambda = jnp.log(s) - jnp.log1p(-s)
    return {
        "x": x,
        "norm_even": 1.0 + nrm((N_EVEN, D_MODEL), 0.02),
        "w_in_even": nrm((N_EVEN, D_MODEL, W_EVEN_IN), D_MODEL ** -0.5),
        "conv_a_w": nrm((N_EVEN, CONV_K, W_CONV), CONV_K ** -0.5),
        "conv_a_b": nrm((N_EVEN, W_CONV), 0.01),
        "ln_a_g": 1.0 + nrm((N_EVEN, W_CONV), 0.02),
        "ln_a_b": nrm((N_EVEN, W_CONV), 0.01),
        "pool_w": nrm((N_EVEN, POOL_GROUPS, POOL_GW, POOL_GW), POOL_GW ** -0.5),
        "pool_b": nrm((N_EVEN, POOL_GROUPS, POOL_GW), 0.01),
        "pool_scale": 1.0 + nrm((N_EVEN, W_POOL), 0.1),
        "w_out_even": nrm((N_EVEN, W_EVEN_MIX, D_MODEL), W_EVEN_MIX ** -0.5),
        "norm_odd": 1.0 + nrm((N_ODD, D_MODEL), 0.02),
        "w_in_odd": nrm((N_ODD, D_MODEL, 2 * W_LRU), D_MODEL ** -0.5),
        "conv_c_w": nrm((N_ODD, LRU_CONV_K, W_LRU), LRU_CONV_K ** -0.5),
        "conv_c_b": nrm((N_ODD, W_LRU), 0.01),
        "w_rg": nrm((N_ODD, LRU_HEADS, LRU_HD, LRU_HD), LRU_HD ** -0.5),
        "b_rg": nrm((N_ODD, W_LRU), 0.01),
        "w_ig": nrm((N_ODD, LRU_HEADS, LRU_HD, LRU_HD), LRU_HD ** -0.5),
        "b_ig": nrm((N_ODD, W_LRU), 0.01),
        "lru_lambda": lru_lambda,
        "w_out_odd": nrm((N_ODD, W_LRU, D_MODEL), W_LRU ** -0.5),
        "final_norm": 1.0 + nrm((D_MODEL,), 0.02),
    }

def first_block(x, norm_even, w_in_even, conv_a_w, conv_a_b, ln_a_g, ln_a_b, pool_w, pool_b,
              pool_scale, w_out_even, norm_odd, w_in_odd, conv_c_w, conv_c_b, w_rg, b_rg,
              w_ig, b_ig, lru_lambda, w_out_odd, final_norm):
    h = x
    for layer in range(DEPTH):
        if layer % 2 == 0:
            j = layer // 2
            h = h + even_mixer(rmsnorm(h, norm_even[j]), w_in_even[j], conv_a_w[j], conv_a_b[j],
                               ln_a_g[j], ln_a_b[j], pool_w[j], pool_b[j], pool_scale[j],
                               w_out_even[j])
        else:
            j = layer // 2
            h = h + odd_mixer(rmsnorm(h, norm_odd[j]), w_in_odd[j], conv_c_w[j], conv_c_b[j],
                              w_rg[j], b_rg[j], w_ig[j], b_ig[j], lru_lambda[j], w_out_odd[j])
    return rmsnorm(h, final_norm)


N_A_LAYERS = DEPTH // 2
N_B_LAYERS = DEPTH - N_A_LAYERS
SSM_GROUP = 16
SSM_GROUPS = D_MODEL // SSM_GROUP
SSM_STATE = 64
SSM_CHUNK = 128
DT_MIN = 1e-3
DT_MAX = 1e-1
HEAD_DIM = 64
N_HEADS = D_MODEL // HEAD_DIM
N_KV_HEADS = N_HEADS // 4
GQA_GROUP = N_HEADS // N_KV_HEADS
WINDOW = 128
ATTN_BLOCK = 128
ROPE_THETA = 500000.0
ROT_DIM = HEAD_DIM // 4
D_FF = 4 * D_MODEL
PLE_DIM = 256
RMS_EPS = 1e-6
NEG_INF = -1e30


def rmsnorm_2(x, g):
    xf = x.astype(jnp.float32)
    y = xf * lax.rsqrt(jnp.mean(xf * xf, axis=-1, keepdims=True) + RMS_EPS)
    return (y * g.astype(jnp.float32)).astype(x.dtype)

def partial_rope(x, pos):
    inv = ROPE_THETA ** (-jnp.arange(0, ROT_DIM, 2, dtype=jnp.float32) / ROT_DIM)
    ang = pos.astype(jnp.float32)[:, None] * inv[None, :]
    cos = jnp.cos(ang)[None, :, None, :]
    sin = jnp.sin(ang)[None, :, None, :]
    xr = x[..., :ROT_DIM].astype(jnp.float32)
    x1, x2 = xr[..., :ROT_DIM // 2], xr[..., ROT_DIM // 2:]
    rot = jnp.concatenate([x1 * cos - x2 * sin, x2 * cos + x1 * sin], axis=-1).astype(x.dtype)
    return jnp.concatenate([rot, x[..., ROT_DIM:]], axis=-1)

def s5_mixer(u, lam_re, lam_im, log_dt, b_re, b_im, c_re, c_im, d, w_glu):
    bsz, seqlen, dm = u.shape
    f32 = jnp.float32
    lam_re = lam_re.astype(f32); lam_im = lam_im.astype(f32)
    b_re = b_re.astype(f32); b_im = b_im.astype(f32)
    c_re = c_re.astype(f32); c_im = c_im.astype(f32)
    dt = jnp.exp(log_dt.astype(f32))[:, None]
    mag = jnp.exp(lam_re * dt)
    a_r = mag * jnp.cos(lam_im * dt)
    a_i = mag * jnp.sin(lam_im * dt)
    den = lam_re * lam_re + lam_im * lam_im
    nr = a_r - 1.0
    coef_r = (nr * lam_re + a_i * lam_im) / den
    coef_i = (a_i * lam_re - nr * lam_im) / den
    bb_r = coef_r[..., None] * b_re - coef_i[..., None] * b_im
    bb_i = coef_r[..., None] * b_im + coef_i[..., None] * b_re

    n_chunks = seqlen // SSM_CHUNK
    ug = u.astype(f32).reshape(bsz, n_chunks, SSM_CHUNK, SSM_GROUPS, SSM_GROUP)
    ug = jnp.transpose(ug, (1, 0, 2, 3, 4))

    def combine(e1, e2):
        a1r, a1i, s1r, s1i = e1
        a2r, a2i, s2r, s2i = e2
        return (a2r * a1r - a2i * a1i,
                a2r * a1i + a2i * a1r,
                a2r * s1r - a2i * s1i + s2r,
                a2r * s1i + a2i * s1r + s2i)

    def chunk_step(carry, uc):
        cr, ci = carry
        bur = jnp.einsum('gnh,btgh->btgn', bb_r, uc)
        bui = jnp.einsum('gnh,btgh->btgn', bb_i, uc)
        ar = jnp.broadcast_to(a_r, bur.shape)
        ai = jnp.broadcast_to(a_i, bui.shape)
        pr, pi, sr, si = lax.associative_scan(combine, (ar, ai, bur, bui), axis=1)
        xr = sr + pr * cr[:, None] - pi * ci[:, None]
        xi = si + pr * ci[:, None] + pi * cr[:, None]
        y = jnp.einsum('ghn,btgn->btgh', c_re, xr) - jnp.einsum('ghn,btgn->btgh', c_im, xi)
        return (xr[:, -1], xi[:, -1]), y

    init = (jnp.zeros((bsz, SSM_GROUPS, SSM_STATE), f32), jnp.zeros((bsz, SSM_GROUPS, SSM_STATE), f32))
    _, ys = lax.scan(chunk_step, init, ug)
    y = jnp.transpose(ys, (1, 0, 2, 3, 4)).reshape(bsz, seqlen, dm)
    y = y + d.astype(f32) * u.astype(f32)
    y = jax.nn.gelu(y).astype(u.dtype)
    ab = y @ w_glu
    a, b = ab[..., :dm], ab[..., dm:]
    return a * jax.nn.sigmoid(b)

def swa_sink_attention(q, k, v, sinks):
    bsz, seqlen = q.shape[0], q.shape[1]
    nb = seqlen // ATTN_BLOCK
    f32 = jnp.float32
    qb = q.astype(f32).reshape(bsz, nb, ATTN_BLOCK, N_KV_HEADS, GQA_GROUP, HEAD_DIM)
    kb = k.astype(f32).reshape(bsz, nb, ATTN_BLOCK, N_KV_HEADS, HEAD_DIM)
    vb = v.astype(f32).reshape(bsz, nb, ATTN_BLOCK, N_KV_HEADS, HEAD_DIM)
    k_prev = jnp.concatenate([jnp.zeros_like(kb[:, :1]), kb[:, :-1]], axis=1)
    v_prev = jnp.concatenate([jnp.zeros_like(vb[:, :1]), vb[:, :-1]], axis=1)
    kk = jnp.concatenate([k_prev, kb], axis=2)
    vv = jnp.concatenate([v_prev, vb], axis=2)
    s = jnp.einsum('bnqkgd,bnjkd->bnkgqj', qb, kk) * (HEAD_DIM ** -0.5)
    qi = jnp.arange(ATTN_BLOCK)[:, None] + ATTN_BLOCK
    kj = jnp.arange(2 * ATTN_BLOCK)[None, :]
    band = (kj <= qi) & (qi - kj < WINDOW)
    has_prev = jnp.arange(nb) > 0
    mask = band[None] & ((kj >= ATTN_BLOCK)[None] | has_prev[:, None, None])
    s = jnp.where(mask[None, :, None, None], s, NEG_INF)
    sink = sinks.astype(f32).reshape(1, 1, N_KV_HEADS, GQA_GROUP, 1, 1)
    m = jnp.maximum(jnp.max(s, axis=-1, keepdims=True), sink)
    pr = jnp.exp(s - m)
    w = pr / (jnp.sum(pr, axis=-1, keepdims=True) + jnp.exp(sink - m))
    o = jnp.einsum('bnkgqj,bnjkd->bnqkgd', w, vv)
    return o.reshape(bsz, seqlen, N_HEADS * HEAD_DIM).astype(q.dtype)

def second_inputs(seed: int = 0) -> dict:
    key = jax.random.key(seed)
    ks = jax.random.split(key, 32)
    f32 = jnp.float32
    nrm = lambda k, shape, scale: jax.random.normal(k, shape, f32) * scale
    x = nrm(ks[0], (BATCH, SEQ, D_MODEL), 1.0)
    p = nrm(ks[1], (DEPTH, BATCH, SEQ, PLE_DIM), 1.0)
    norm_mix = 1.0 + nrm(ks[2], (DEPTH, D_MODEL), 0.02)
    ssm_lambda_re = -0.5 + nrm(ks[3], (N_A_LAYERS, SSM_GROUPS, SSM_STATE), 0.01)
    ssm_lambda_im = (jnp.pi * jnp.arange(SSM_STATE, dtype=f32))[None, None, :] + nrm(ks[4], (N_A_LAYERS, SSM_GROUPS, SSM_STATE), 0.01)
    ssm_log_dt = math.log(DT_MIN) + jax.random.uniform(ks[5], (N_A_LAYERS, SSM_GROUPS), f32) * (math.log(DT_MAX) - math.log(DT_MIN))
    ssm_b_re = nrm(ks[6], (N_A_LAYERS, SSM_GROUPS, SSM_STATE, SSM_GROUP), (2 * SSM_GROUP) ** -0.5)
    ssm_b_im = nrm(ks[7], (N_A_LAYERS, SSM_GROUPS, SSM_STATE, SSM_GROUP), (2 * SSM_GROUP) ** -0.5)
    ssm_c_re = nrm(ks[8], (N_A_LAYERS, SSM_GROUPS, SSM_GROUP, SSM_STATE), (2 * SSM_STATE) ** -0.5)
    ssm_c_im = nrm(ks[9], (N_A_LAYERS, SSM_GROUPS, SSM_GROUP, SSM_STATE), (2 * SSM_STATE) ** -0.5)
    ssm_d = nrm(ks[10], (N_A_LAYERS, D_MODEL), 1.0)
    ssm_w_glu = nrm(ks[11], (N_A_LAYERS, D_MODEL, 2 * D_MODEL), D_MODEL ** -0.5)
    kv_norm = 1.0 + nrm(ks[12], (D_MODEL,), 0.02)
    w_k = nrm(ks[13], (D_MODEL, N_KV_HEADS * HEAD_DIM), D_MODEL ** -0.5)
    w_v = nrm(ks[14], (D_MODEL, N_KV_HEADS * HEAD_DIM), D_MODEL ** -0.5)
    w_q = nrm(ks[15], (N_B_LAYERS, D_MODEL, N_HEADS * HEAD_DIM), D_MODEL ** -0.5)
    attn_sinks = nrm(ks[16], (N_B_LAYERS, N_HEADS), 0.5)
    w_o = nrm(ks[17], (N_B_LAYERS, N_HEADS * HEAD_DIM, D_MODEL), (N_HEADS * HEAD_DIM) ** -0.5)
    norm_mlp = 1.0 + nrm(ks[18], (DEPTH, D_MODEL), 0.02)
    w_up = nrm(ks[19], (DEPTH, D_MODEL, D_FF), D_MODEL ** -0.5)
    w_down = nrm(ks[20], (DEPTH, D_FF, D_MODEL), D_FF ** -0.5)
    norm_ple = 1.0 + nrm(ks[21], (DEPTH, D_MODEL), 0.02)
    w_ple_gate = nrm(ks[22], (DEPTH, D_MODEL, D_MODEL), D_MODEL ** -0.5)
    w_ple_proj = nrm(ks[23], (DEPTH, PLE_DIM, D_MODEL), PLE_DIM ** -0.5)
    norm_final = 1.0 + nrm(ks[24], (D_MODEL,), 0.02)
    return {'x': x, 'p': p, 'norm_mix': norm_mix,
            'ssm_lambda_re': ssm_lambda_re, 'ssm_lambda_im': ssm_lambda_im, 'ssm_log_dt': ssm_log_dt,
            'ssm_b_re': ssm_b_re, 'ssm_b_im': ssm_b_im, 'ssm_c_re': ssm_c_re, 'ssm_c_im': ssm_c_im,
            'ssm_d': ssm_d, 'ssm_w_glu': ssm_w_glu,
            'kv_norm': kv_norm, 'w_k': w_k, 'w_v': w_v, 'w_q': w_q, 'attn_sinks': attn_sinks, 'w_o': w_o,
            'norm_mlp': norm_mlp, 'w_up': w_up, 'w_down': w_down,
            'norm_ple': norm_ple, 'w_ple_gate': w_ple_gate, 'w_ple_proj': w_ple_proj,
            'norm_final': norm_final}

def second_block(x, p, norm_mix, ssm_lambda_re, ssm_lambda_im, ssm_log_dt, ssm_b_re, ssm_b_im,
              ssm_c_re, ssm_c_im, ssm_d, ssm_w_glu, kv_norm, w_k, w_v, w_q, attn_sinks, w_o,
              norm_mlp, w_up, w_down, norm_ple, w_ple_gate, w_ple_proj, norm_final):
    bsz, seqlen, _ = x.shape
    pos = jnp.arange(seqlen, dtype=jnp.int32)
    h = x
    k_shared = None
    v_shared = None
    for i in range(DEPTH):
        hn = rmsnorm_2(h, norm_mix[i])
        if i < N_A_LAYERS:
            mix = s5_mixer(hn, ssm_lambda_re[i], ssm_lambda_im[i], ssm_log_dt[i], ssm_b_re[i], ssm_b_im[i],
                           ssm_c_re[i], ssm_c_im[i], ssm_d[i], ssm_w_glu[i])
        else:
            j = i - N_A_LAYERS
            q = (hn @ w_q[j]).reshape(bsz, seqlen, N_HEADS, HEAD_DIM)
            q = partial_rope(q, pos)
            mix = swa_sink_attention(q, k_shared, v_shared, attn_sinks[j]) @ w_o[j]
        h = h + mix
        hm = rmsnorm_2(h, norm_mlp[i])
        h = h + jnp.square(jax.nn.relu(hm @ w_up[i])) @ w_down[i]
        gate = jax.nn.sigmoid(rmsnorm_2(h, norm_ple[i]) @ w_ple_gate[i])
        h = h + gate * (p[i] @ w_ple_proj[i])
        if i == N_A_LAYERS - 1:
            hk = rmsnorm_2(h, kv_norm)
            k_shared = partial_rope((hk @ w_k).reshape(bsz, seqlen, N_KV_HEADS, HEAD_DIM), pos)
            v_shared = (hk @ w_v).reshape(bsz, seqlen, N_KV_HEADS, HEAD_DIM)
    return rmsnorm_2(h, norm_final)


def setup_inputs(seed=0):
    out = dict(first_inputs(seed))
    for name, value in second_inputs(seed + 1).items():
        if name != "x":
            out[name + "_2"] = value
    return out


def reference(
    x, norm_even, w_in_even, conv_a_w, conv_a_b, ln_a_g, ln_a_b, pool_w, pool_b, pool_scale,
    w_out_even, norm_odd, w_in_odd, conv_c_w, conv_c_b, w_rg, b_rg, w_ig, b_ig, lru_lambda,
    w_out_odd, final_norm, p_2, norm_mix_2, ssm_lambda_re_2, ssm_lambda_im_2, ssm_log_dt_2,
    ssm_b_re_2, ssm_b_im_2, ssm_c_re_2, ssm_c_im_2, ssm_d_2, ssm_w_glu_2, kv_norm_2, w_k_2,
    w_v_2, w_q_2, attn_sinks_2, w_o_2, norm_mlp_2, w_up_2, w_down_2, norm_ple_2, w_ple_gate_2,
    w_ple_proj_2, norm_final_2,
):
    x = first_block(
        x, norm_even, w_in_even, conv_a_w, conv_a_b, ln_a_g, ln_a_b, pool_w, pool_b, pool_scale,
        w_out_even, norm_odd, w_in_odd, conv_c_w, conv_c_b, w_rg, b_rg, w_ig, b_ig, lru_lambda,
        w_out_odd, final_norm,
    )
    return second_block(
        x, p_2, norm_mix_2, ssm_lambda_re_2, ssm_lambda_im_2, ssm_log_dt_2, ssm_b_re_2,
        ssm_b_im_2, ssm_c_re_2, ssm_c_im_2, ssm_d_2, ssm_w_glu_2, kv_norm_2, w_k_2, w_v_2,
        w_q_2, attn_sinks_2, w_o_2, norm_mlp_2, w_up_2, w_down_2, norm_ple_2, w_ple_gate_2,
        w_ple_proj_2, norm_final_2,
    )


_drawn_inputs = setup_inputs


def setup_inputs(seed=0):
    import zlib

    import numpy as np

    out = dict(_drawn_inputs(seed))
    spreads = {}
    factors = {'norm_even': 4.147,
     'conv_a_b': 8.0,
     'ln_a_g': 8.0,
     'ln_a_b': 8.0,
     'pool_b': 8.0,
     'norm_odd': 6.184,
     'b_rg': 8.0,
     'b_ig': 8.0,
     'norm_mix_2': 6.611,
     'ssm_lambda_re_2': 64.0,
     'ssm_log_dt_2': 2.714,
     'ssm_b_re_2': 3.684,
     'ssm_b_im_2': 3.704,
     'ssm_c_re_2': 3.753,
     'ssm_c_im_2': 3.718,
     'kv_norm_2': 8.0,
     'attn_sinks_2': 24.665,
     'norm_ple_2': 8.0,
     'norm_final_2': 7.99}
    for name, (base, spread) in spreads.items():
        noise = np.random.default_rng([zlib.crc32(name.encode()), seed]).standard_normal(out[name].shape)
        drawn = base * np.exp(spread * noise) if base else spread * noise
        out[name] = __import__('jax').numpy.asarray(drawn.astype(out[name].dtype))
    for name, factor in factors.items():
        out[name] = (out[name] * factor).astype(out[name].dtype)
    return out
```

```python
import math
from contextlib import ExitStack

import numpy as np
import concourse.bass as bass
from concourse import mybir

F32 = mybir.dt.float32
F32R = mybir.dt.float32r
ALU = mybir.AluOpType
ACT = mybir.ActivationFunctionType
AX = mybir.AxisListType

T = 512
NC8 = 8
PI = math.pi
TWO_PI_HI = 6.28125
TWO_PI_MID = float(np.float32(2 * PI - 6.28125))
TWO_PI_LO = float(np.float32(2 * PI - 6.28125 - TWO_PI_MID))
ROUND = 12582912.0

VECS = [
    ("norm_even", 8), ("conv_a_w", 31 * 8), ("conv_a_b", 8), ("ln_a_g", 8), ("ln_a_b", 8),
    ("pool_b", 8), ("pool_scale", 8), ("norm_odd", 8), ("conv_c_w", 4 * 12), ("conv_c_b", 12),
    ("b_rg", 12), ("b_ig", 12), ("lru_lambda", 12), ("final_norm", 8), ("norm_mix", 16),
    ("ssm_d", 8), ("kv_norm", 8), ("norm_mlp", 16), ("norm_ple", 16), ("norm_final", 8),
    ("sinks", 16),
]
VCOL = {}
_at = 0
for _n, _c in VECS:
    VCOL[_n] = _at
    _at += _c
NV = _at

CC = {"ident": 0, "rot": 128, "mask": 256, "cnt": 512, "sgn": 576}
NCC = 580
SC = {"lre": 0, "lim": 32, "ldt": 64, "br": 96, "bi": 608, "cr": 1120, "ci": 1632}
NSC = 2144


class Engine:

    def __init__(self, k, name):
        self.k, self.name, self.items, self.seen, self.sem, self.n = k, name, [], {}, None, 0

    def stage(self, name):
        self.sem, self.n = self.k.semaphore(f"{self.name}_{name}"), 0

    def wait(self, *tokens):
        for t in tokens:
            if isinstance(t, (list, tuple)) and not (len(t) == 2 and isinstance(t[1], int)):
                self.wait(*t)
                continue
            if t is None:
                continue
            sem, value = t
            if self.seen.get(sem, 0) < value:
                self.seen[sem] = value
                self.items.append(("wait", sem, value))

    def __call__(self, fn, *tokens, quiet=False):
        self.wait(*tokens)
        if quiet:
            self.items.append(("op", fn, None, 0))
            return None
        self.n += 1
        self.items.append(("op", fn, self.sem, 1))
        return (self.sem, self.n)

    @property
    def last(self):
        return (self.sem, self.n) if self.n else None


class Slot:

    def __init__(self, ap):
        self.ap, self.free = ap, []


class Ring:

    def __init__(self, aps):
        self.slots = [Slot(a) for a in aps]

    def take(self):
        return self.slots.pop(0)

    def give(self, s, *tokens):
        s.free = list(tokens)
        self.slots.append(s)


class Split:

    def __init__(self, hi, lo):
        self.hi, self.lo = hi, lo
        self.free = []
        self.ready = {}


class Builder:
    NR, NS = 3, 3

    def __init__(self, nc, ctx, order):
        self.nc, self.ctx, self.dry = nc, ctx, order is None
        self.order = order or []
        self.used = []
        self.sems = {}
        self.pe, self.act, self.dve, self.pool, self.sp = (Engine(self, n) for n in ("pe", "act", "dve", "pool", "sp"))
        self.engines = (self.pe, self.act, self.dve, self.pool)
        self.bg = []
        self.dma_n = {}

    def semaphore(self, name):
        assert name not in self.sems
        self.sems[name] = self.ctx.enter_context(self.nc.semaphore(name))
        return name

    def stage(self, name):
        for e in self.engines:
            e.stage(name)

    def load(self, dst, src, *tokens, sem):
        self.sp.wait(*tokens)
        if sem not in self.sems:
            self.semaphore(sem)
            self.dma_n[sem] = 0
        self.dma_n[sem] += 16
        self.sp.items.append(("op", lambda e: e.dma_start(dst, src), sem, 16))
        return (sem, self.dma_n[sem])

    def fence(self):
        return [e.last for e in self.engines if e.last]

    def weights_init(self, raw, hi, lo, dram):
        self.raw, self.hi, self.lo, self.dram = raw, hi, lo, dram
        self.hi_tok, self.lo_tok, self.pe_tok, self.raw_tok = {}, {}, {}, {}
        self.next_dma = self.next_split = 0
        for _ in range(self.NR):
            self._dma()

    def _dma(self):
        i = self.next_dma
        if i >= len(self.order):
            return
        self.next_dma += 1
        j = i % self.NR
        w = [self.hi_tok[i - self.NR], self.lo_tok[i - self.NR]] if i >= self.NR else []
        self.raw_tok[i] = self.load(self.raw[:, j, :], self.dram[i, :, :], *w, sem=f"raw{j}")

    def _split(self):
        i = self.next_split
        if i >= len(self.order):
            return
        self.next_split += 1
        r, s = i % self.NR, i % self.NS
        done = self.pe_tok[i - self.NS] if i >= self.NS else None
        raw, hi, lo = self.raw[:, r, :], self.hi[:, s, :], self.lo[:, s, :]
        self.hi_tok[i] = self.act(lambda e: e.activation(hi, raw, ACT.Copy), self.raw_tok[i], done)
        self.lo_tok[i] = self.pool(
            lambda e: e.tensor_tensor(lo, raw, hi.bitcast(F32), ALU.subtract), self.hi_tok[i], done)
        self._dma()

    def weights(self, what):
        i = len(self.used)
        self.used.append(what)
        if self.dry:
            self.order.append(what)
            self.hi_tok[i] = self.lo_tok[i] = None
            return i
        assert self.order[i] == what
        while self.next_split < min(i + self.NS, len(self.order)):
            self._split()
        return i

    def tiles(self, i):
        s = i % self.NS
        return self.hi[:, s, :], self.lo[:, s, :]

    def unit_done(self, i, tok):
        self.pe_tok[i] = tok

    def mm3(self, out, wh, wl, xh, xl, start, stop, *tokens, last=False):
        self.pe.wait(*tokens)
        self.pe(lambda e: e.matmul(out, wh, xh, start=start, stop=False), quiet=True)
        self.pe(lambda e: e.matmul(out, wl, xh, start=False, stop=False), quiet=True)
        return self.pe(lambda e: e.matmul(out, wh, xl, start=False, stop=stop), quiet=not last)

    def linear(self, what, x, chunks, bank, wait_x=True):
        i = self.weights(what)
        wh, wl = self.tiles(i)
        tok = None
        self.pe.wait(bank.free, self.hi_tok[i], self.lo_tok[i])
        for n, c in enumerate(chunks):
            ws = slice(n * 128, n * 128 + 128)
            tok = self.mm3(bank.ap[:, :], wh[:, ws], wl[:, ws], x.hi[:, c, :], x.lo[:, c, :],
                           n == 0, n == len(chunks) - 1, x.ready[c], last=n == len(chunks) - 1)
        self.unit_done(i, tok)
        return tok

    def emit(self, block):
        def run(q, sems):
            def go(eng):
                for it in q.items:
                    if it[0] == "wait":
                        eng.wait_ge(sems[it[1]], it[2])
                    else:
                        ins = it[1](eng)
                        if it[2] is not None:
                            ins.then_inc(sems[it[2]], it[3])
            return go
        block.tensor(run(self.pe, self.sems))
        block.scalar(run(self.act, self.sems))
        block.vector(run(self.dve, self.sems))
        block.gpsimd(run(self.pool, self.sems))
        block.sync(run(self.sp, self.sems))


def program(nc, ctx, k, D, stop=None):
    pe, act, dve, pool = k.pe, k.act, k.dve, k.pool

    def sb(name, shape, dt=F32, c=ctx):
        return c.enter_context(nc.sbuf_tensor(name, shape, dt))

    H = sb("H", [128, 8, T])
    RAW = sb("RAW", [128, k.NR, 1024])
    WH = sb("WH", [128, k.NS, 1024], F32R)
    WL = sb("WL", [128, k.NS, 1024], F32R)
    VE = sb("VE", [128, NV])
    CO = sb("CO", [128, NCC])
    ONES = sb("ONES", [128, 128])
    NT = 9
    TMP = sb("TMP", [128, NT, 576])
    RS = sb("RS", [128, 2, T])
    SM = sb("SM", [128, 64])
    P0h = sb("P0h", [128, 8, T], F32R)
    P0l = sb("P0l", [128, 8, T], F32R)
    P0 = Split(P0h, P0l)
    banks = [ctx.enter_context(nc.psum_tensor(f"B{i}", [128, 512], F32)) for i in range(8)]
    BK = Ring(banks)
    TR = Ring([TMP[:, i, :] for i in range(NT)])
    ident = CO[:, 0:128]

    def vec(name, c):
        return VE[:, VCOL[name] + c:VCOL[name] + c + 1]

    k.stage("init")
    t_ve = k.load(VE[:, :], D["vecs"], sem="d_ve")
    t_h = [k.load(H[:, c, :], D["xT"][c], sem=f"d_h{c}") for c in range(8)]
    k.weights_init(RAW, WH, WL, D["w"])
    t_co = k.load(CO[:, :], D["consts"], sem="d_co")
    t_ones = dve(lambda e: e.memset(ONES[:, :], 1.0))
    t_mh = dve(lambda e: e.memset(SM[:, 0:4], -0.5))
    H_tok = list(t_h)
    H_rd = [[] for _ in range(8)]
    pe.wait(t_ones, t_co)
    act.wait(t_ve)
    dve.wait(t_ve, t_co)
    sm_free = [None]
    ACC = sb("ACC", [128, T])
    acc_free = [None]

    def sumsq(src, c, tok, first):
        if first:
            t = act(lambda e: e.activation(ACC[:, :], src, ACT.Square), tok, acc_free[0])
            sumsq.tok = t
            return t
        s = TR.take()
        a = act(lambda e: e.activation(s.ap[:, 0:T], src, ACT.Square), tok, s.free)
        t = pool(lambda e: e.tensor_tensor(ACC[:, :], ACC[:, :], s.ap[:, 0:T], ALU.add), a, sumsq.tok)
        TR.give(s, t)
        sumsq.tok = t
        return a

    rs_i = [0]
    rs_free = [[], []]

    def stat_a(eps):
        b = BK.take()
        pe.wait(sumsq.tok, b.free)
        for j in range(4):
            t = pe(lambda e, j=j: e.matmul(b.ap[:, j:j + 1], ACC[:, j * 128:j * 128 + 128], ONES[:, 0:1],
                                           start=True, stop=True), quiet=j < 3)
        acc_free[0] = t
        d = dve(lambda e: e.tensor_scalar(SM[:, 4:8], b.ap[:, 0:4], 1.0 / 1024, eps, ALU.mult, ALU.add), t, sm_free[0])
        BK.give(b, d)
        return pool(lambda e: e.tensor_tensor(SM[:, 8:12], SM[:, 4:8], SM[:, 0:4], ALU.pow), d, t_mh, sm_free[0])

    def stat_b(tok):
        b = BK.take()
        pe.wait(tok, b.free)
        for j in range(4):
            t = pe(lambda e, j=j: e.matmul(b.ap[:, j * 128:j * 128 + 128], SM[:, 8 + j:9 + j].to_broadcast([128, 128]),
                                           ident, start=True, stop=True), quiet=j < 3)
        sm_free[0] = t
        i = rs_i[0] % 2
        rs_i[0] += 1
        a = act(lambda e: e.activation(RS[:, i, :], b.ap[:, :], ACT.Copy), t, rs_free[i])
        BK.give(b, a)
        rs_free[i] = []
        return RS[:, i, :], a, i

    def split_scaled(dst, c, src, g, tok):
        a = act(lambda e: e.activation(dst.hi[:, c, :], src, ACT.Copy, scale=g), tok, dst.free)
        d = dve(lambda e: e.scalar_tensor_tensor(dst.lo[:, c, :], src, g, dst.hi[:, c, :].bitcast(F32),
                                                 ALU.mult, ALU.subtract), a, tok, dst.free)
        dst.ready[c] = [a, d]
        return [a, d]

    def split(dst, c, src, tok):
        a = act(lambda e: e.activation(dst.hi[:, c, :], src, ACT.Copy), tok, dst.free)
        d = dve(lambda e: e.tensor_tensor(dst.lo[:, c, :], src, dst.hi[:, c, :].bitcast(F32), ALU.subtract),
                a, tok, dst.free)
        dst.ready[c] = [a, d]
        return [a, d]

    def norm_in(c, outs):
        r = [sumsq(H[:, c, :], c, H_tok[c], c == 0)]
        for dst, name, off in outs:
            r += split_scaled(dst, c, H[:, c, :], vec(name, off + c), H_tok[c])
        H_rd[c] = r

    def add_to_h(c, src, toks):
        H_tok[c] = dve(lambda e: e.tensor_tensor(H[:, c, :], H[:, c, :], src, ALU.add), toks, H_tok[c], H_rd[c])
        return H_tok[c]

    def bg(n):
        for _ in range(n):
            if k.bg:
                k.bg.pop(0)()

    class Lag:

        def __init__(self, eps=1e-6):
            self.pend, self.n, self.eps, self.rs = [], 0, eps, None

        def put(self, evac):
            self.pend.append(evac)
            self.n += 1
            if self.n == 1:
                self.a = stat_a(self.eps)
            elif self.n == 2:
                self.rs, self.rt, self.ri = stat_b(self.a)
            if self.rs is not None:
                for f in self.pend:
                    f(self.rs, self.rt)
                self.pend = []

        def end(self, tok):
            rs_free[self.ri] = tok

    def scale_psum(dst, b, rs, rt, t, *w):
        return dve(lambda e: e.tensor_tensor(dst, b.ap[:, :], rs, ALU.mult), t, rt, *w)

    def gate(b, t, lag, s, ts, dst, c):
        g, sg = TR.take(), TR.take()
        d = scale_psum(g.ap[:, 0:T], b, lag.rs, lag.rt, t, g.free)
        BK.give(b, d)
        a = act(lambda e: e.activation(sg.ap[:, 0:T], g.ap[:, 0:T], ACT.Sigmoid), d, sg.free)
        m = pool(lambda e: e.tensor_tensor(s.ap[:, 0:T], g.ap[:, 0:T], s.ap[:, 0:T], ALU.mult), d, ts)
        TR.give(g, a, m)
        m2 = dve(lambda e: e.tensor_tensor(sg.ap[:, 0:T], s.ap[:, 0:T], sg.ap[:, 0:T], ALU.mult), a, m)
        TR.give(sg, *split(dst, c, sg.ap[:, 0:T], m2))
        return m2

    def done(name):
        if stop != name:
            return False
        for c in range(8):
            k.load(D["out"][c], H[:, c, :], H_tok[c], sem="d_out")
        k.sp.wait(("d_out", k.dma_n["d_out"]))
        return True

    k.stage("even")
    scope = ExitStack()
    P1 = Split(sb("P1h", [128, 8, T], F32R, scope), sb("P1l", [128, 8, T], F32R, scope))
    P2 = Split(sb("P2h", [128, 8, T], F32R, scope), sb("P2l", [128, 8, T], F32R, scope))
    UP = sb("UP", [128, 3, 30 + T], F32, scope)
    CV = sb("CV", [128, 8, T], F32, scope)
    PBS = sb("PBS", [128, 8], F32, scope)
    t_pad = pool(lambda e: e.memset(UP[:, :, 0:30], 0.0))
    t_pbs = dve(lambda e: e.tensor_tensor(PBS[:, :], VE[:, VCOL["pool_b"]:VCOL["pool_b"] + 8],
                                          VE[:, VCOL["pool_scale"]:VCOL["pool_scale"] + 8], ALU.mult))
    for c in range(8):
        norm_in(c, [(P0, "norm_even", 0)])
    UR = Ring([UP[:, i, :] for i in range(3)])
    lag = Lag()
    cv_tok = [None] * 8

    def conv_ops(c, u, t_u):
        def tap(j):
            w = VE[:, VCOL["conv_a_w"] + c * 31 + j:VCOL["conv_a_w"] + c * 31 + j + 1]
            x = u.ap[:, j:j + T]
            if j == 0:
                cv_tok[c] = act(lambda e: e.activation(CV[:, c, :], x, ACT.Identity, bias=vec("conv_a_b", c), scale=w), t_u)
                return
            cv_tok[c] = dve(lambda e: e.scalar_tensor_tensor(CV[:, c, :], x, w, CV[:, c, :], ALU.mult, ALU.add), cv_tok[c], t_u)
            if j == 30:
                UR.give(u, cv_tok[c])
        return [lambda j=j: tap(j) for j in range(31)]

    for c in range(8):
        bg_ = BK.take()
        t_g = k.linear(("in_even", 0, 8 + c), P0, range(8), bg_)
        st = {}

        def glu(rs, rt, b=bg_, t=t_g, st=st):
            s = st["s"] = TR.take()
            d = scale_psum(s.ap[:, 0:T], b, rs, rt, t, s.free)
            BK.give(b, d)
            st["t"] = act(lambda e: e.activation(s.ap[:, 0:T], s.ap[:, 0:T], ACT.Sigmoid), d)
        lag.put(glu)
        bv = BK.take()
        t_v = k.linear(("in_even", 0, c), P0, range(8), bv)

        def val(rs, rt, b=bv, t=t_v, st=st, c=c):
            s = st["s"]
            v = TR.take()
            d = scale_psum(v.ap[:, 0:T], b, rs, rt, t, v.free)
            BK.give(b, d)
            while len(k.bg) > 31 * 2:
                bg(1)
            u = UR.take()
            m = dve(lambda e: e.tensor_tensor(u.ap[:, 30:], v.ap[:, 0:T], s.ap[:, 0:T], ALU.mult), d, st["t"], u.free, t_pad)
            TR.give(s, m)
            TR.give(v, m)
            k.bg += conv_ops(c, u, m)
        lag.put(val)
        bg(10)

    def windows(c, v, tv):
        g = c // 2
        w = 2 << g
        cur, tok = v, tv
        for s in range(g + 1):
            sh = 1 << s
            nx = TR.take()
            a = pool(lambda e, cur=cur, nx=nx, sh=sh: e.tensor_tensor(
                nx.ap[:, sh:T], cur.ap[:, sh:T], cur.ap[:, 0:T - sh], ALU.add), tok, nx.free)
            b = pool(lambda e, cur=cur, nx=nx, sh=sh: e.tensor_copy(nx.ap[:, 0:sh], cur.ap[:, 0:sh]), tok, nx.free)
            if cur is not v:
                TR.give(cur, a, b)
            cur, tok = nx, [a, b]
        a = pool(lambda e, cur=cur: e.tensor_tensor(cur.ap[:, 0:16], cur.ap[:, 0:16],
                                                    CO[:, CC["cnt"] + 16 * g:CC["cnt"] + 16 * g + 16], ALU.mult), tok, t_co)
        d = dve(lambda e, cur=cur: e.scalar_tensor_tensor(v.ap[:, 0:T], cur.ap[:, 0:T], 1.0 / w, v.ap[:, 0:T],
                                                          ALU.mult, ALU.subtract), a, tok, tv)
        TR.give(cur, d)
        return d


    for h in range(2):
        for c in range(4 * h, 4 * h + 4):
            b = BK.take()
            t = k.linear(("in_even", 0, 24 + c), P0, range(8), b)
            v = TR.take()
            d = scale_psum(v.ap[:, 0:T], b, lag.rs, lag.rt, t, v.free)
            BK.give(b, d)
            d = windows(c, v, d)
            TR.give(v, *split(P2, c, v.ap[:, 0:T], d))
            bg(6)
        i = k.weights(("pool", 0, h))
        wh, wl = k.tiles(i)
        pe.wait(k.hi_tok[i], k.lo_tok[i])
        yb = {}
        for g in range(2):
            for n in range(2):
                b = BK.take()
                pe.wait(b.free)
                for kc in range(2):
                    o = ((g * 2 + kc) * 2 + n) * 128
                    c = (h * 2 + g) * 2 + kc
                    t = k.mm3(b.ap[:, :], wh[:, o:o + 128], wl[:, o:o + 128], P2.hi[:, c, :], P2.lo[:, c, :],
                              kc == 0, kc == 1, P2.ready[c], last=kc == 1)
                c = (h * 2 + g) * 2 + n
                s = TR.take()
                a = act(lambda e, b=b, c=c, s=s: e.activation(
                    s.ap[:, 0:T], b.ap[:, :], ACT.Identity, bias=PBS[:, c:c + 1], scale=vec("pool_scale", c)),
                    t, t_pbs, s.free)
                BK.give(b, a)
                yb[c] = (s, a)
        k.unit_done(i, t)
        t_d = t
        bg(6)
        for c in range(4 * h, 4 * h + 4):
            b = BK.take()
            t = k.linear(("in_even", 0, 32 + c), P0, range(8), b)
            m = gate(b, t, lag, *yb[c], P1, c)
            TR.give(yb[c][0], m)
            bg(6)
    P2.free = [t_d]

    def out_pass(what, src, base, final, outs=(), x0=0):
        for n in range(8):
            b = BK.take()
            t = k.linear((what, base, n), src, range(x0, x0 + 8), b)
            BK.give(b, add_to_h(n, b.ap[:, :], t))
            if final:
                norm_in(n, outs)
            bg(6)
        src.free = [t]

    out_pass("out_even", P1, 1, False)
    bg(len(k.bg))
    acc = acc_free[0]
    t1 = pool(lambda e: e.tensor_tensor(ACC[:, :], CV[:, 0, :], CV[:, 1, :], ALU.add), cv_tok[0], cv_tok[1], acc)
    for c in range(2, 8):
        t1 = pool(lambda e, c=c: e.tensor_tensor(ACC[:, :], ACC[:, :], CV[:, c, :], ALU.add), cv_tok[c], t1)
    b = BK.take()
    t = pe(lambda e, b=b: e.matmul(b.ap[:, :], ONES[:, :], ACC[:, :], start=True, stop=True), t1, b.free)
    acc_free[0] = t
    mu = TR.take()
    a = act(lambda e, b=b: e.activation(mu.ap[:, 0:T], b.ap[:, :], ACT.Copy, scale=1.0 / 1024), t, mu.free)
    BK.give(b, a)
    cs = []
    for c in range(8):
        d = dve(lambda e, c=c: e.tensor_tensor(CV[:, c, :], CV[:, c, :], mu.ap[:, 0:T], ALU.subtract), a, t1, cv_tok[c])
        cs.append(d)
        sumsq(CV[:, c, :], c, d, c == 0)
    TR.give(mu, cs[-1])
    ln_rs, ln_t, ln_i = stat_b(stat_a(1e-5))
    ln = []
    for c in range(8):
        d = dve(lambda e, c=c: e.tensor_tensor(CV[:, c, :], CV[:, c, :], ln_rs, ALU.mult), ln_t, cs[c], sumsq.tok)
        s = TR.take()
        a = act(lambda e, c=c, s=s: e.activation(s.ap[:, 0:T], CV[:, c, :], ACT.Sigmoid, bias=vec("ln_a_b", c),
                                                 scale=vec("ln_a_g", c)), d, s.free)
        a2 = dve(lambda e, c=c: e.tensor_scalar(CV[:, c, :], CV[:, c, :], vec("ln_a_g", c), vec("ln_a_b", c),
                                                ALU.mult, ALU.add), a, d)
        d = dve(lambda e, c=c, s=s: e.tensor_tensor(CV[:, c, :], CV[:, c, :], s.ap[:, 0:T], ALU.mult), a2, a)
        TR.give(s, d)
        ln.append(d)
    rs_free[ln_i] = [ln[-1]]
    for c in range(8):
        b = BK.take()
        t = k.linear(("in_even", 0, 16 + c), P0, range(8), b)
        gate(b, t, lag, Slot(CV[:, c, :]), ln[c], P2, c)
    P0.free = [t]
    lag.end([dve.last])
    P2.free = []
    out_pass("out_even", P2, 0, True, [(P0, "norm_odd", 0)])
    fence = k.fence()
    scope.close()
    if done("even"):
        return

    k.stage("odd")
    psc = ExitStack()
    SPT = sb("SPT", [128, NSC], F32, psc)
    PW = sb("PW", [128, 2, 9, 32], F32, psc)
    BB = sb("BB", [128, 2, 32, 16], F32, psc)
    A8 = sb("A8", [128, 2, 2, 32], F32, psc)
    SW = sb("SW", [128, 12, 32], F32, psc)
    SP4 = sb("SP4", [128, 2, 12], F32, psc)
    scope = ExitStack()
    Yh = sb("Yh", [128, 12, T], F32R, scope)
    Yl = sb("Yl", [128, 12, T], F32R, scope)
    Y = Split(Yh, Yl)
    Y.free = fence
    XP = sb("XP", [128, 3, 3 + T], F32, scope)
    GT = sb("GT", [128, 9, T], F32, scope)
    GR = Ring([GT[:, i, :] for i in range(9)])
    XR = Ring([XP[:, i, :] for i in range(3)])
    for s in GR.slots + XR.slots:
        s.free = fence
    t_xp = pool(lambda e: e.memset(XP[:, :, 0:3], 0.0), fence)
    t_sp = k.load(SPT[:, :], D["ssm"], fence, sem="d_sp")
    lam = VE[:, VCOL["lru_lambda"]:VCOL["lru_lambda"] + 12]
    a = act(lambda e: e.activation(SP4[:, 0, :], lam, ACT.Abs), fence)
    a = act(lambda e: e.activation(SP4[:, 0, :], SP4[:, 0, :], ACT.Exp, scale=-1.0), a)
    a = act(lambda e: e.activation(SP4[:, 0, :], SP4[:, 0, :], ACT.Ln, bias=1.0), a)
    d = dve(lambda e: e.tensor_scalar(SP4[:, 1, :], lam, -1.0, 0.0, ALU.mult, ALU.max), fence)
    d = dve(lambda e: e.tensor_tensor(SP4[:, 0, :], SP4[:, 0, :], SP4[:, 1, :], ALU.add), a, d)
    t_sp4 = dve(lambda e: e.tensor_scalar(SP4[:, 0, :], SP4[:, 0, :], 4.0, None, ALU.mult), d)

    ch = {"t": [t_sp] + fence, "m": None}

    def small(eng, fn):
        def go():
            ch["t"] = eng(fn, ch["t"])
        k.bg.append(go)

    def sw(i):
        return SW[:, i, :]

    def spc(n):
        return SPT[:, SC[n]:SC[n] + 32]

    small(act, lambda e: e.activation(sw(0), spc("ldt"), ACT.Exp))
    small(dve, lambda e: e.tensor_tensor(sw(1), spc("lre"), sw(0), ALU.mult))
    small(act, lambda e: e.activation(sw(1), sw(1), ACT.Exp))
    small(dve, lambda e: e.tensor_tensor(sw(2), spc("lim"), sw(0), ALU.mult))
    for which, quarter in ((3, 0.0), (4, 0.25)):
        small(dve, lambda e, q=quarter: e.tensor_scalar(sw(5), sw(2), 1.0 / (2 * PI), q, ALU.mult, ALU.add))
        small(dve, lambda e: e.tensor_scalar(sw(5), sw(5), ROUND, None, ALU.add))
        small(dve, lambda e: e.tensor_scalar(sw(5), sw(5), ROUND, None, ALU.subtract))
        small(dve, lambda e: e.scalar_tensor_tensor(sw(6), sw(5), -TWO_PI_HI, sw(2), ALU.mult, ALU.add))
        small(dve, lambda e: e.scalar_tensor_tensor(sw(6), sw(5), -TWO_PI_MID, sw(6), ALU.mult, ALU.add))
        small(dve, lambda e: e.scalar_tensor_tensor(sw(6), sw(5), -TWO_PI_LO, sw(6), ALU.mult, ALU.add))
        small(dve, lambda e, q=quarter: e.tensor_scalar(sw(6), sw(6), 2 * PI * q, PI, ALU.add, ALU.min))
        small(dve, lambda e: e.tensor_scalar(sw(6), sw(6), -PI, None, ALU.max))
        small(act, lambda e, w=which: e.activation(sw(w), sw(6), ACT.Sin))
    small(dve, lambda e: e.memset(PW[:, 0, 0, :], 1.0))
    small(dve, lambda e: e.memset(PW[:, 1, 0, :], 0.0))
    small(dve, lambda e: e.tensor_tensor(PW[:, 0, 1, :], sw(1), sw(4), ALU.mult))
    small(dve, lambda e: e.tensor_tensor(PW[:, 1, 1, :], sw(1), sw(3), ALU.mult))

    def small_cmul(o, x, y, t):
        for i, (p, q) in enumerate(((0, 0), (1, 1), (0, 1), (1, 0))):
            small(dve, lambda e, i=i, p=p, q=q: e.tensor_tensor(t[i], x[p], y[q], ALU.mult))
        small(dve, lambda e: e.tensor_tensor(o[0], t[0], t[1], ALU.subtract))
        small(dve, lambda e: e.tensor_tensor(o[1], t[2], t[3], ALU.add))

    tmp4 = SW[:, 0:12, :]
    for n in (1, 2, 4):
        x = [PW[:, r, 1:1 + n, :] for r in range(2)]
        y = [PW[:, r, n:n + 1, :].to_broadcast([128, n, 32]) for r in range(2)]
        o = [PW[:, r, n + 1:2 * n + 1, :] for r in range(2)]
        if n < 4:
            t4 = [SW[:, 4 + 2 * i:4 + 2 * i + n, :] for i in range(4)]
        else:
            t4 = [BB[:, 0, 4 * 2 * i:4 * 2 * i + 8, :].rearrange("p a b -> p (a b)").rearrange("p (m g) -> p m g", m=4)
                  for i in range(4)]
        small_cmul(o, x, y, t4)
    lre, lim = spc("lre"), spc("lim")
    small(dve, lambda e: e.tensor_tensor(sw(0), lre, lre, ALU.mult))
    small(dve, lambda e: e.tensor_tensor(sw(1), lim, lim, ALU.mult))
    small(dve, lambda e: e.tensor_tensor(sw(0), sw(0), sw(1), ALU.add))
    small(dve, lambda e: e.reciprocal(sw(0), sw(0)))
    small(dve, lambda e: e.tensor_scalar(sw(1), PW[:, 0, 1, :], 1.0, None, ALU.subtract))
    small(dve, lambda e: e.tensor_tensor(sw(2), sw(1), lre, ALU.mult))
    small(dve, lambda e: e.tensor_tensor(sw(3), PW[:, 1, 1, :], lim, ALU.mult))
    small(dve, lambda e: e.tensor_tensor(sw(4), PW[:, 1, 1, :], lre, ALU.mult))
    small(dve, lambda e: e.tensor_tensor(sw(5), sw(1), lim, ALU.mult))
    small(dve, lambda e: e.tensor_tensor(sw(2), sw(2), sw(3), ALU.add))
    small(dve, lambda e: e.tensor_tensor(sw(4), sw(4), sw(5), ALU.subtract))
    small(dve, lambda e: e.tensor_tensor(sw(2), sw(2), sw(0), ALU.mult))
    small(dve, lambda e: e.tensor_tensor(sw(4), sw(4), sw(0), ALU.mult))

    def v3(ap):
        return ap.rearrange("p (g h) -> p g h", h=16)

    def coef(i):
        return SW[:, i, :].unsqueeze(2).to_broadcast([128, 32, 16])

    br_, bi_ = (v3(SPT[:, SC[n]:SC[n] + 512]) for n in ("br", "bi"))

    def bbar():
        s = [TR.take() for _ in range(2)]
        w = ch["t"]
        for r, (x, y, op) in enumerate(((br_, bi_, ALU.subtract), (bi_, br_, ALU.add))):
            u0 = v3(s[0].ap[:, 0:512])
            u1 = v3(s[1].ap[:, 0:512])
            a = dve(lambda e, u0=u0, x=x: e.tensor_tensor(u0, coef(2), x, ALU.mult), w, s[0].free)
            b = dve(lambda e, u1=u1, y=y: e.tensor_tensor(u1, coef(4), y, ALU.mult), w, s[1].free)
            w = dve(lambda e, u0=u0, u1=u1, r=r, op=op: e.tensor_tensor(BB[:, r, :, :], u0, u1, op), a, b)
        TR.give(s[0], w)
        TR.give(s[1], w)
        ch["t"] = w
    k.bg.append(bbar)
    for i, (r, sg) in enumerate(((0, 1.0), (0, 1.0), (1, -1.0), (1, 1.0))):
        small(dve, lambda e, i=i, r=r, sg=sg: e.tensor_scalar(A8[:, i // 2, i % 2, :], PW[:, r, 8, :], sg, None, ALU.mult))

    lag = Lag()
    xcs, heads = {}, {}

    def xr_unit(h):
        b = BK.take()
        t = k.linear(("in_odd", 0, h), P0, range(8), b)

        def evac(rs, rt):
            x = XR.take()
            d = scale_psum(x.ap[:, 3:], b, rs, rt, t, x.free, t_xp)
            BK.give(b, d)
            s = TR.take()
            w = [VE[:, VCOL["conv_c_w"] + 4 * h + j:VCOL["conv_c_w"] + 4 * h + j + 1] for j in range(4)]
            a = act(lambda e: e.activation(s.ap[:, 0:T], x.ap[:, 0:T], ACT.Identity, bias=vec("conv_c_b", h), scale=w[0]),
                    d, s.free)
            for j in range(1, 4):
                a = dve(lambda e, j=j: e.scalar_tensor_tensor(s.ap[:, 0:T], x.ap[:, j:j + T], w[j], s.ap[:, 0:T],
                                                             ALU.mult, ALU.add), a)
            XR.give(x, a)
            xcs[h] = (s, a, split(Y, h, s.ap[:, 0:T], a))
        lag.put(evac)

    def rgig(g):
        i = k.weights(("rgig", 0, g))
        wh, wl = k.tiles(i)
        pe.wait(k.hi_tok[i], k.lo_tok[i])
        tt = []
        for h in range(4 * g, 4 * g + 4):
            o = (h % 4) * 256
            bs = []
            for r in range(2):
                b = BK.take()
                pe.wait(b.free)
                ws = slice(o + 128 * r, o + 128 * r + 128)
                bs.append((b, k.mm3(b.ap[:, :], wh[:, ws], wl[:, ws], Y.hi[:, h, :], Y.lo[:, h, :],
                                    True, True, Y.ready[h], last=True)))
            t = GR.take()
            ix = GR.take()
            (b0, p0), (b1, p1) = bs
            a = act(lambda e, t=t, b=b0, h=h: e.activation(t.ap, b.ap[:, :], ACT.Sigmoid, bias=vec("b_rg", h)), p0, t.free)
            BK.give(b0, a)
            a2 = act(lambda e, x=ix, b=b1, h=h: e.activation(x.ap, b.ap[:, :], ACT.Sigmoid, bias=vec("b_ig", h)), p1, ix.free)
            BK.give(b1, a2)
            a = act(lambda e, t=t, h=h: e.activation(t.ap, t.ap, ACT.Tanh, scale=SP4[:, 0, h:h + 1]), a, t_sp4)
            xc, tx, ts = xcs[h]
            m = pool(lambda e, x=ix, xc=xc: e.tensor_tensor(x.ap, x.ap, xc.ap[:, 0:T], ALU.mult), a2, tx)
            TR.give(xc, m, *ts)
            tt.append((h, t, a, ix, m))
        k.unit_done(i, bs[1][1])
        for h, t, a, ix, m in tt:
            s, r = TR.take(), TR.take()
            q = act(lambda e, s=s, t=t: e.activation(s.ap[:, 0:T], t.ap, ACT.Sqrt), a, s.free)
            d = dve(lambda e, r=r, t=t: e.tensor_scalar(r.ap[:, 0:T], t.ap, 1.0, None, ALU.add), a, r.free)
            d = dve(lambda e, r=r: e.reciprocal(r.ap[:, 0:T], r.ap[:, 0:T]), d)
            n = dve(lambda e, t=t: e.tensor_scalar(t.ap, t.ap, -1.0, 1.0, ALU.mult, ALU.add), q, d)
            n = dve(lambda e, t=t, r=r: e.tensor_tensor(t.ap, t.ap, r.ap[:, 0:T], ALU.mult), n, d)
            q = dve(lambda e, s=s, r=r: e.scalar_tensor_tensor(s.ap[:, 0:T], s.ap[:, 0:T], 2.0, r.ap[:, 0:T],
                                                              ALU.mult, ALU.mult), q, d)
            TR.give(r, q, n)
            q2 = dve(lambda e, ix=ix, s=s: e.tensor_tensor(ix.ap, ix.ap, s.ap[:, 0:T], ALU.mult), q, m)
            TR.give(s, q2)
            sc = dve(lambda e, t=t, ix=ix: e.tensor_tensor_scan(ix.ap, t.ap, ix.ap, 0.0, ALU.mult, ALU.add), n, q2)
            GR.give(t, sc)
            heads[h] = (ix, sc)

    def gates(g):
        for h in range(4 * g, 4 * g + 4):
            b = BK.take()
            t = k.linear(("in_odd", 0, 12 + h), P0, range(8), b)
            ix, sc = heads[h]
            Y.free = [k.pe_tok.get(rg_unit[g])]
            m = gate(b, t, lag, ix, sc, Y, h)
            GR.give(ix, m)
            bg(8)
        return t

    rg_unit = {}
    for g in range(3):
        for h in range(4 * g, 4 * g + 4):
            xr_unit(h)
            bg(6)
        if g:
            gates(g - 1)
        rg_unit[g] = len(k.used)
        rgig(g)
    t = gates(2)
    bg(len(k.bg))
    P0.free = [t]
    lag.end([dve.last])
    for n in range(8):
        b = BK.take()
        t = k.linear(("out_odd", 0, n), Y, range(8), b)
        BK.give(b, add_to_h(n, b.ap[:, :], t))
        if n % 2 == 1:
            i = k.weights(("out_odd4", 0, n // 2))
            wh, wl = k.tiles(i)
            pe.wait(k.hi_tok[i], k.lo_tok[i])
            for m in range(2):
                b = BK.take()
                pe.wait(b.free)
                for kc in range(4):
                    ws = slice((4 * m + kc) * 128, (4 * m + kc) * 128 + 128)
                    t = k.mm3(b.ap[:, :], wh[:, ws], wl[:, ws], Y.hi[:, 8 + kc, :], Y.lo[:, 8 + kc, :],
                              kc == 0, kc == 3, Y.ready[8 + kc], last=kc == 3)
                c = n - 1 + m
                BK.give(b, add_to_h(c, b.ap[:, :], t))
                H_rd[c] = [sumsq(H[:, c, :], c, H_tok[c], c == 0)]
            k.unit_done(i, t)
    fence = k.fence()
    scope.close()
    if done("odd"):
        psc.close()
        return

    k.stage("ssm")
    scope = ExitStack()
    U = sb("U", [128, 8, T], F32, scope)
    SS = sb("SS", [128, 65, 2, 32], F32, scope)
    BX = sb("BX", [128, 2, 32, 32], F32, scope)
    sub = ExitStack()
    PX = sb("PX", [128, 2, 2, 8, 128], F32, sub)
    MT = sb("MT", [128, 2, 2, 8, 128], F32, sub)
    t_px = pool(lambda e: e.memset(PX[:, :, :, :, :], 0.0), fence)
    t_ss = pool(lambda e: e.memset(SS[:, 0, :, :], 0.0), fence)
    rs, rt, ri = stat_b(stat_a(1e-6))
    for c in range(8):
        H_tok[c] = dve(lambda e, c=c, rs=rs: e.scalar_tensor_tensor(H[:, c, :], H[:, c, :], vec("final_norm", c), rs,
                                                            ALU.mult, ALU.mult), rt, H_tok[c], H_rd[c])
        H_rd[c] = [sumsq(H[:, c, :], c, H_tok[c], c == 0)]
    rs_free[ri] = [H_tok[7]]
    if done("fnorm"):
        sub.close()
        scope.close()
        psc.close()
        return

    px_free = [[], []]
    mt_free = [[], []]
    px_tok = {}

    def in_tables(q):
        z = q % 2
        t = [TR.take() for _ in range(4)]
        tv = [s.ap[:, 0:512].rearrange("p (j g h) -> p j g h", j=8, g=4) for s in t]

        def pw(r):
            return PW[:, r, 7::-1, 4 * q:4 * q + 4].unsqueeze(3).to_broadcast([128, 8, 4, 16])

        def b_(r):
            return BB[:, r, 4 * q:4 * q + 4, :].unsqueeze(1).to_broadcast([128, 8, 4, 16])
        tk = []
        for i, (x, y) in enumerate(((0, 0), (1, 1), (0, 1), (1, 0))):
            eng = pool if i % 2 else dve
            tk.append(eng(lambda e, i=i, x=x, y=y: e.tensor_tensor(tv[i], pw(x), b_(y), ALU.mult), t[i].free, ch["t"]))
        out = []
        for r, op in ((0, ALU.subtract), (1, ALU.add)):
            for par in range(2):
                ps = slice(64 * par, 64 * par + 64)
                o = PX[ps, z, r, :, :].rearrange("p j (g w h) -> p j g w h", g=4, w=2)[:, :, :, par, :]
                out.append(dve(lambda e, r=r, op=op, ps=ps, o=o: e.tensor_tensor(o, tv[2 * r][ps], tv[2 * r + 1][ps], op),
                               tk[2 * r], tk[2 * r + 1], px_free[z], t_px))
        for s in t:
            TR.give(s, out[-1])
        px_tok[q] = [out[1], out[3]]

    def transposes(q):
        z = q % 2
        toks = []
        last = None
        for r in range(2):
            for hf in range(2):
                b = BK.take()
                pe.wait(b.free, px_tok[q])
                for j in range(4):
                    last = pe(lambda e, b=b, r=r, j=j, hf=hf: e.transpose(
                        b.ap[:, j * 128:j * 128 + 128], PX[:, z, r, 4 * hf + j, :], ident), quiet=j < 3)
                a = act(lambda e, b=b, r=r, hf=hf: e.activation(
                    MT[:, z, r, 4 * hf:4 * hf + 4, :].rearrange("p a b -> p (a b)"), b.ap[:, :], ACT.Copy), last, mt_free[z])
                BK.give(b, a)
                toks.append(a)
        a = act(lambda e: e.activation(BX[:, :, 4 * q:4 * q + 4, :].rearrange("p r g h -> p r (g h)"),
                                       PX[:, z, :, 7, :], ACT.Copy), px_tok[q])
        px_free[z] = [last, a]
        return toks, a

    in_tables(0)
    rs, rt, ri = stat_b(stat_a(1e-6))
    in_tables(1)
    u_tok = []
    for c in range(8):
        u_tok.append(dve(lambda e, c=c, rs=rs: e.scalar_tensor_tensor(U[:, c, :], H[:, c, :], vec("norm_mix", c), rs,
                                                              ALU.mult, ALU.mult), rt, H_tok[c]))
        H_rd[c] = H_rd[c] + [u_tok[c]]
    rs_free[ri] = [u_tok[7]]
    v_tok = []
    bx_tok = []
    SSv = SS[:, :, :, :].rearrange("p c r x -> p r c x")
    for q in range(8):
        z = q % 2
        mt, a = transposes(q)
        bx_tok.append(a)
        for pr in range(4):
            b = BK.take()
            pe.wait(b.free, mt, u_tok[q])
            p_ = slice(32 * pr, 32 * pr + 32)
            for r in range(2):
                for j in range(8):
                    t = pe(lambda e, b=b, r=r, j=j, p_=p_: e.matmul(
                        b.ap[:, 64 * r:64 * r + 64], MT[p_, z, r, j, :], U[p_, q, j::8], start=j == 0, stop=j == 7),
                        quiet=not (r == 1 and j == 7)) if False else pe(
                        (lambda b, r, j, p_, z, q: lambda e: e.matmul(
                            b.ap[:, 64 * r:64 * r + 64], MT[p_, z, r, j, :], U[p_, q, j::8], start=j == 0, stop=j == 7))(b, r, j, p_, z, q),
                        quiet=not (r == 1 and j == 7))
            a = act((lambda b, x: lambda e: e.activation(SSv[:, :, 1:65, x], b.ap[:, 0:128].rearrange("p (r c) -> p r c", r=2),
                                                        ACT.Copy))(b, 4 * q + pr), t, fence)
            BK.give(b, a)
        v_tok.append(a)
        mt_free[z] = [t]
        if q + 2 < 8:
            in_tables(q + 2)
    tS = [v_tok[-1], t_ss]
    SC4 = TR.take()
    s1, s2 = SC4.ap[:, 0:64].rearrange("p (r x) -> p r x", r=2), SC4.ap[:, 64:128].rearrange("p (r x) -> p r x", r=2)
    w = SC4.free
    for c in range(2, 64):
        a = dve(lambda e, c=c: e.tensor_tensor(s1, SS[:, c - 1, :, :], A8[:, 0, :, :], ALU.mult), tS, w)
        b = dve(lambda e, c=c: e.tensor_tensor(s2, SS[:, c - 1, ::-1, :], A8[:, 1, :, :], ALU.mult), tS, w)
        a = dve(lambda e, c=c: e.tensor_tensor(s1, s1, SS[:, c, :, :], ALU.add), a)
        tS = dve(lambda e, c=c: e.tensor_tensor(SS[:, c, :, :], s1, s2, ALU.add), a, b)
        w = tS
    TR.give(SC4, tS)
    fence2 = [pe.last, act.last, dve.last, pool.last]
    sub.close()
    sub = ExitStack()
    CA = sb("CA", [128, 2, 2, 4, 9, 32], F32, sub)
    BD = sb("BD", [128, 2, 8, 128], F32, sub)
    t_ca = pool(lambda e: e.memset(CA[:, :, :, :, :, :], 0.0), fence2)
    t_bd = pool(lambda e: e.memset(BD[:, :, :, :], 0.0), fence2)
    cr_, ci_ = (v3(SPT[:, SC[n]:SC[n] + 512]) for n in ("cr", "ci"))
    ca_free = [[], []]
    bd_free = [[], []]
    G = P0
    for q in range(8):
        z = q % 2
        t = [TR.take() for _ in range(4)]
        tv = [s.ap[:, 0:576].rearrange("p (g m h) -> p g m h", g=4, m=9) for s in t]

        def pw(r, q=q):
            return PW[:, r, :, 4 * q:4 * q + 4].rearrange("p m g -> p g m").unsqueeze(3).to_broadcast([128, 4, 9, 16])

        def c_(x, q=q):
            return x[:, 4 * q:4 * q + 4, :].unsqueeze(2).to_broadcast([128, 4, 9, 16])
        tk = []
        for i, (x, y) in enumerate(((cr_, 0), (ci_, 1), (cr_, 1), (ci_, 0))):
            eng = pool if i % 2 else dve
            tk.append(eng(lambda e, o=tv[i], x=c_(x), y=pw(y): e.tensor_tensor(o, x, y, ALU.mult), t[i].free, ch["t"]))
        out = []
        for par in range(2):
            ps = slice(64 * par, 64 * par + 64)
            o = CA[ps, z, 0, :, :, 16 * par:16 * par + 16]
            out.append(dve(lambda e, ps=ps, o=o, x=tv[0], y=tv[1]: e.tensor_tensor(o, x[ps], y[ps], ALU.subtract),
                           tk[0], tk[1], ca_free[z], t_ca))
            o = CA[ps, z, 1, :, :, 16 * par:16 * par + 16]
            n = dve(lambda e, ps=ps, x=tv[2]: e.tensor_scalar(x[ps], x[ps], -1.0, None, ALU.mult), tk[2])
            out.append(dve(lambda e, ps=ps, o=o, x=tv[2], y=tv[3]: e.tensor_tensor(o, x[ps], y[ps], ALU.subtract),
                           n, tk[3], ca_free[z], t_ca))
        for s in t:
            TR.give(s, out[-1])
        b = BK.take()
        pe.wait(b.free, out, bx_tok)
        for pr in range(4):
            for r in range(2):
                t_k = pe((lambda b, pr, r, z, q: lambda e: e.matmul(
                    b.ap[32 * pr:32 * pr + 32, 0:256], BX[:, r, 4 * q + pr, :],
                    CA[:, z, r, pr, 0:8, :].rearrange("p m h -> p (m h)"), start=r == 0, stop=r == 1))(b, pr, r, z, q),
                    quiet=not (pr == 3 and r == 1))
        bd = []
        for pr in range(4):
            p_ = slice(32 * pr, 32 * pr + 32)
            bd.append(act((lambda b, p_, z: lambda e: e.activation(
                BD[p_, z, :, p_], b.ap[p_, 0:256].rearrange("p (m h) -> p m h", m=8), ACT.Copy))(b, p_, z),
                t_k, bd_free[z], t_bd))
        BK.give(b, bd[-1])
        b = BK.take()
        pe.wait(b.free, u_tok[q], tS)
        for pr in range(4):
            pass
        pe.wait(bd)
        bv = b.ap[:, :].rearrange("p (i c) -> p i c", i=8)
        uv = U[:, q, :].rearrange("p (c i) -> p i c", i=8)
        for tau in range(8):
            pe(lambda e, bv=bv, uv=uv, z=z, tau=tau: e.matmul(bv[:, tau:8, :], BD[:, z, tau, :], uv[:, 0:8 - tau, :],
                                                             start=tau == 0, stop=False, skip_group_check=True), quiet=True)
        for pr in range(4):
            p_ = slice(32 * pr, 32 * pr + 32)
            for i in range(8):
                for r in range(2):
                    t_y = pe((lambda bv, p_, i, r, pr, z, q: lambda e: e.matmul(
                        bv[p_, i, :], CA[:, z, r, pr, 1 + i, :], SS[:, 0:64, r, 4 * q + pr], start=False,
                        stop=r == 1 and i == 7, skip_group_check=True))(bv, p_, i, r, pr, z, q),
                        quiet=not (pr == 3 and i == 7 and r == 1))
        ca_free[z] = [t_y]
        bd_free[z] = [t_y]
        y, g1 = TR.take(), TR.take()
        yv = y.ap[:, 0:T].rearrange("p (c i) -> p i c", i=8)
        d = dve(lambda e, yv=yv, uv=uv, bv=bv, q=q: e.scalar_tensor_tensor(yv, uv, vec("ssm_d", q), bv, ALU.mult, ALU.add),
                t_y, y.free)
        BK.give(b, d)
        a = act(lambda e, y=y, g=g1: e.activation(g.ap[:, 0:T], y.ap[:, 0:T], ACT.Square), d, g1.free)
        a = dve(lambda e, g=g1: e.tensor_scalar(g.ap[:, 0:T], g.ap[:, 0:T], 0.044715, 1.0, ALU.mult, ALU.add), a)
        a = dve(lambda e, y=y, g=g1: e.tensor_tensor(g.ap[:, 0:T], g.ap[:, 0:T], y.ap[:, 0:T], ALU.mult), a)
        a = act(lambda e, g=g1: e.activation(g.ap[:, 0:T], g.ap[:, 0:T], ACT.Sigmoid, scale=2 * math.sqrt(2 / PI)), a)
        a = dve(lambda e, y=y, g=g1: e.tensor_tensor(g.ap[:, 0:T], g.ap[:, 0:T], y.ap[:, 0:T], ALU.mult), a)
        TR.give(y, a)
        TR.give(g1, *split(G, q, g1.ap[:, 0:T], a))
    fence = k.fence()
    sub.close()
    scope.close()
    psc.close()
    if done("ssmx"):
        return
    scope = ExitStack()
    P1 = Split(sb("P1hb", [128, 8, T], F32R, scope), sb("P1lb", [128, 8, T], F32R, scope))
    P2 = Split(sb("P2hb", [128, 8, T], F32R, scope), sb("P2lb", [128, 8, T], F32R, scope))
    P1.free = P2.free = fence
    for n in range(8):
        b = BK.take()
        t = k.linear(("glu", 0, 8 + n), P0, range(8), b)
        s = TR.take()
        a = act(lambda e, b=b, s=s: e.activation(s.ap[:, 0:T], b.ap[:, :], ACT.Sigmoid), t, s.free)
        BK.give(b, a)
        b = BK.take()
        t = k.linear(("glu", 0, n), P0, range(8), b)
        d = dve(lambda e, b=b, s=s: e.tensor_tensor(s.ap[:, 0:T], s.ap[:, 0:T], b.ap[:, :], ALU.mult), t, a)
        BK.give(b, d)
        TR.give(s, add_to_h(n, s.ap[:, 0:T], d))
        norm_in(n, [(P1, "norm_mlp", 0)])
    P0.free = [t]
    if done("mix0"):
        scope.close()
        return

    def mlp(l, src, ha, hb, dst):
        bufs = [ha, hb]
        lag = Lag()

        def up(qt):
            dstq = bufs[qt % 2]
            for c in range(8):
                b = BK.take()
                t = k.linear((f"up{l}", 0, 8 * qt + c), src, range(8), b)

                def evac(rs, rt, b=b, t=t, c=c):
                    s = TR.take()
                    d = dve(lambda e: e.scalar_tensor_tensor(s.ap[:, 0:T], b.ap[:, :], 0.0, rs, ALU.max, ALU.mult),
                            t, rt, s.free)
                    BK.give(b, d)
                    a = act(lambda e: e.activation(dstq.hi[:, c, :], s.ap[:, 0:T], ACT.Square), d, dstq.free)
                    a2 = act(lambda e: e.activation(s.ap[:, 0:T], s.ap[:, 0:T], ACT.Square), a)
                    x = dve(lambda e: e.tensor_tensor(dstq.lo[:, c, :], s.ap[:, 0:T], dstq.hi[:, c, :].bitcast(F32),
                                                      ALU.subtract), a2, dstq.free)
                    TR.give(s, x)
                    dstq.ready[c] = [a, x]
                lag.put(evac)
            return t

        def down(qt):
            x = bufs[qt % 2]
            for n in range(8):
                b = BK.take()
                t = k.linear((f"down{l}", qt, n), x, range(8), b)
                BK.give(b, add_to_h(n, b.ap[:, :], t))
                if qt == 3:
                    norm_in(n, [(dst, "norm_ple", 8 * l)])
            x.free = [t]
        up(0)
        up(1)
        down(0)
        up(2)
        down(1)
        src.free = [up(3)]
        lag.end([dve.last])
        down(2)
        down(3)

    def proj(l, PJ, PT):
        for kc in range(2):
            s = TR.take()
            a = k.load(s.ap[:, 0:T], D["pT"][l][:, kc, :], s.free, sem=f"d_p{l}{kc}")
            TR.give(s, *split(PT, kc, s.ap[:, 0:T], a))
        toks = []
        for h in range(2):
            i = k.weights((f"proj{l}", 0, h))
            wh, wl = k.tiles(i)
            pe.wait(k.hi_tok[i], k.lo_tok[i])
            for n in range(4):
                b = BK.take()
                pe.wait(b.free)
                for kc in range(2):
                    ws = slice((n * 2 + kc) * 128, (n * 2 + kc) * 128 + 128)
                    t = k.mm3(b.ap[:, :], wh[:, ws], wl[:, ws], PT.hi[:, kc, :], PT.lo[:, kc, :],
                              kc == 0, kc == 1, PT.ready[kc], last=kc == 1)
                toks.append(act(lambda e, b=b, c=4 * h + n: e.activation(PJ[:, c, :], b.ap[:, :], ACT.Copy), t, PT.free))
                BK.give(b, toks[-1])
            k.unit_done(i, t)
        return toks

    def ple(l, src, PJ, tp, outs):
        lag = Lag()
        for n in range(8):
            b = BK.take()
            t = k.linear((f"gate{l}", 0, n), src, range(8), b)

            def evac(rs, rt, b=b, t=t, n=n):
                s = TR.take()
                d = scale_psum(s.ap[:, 0:T], b, rs, rt, t, s.free)
                BK.give(b, d)
                a = act(lambda e: e.activation(s.ap[:, 0:T], s.ap[:, 0:T], ACT.Sigmoid), d)
                d = pool(lambda e: e.tensor_tensor(s.ap[:, 0:T], s.ap[:, 0:T], PJ[:, n, :], ALU.mult), a, tp[n])
                TR.give(s, add_to_h(n, s.ap[:, 0:T], d))
                norm_in(n, outs)
            lag.put(evac)
        src.free = [t]
        lag.end([dve.last])

    PJ = sb("PJ", [128, 8, T], F32, scope)
    PT = Split(sb("PTh", [128, 2, T], F32R, scope), sb("PTl", [128, 2, T], F32R, scope))
    PT.free = fence
    tp = proj(0, PJ, PT)
    mlp(0, P1, P0, P2, P1)
    if done("mlp0"):
        scope.close()
        return
    ple(0, P1, PJ, tp, [(P0, "norm_mix", 8), (P2, "kv_norm", 0)])
    if done("ple0"):
        scope.close()
        return
    fence = k.fence()
    scope.close()

    k.stage("att")
    scope = ExitStack()
    P1 = Split(sb("P1hc", [128, 8, T], F32R, scope), sb("P1lc", [128, 8, T], F32R, scope))
    P2b = Split(sb("P2hc", [128, 8, T], F32R, scope), sb("P2lc", [128, 8, T], F32R, scope))
    P1.free = fence
    at = ExitStack()
    KT = sb("KT", [128, 2, T], F32, at)
    V = sb("V", [128, 4, 256], F32, at)
    Q = sb("Q", [128, 8, T], F32, at)
    RO = sb("RO", [128, 2, T], F32, at)
    AS = ACC[:, :].rearrange("p (n k) -> p n k", n=16)
    RK = sb("RK", [128, 4], F32, at)
    t_ro = k.load(RO[:, :, :], D["rope"], fence, sem="d_ro")
    rot = CO[:, CC["rot"]:CC["rot"] + 128]
    lag = Lag()
    pend = []

    def rope_out(dst, s, d):
        b = BK.take()
        t = pe(lambda e: e.matmul(b.ap[:, :], rot, s.ap[:, 0:T], start=True, stop=True), d, b.free)
        m = TR.take()
        x = dve(lambda e: e.tensor_tensor(m.ap[:, 0:T], b.ap[:, :], RO[:, 1, :], ALU.mult), t, m.free, t_ro)
        BK.give(b, x)
        y = pool(lambda e: e.tensor_tensor(s.ap[:, 0:T], s.ap[:, 0:T], RO[:, 0, :], ALU.mult), t, t_ro)
        r = dve(lambda e: e.tensor_tensor(dst, s.ap[:, 0:T], m.ap[:, 0:T], ALU.add), x, y, fence)
        TR.give(s, r)
        TR.give(m, r)
        return r

    rope_tok = {}

    def proj_rope(what, n, src, dst, key):
        b = BK.take()
        t = k.linear((what, 0, n), src, range(8), b)

        def evac(rs, rt):
            s = TR.take()
            d = scale_psum(s.ap[:, 0:T], b, rs, rt, t, s.free)
            BK.give(b, d)
            pend.append((dst, s, d, key))
        lag.put(evac)
        return t

    def ropes(keep):
        while len(pend) > keep:
            dst, s, d, key = pend.pop(0)
            rope_tok[key] = rope_out(dst, s, d)

    for n in range(2):
        proj_rope("wk", n, P2, KT[:, n, :], ("k", n))
    t_rk = dve(lambda e: e.tensor_copy(RK[:, :], SM[:, 8:12]), lag.a, fence)
    vb = [BK.take() for _ in range(4)]
    for hf in range(2):
        i = k.weights(("wv", 0, hf))
        wh, wl = k.tiles(i)
        pe.wait(k.hi_tok[i], k.lo_tok[i], [b.free for b in vb])
        for tb in range(4):
            for kc in range(4):
                c = 4 * hf + kc
                xh = P2.hi[:, c, 128 * tb:128 * tb + 128]
                xl = P2.lo[:, c, 128 * tb:128 * tb + 128]
                ws = slice(256 * kc, 256 * kc + 256)
                o = vb[tb].ap[:, 0:256]
                pe.wait(P2.ready[c])
                pe(lambda e, o=o, xh=xh, w=wh[:, ws], c=c: e.matmul(o, xh, w, start=c == 0, stop=False), quiet=True)
                pe(lambda e, o=o, xh=xh, w=wl[:, ws]: e.matmul(o, xh, w, start=False, stop=False), quiet=True)
                t = pe(lambda e, o=o, xl=xl, w=wh[:, ws], c=c: e.matmul(o, xl, w, start=False, stop=c == 7),
                       quiet=kc != 3)
            if hf == 1:
                a = act(lambda e, o=o, tb=tb: e.activation(V[:, tb, :], o, ACT.Copy, scale=RK[:, tb:tb + 1]), t, t_rk, fence)
                BK.give(vb[tb], a)
                rope_tok["v", tb] = a
        k.unit_done(i, t)
    ropes(0)
    for n in range(8):
        t = proj_rope("wq", n, P0, Q[:, n, :], ("q", n))
        ropes(1)
    ropes(0)
    P0.free = [t]
    lag.end([dve.last])
    mask = CO[:, CC["mask"]:CC["mask"] + 256]
    sink = VE[:, VCOL["sinks"]:VCOL["sinks"] + 16]
    o_parts = {}

    def scores(n):
        blk, kv = n // 4, n % 4
        k0, nk = (128, 128) if blk == 0 else (0, 256)
        p_ = slice(64 * (kv % 2), 64 * (kv % 2) + 64)
        ks = slice(128 * blk - 128 + k0, 128 * blk + 128)
        st = AS[:, n, :]
        out, mx = [], []
        for hp in range(2):
            b = BK.take()
            pe.wait(b.free, rope_tok["k", kv // 2])
            for j in range(2):
                c = 4 * (kv // 2) + 2 * hp + j
                t = pe((lambda b, j, c: lambda e: e.matmul(
                    b.ap[:, 256 * j:256 * j + nk], Q[p_, c, 128 * blk:128 * blk + 128], KT[p_, kv // 2, ks],
                    start=True, stop=True))(b, j, c), rope_tok["q", c], quiet=j == 0)
            s = TR.take()
            bv = b.ap[:, :].rearrange("p (a k) -> p a k", a=2)[:, :, 0:nk]
            sv = s.ap[:, 0:512].rearrange("p (a k) -> p a k", a=2)[:, :, 0:nk]
            mv = mask[:, k0:256].unsqueeze(1).to_broadcast([128, 2, nk])
            d = dve(lambda e, bv=bv, sv=sv: e.scalar_tensor_tensor(sv, bv, 0.125, mv, ALU.mult, ALU.add), t, s.free)
            BK.give(b, d)
            mx.append(dve(lambda e, sv=sv, hp=hp: e.tensor_reduce(st[:, 2 * hp:2 * hp + 2], sv, AX.X, ALU.max), d, acc_free[0]))
            out.append((s, sv))
        sk = sink[:, 4 * kv:4 * kv + 4]
        d = dve(lambda e: e.tensor_tensor(st[:, 0:4], st[:, 0:4], sk, ALU.max), mx)
        d1 = dve(lambda e: e.tensor_scalar(st[:, 4:8], st[:, 0:4], -1.0, None, ALU.mult), d)
        d2 = dve(lambda e: e.tensor_tensor(st[:, 8:12], sk, st[:, 0:4], ALU.subtract), d)
        ex = []
        for h in range(4):
            sv = out[h // 2][1][:, h % 2, :]
            ex.append(act(lambda e, sv=sv, h=h: e.activation(sv, sv, ACT.Exp, bias=st[:, 4 + h:5 + h],
                                                            accum_out=st[:, 12 + h:13 + h]), d1))
        a = act(lambda e: e.activation(st[:, 8:12], st[:, 8:12], ACT.Exp), d2)
        d = dve(lambda e: e.tensor_tensor(st[:, 16:20], st[:, 12:16], st[:, 8:12], ALU.add), a, ex)
        d = dve(lambda e: e.reciprocal(st[:, 16:20], st[:, 16:20]), d)
        w = []
        for h in range(4):
            sv = out[h // 2][1][:, h % 2, :]
            w.append(dve(lambda e, sv=sv, h=h: e.tensor_scalar(sv, sv, st[:, 16 + h:17 + h], None, ALU.mult), d, ex[h]))
        return out, w

    def attend(n, out, w):
        blk, kv = n // 4, n % 4
        halves = [1] if blk == 0 else [0, 1]
        wt = []
        for hf in halves:
            b = BK.take()
            pe.wait(b.free)
            for h in range(4):
                sv = out[h // 2][1][:, h % 2, 128 * (hf if blk else 0):128 * (hf if blk else 0) + 128]
                t = pe((lambda b, h, sv: lambda e: e.transpose(b.ap[:, 128 * h:128 * h + 128], sv, ident))(b, h, sv),
                       w[h], quiet=h < 3)
            s = TR.take()
            a = act((lambda b, s: lambda e: e.activation(s.ap[:, 0:512], b.ap[:, :], ACT.Copy))(b, s), t, s.free)
            BK.give(b, a)
            wt.append((s, a, blk - 1 + hf))
        for s, _ in out:
            TR.give(s, t)
        b = BK.take()
        pe.wait(b.free)
        p_ = slice(64 * (kv % 2), 64 * (kv % 2) + 64)
        for i, (s, a, vb_) in enumerate(wt):
            t = pe((lambda b, s, vb_, i: lambda e: e.matmul(b.ap[p_, :], V[:, vb_, 64 * kv:64 * kv + 64], s.ap[:, 0:512],
                                                          start=i == 0, stop=i == len(wt) - 1))(b, s, vb_, i),
                   a, rope_tok["v", vb_], quiet=i < len(wt) - 1)
        for s, _, _ in wt:
            TR.give(s, t)
        cs = slice(4 * (kv // 2), 4 * (kv // 2) + 4)
        ts = slice(128 * blk, 128 * blk + 128)
        bv = b.ap[p_, :].rearrange("p (c t) -> p c t", c=4)
        hi, lo = P1.hi[p_, cs, ts], P1.lo[p_, cs, ts]
        a = act(lambda e: e.activation(hi, bv, ACT.Copy), t, P1.free)
        d = dve(lambda e: e.tensor_tensor(lo, bv, hi.bitcast(F32), ALU.subtract), a, P1.free)
        BK.give(b, d)
        for c in range(4 * (kv // 2), 4 * (kv // 2) + 4):
            o_parts.setdefault(c, []).extend([a, d])

    prev = None
    for n in range(16):
        cur = (n, *scores(n))
        if prev:
            attend(*prev)
        prev = cur
    attend(*prev)
    for c in range(8):
        P1.ready[c] = o_parts[c]
    acc_free[0] = [dve.last, act.last]
    fence = k.fence()
    at.close()
    PJ = sb("PJb", [128, 8, T], F32, scope)
    PT = Split(sb("PThb", [128, 2, T], F32R, scope), sb("PTlb", [128, 2, T], F32R, scope))
    PT.free = fence
    P2b.free = fence
    for n in range(8):
        b = BK.take()
        t = k.linear(("wo", 0, n), P1, range(8), b)
        BK.give(b, add_to_h(n, b.ap[:, :], t))
        norm_in(n, [(P0, "norm_mlp", 8)])
    P1.free = [t]
    if done("mix1"):
        scope.close()
        return
    tp = proj(1, PJ, PT)
    mlp(1, P0, P1, P2b, P0)
    if done("mlp1"):
        scope.close()
        return
    ple(1, P0, PJ, tp, [])
    rs, rt, ri = stat_b(stat_a(1e-6))
    for c in range(8):
        s = TR.take()
        d = dve(lambda e, c=c, s=s, rs=rs: e.scalar_tensor_tensor(s.ap[:, 0:T], H[:, c, :], vec("norm_final", c), rs,
                                                          ALU.mult, ALU.mult), rt, H_tok[c], s.free)
        o = k.load(D["out"][c], s.ap[:, 0:T], d, sem="d_out")
    k.sp.wait(o)
    scope.close()


def matrices(x):
    heads = [(0, 4), (1, 5), (2, 6), (3, 7), (8, 12), (9, 13), (10, 14), (11, 15)]
    cols = np.concatenate([np.arange(64) + 64 * h for pair in heads for h in pair])
    rg = np.concatenate([x["w_rg"][0], x["w_ig"][0]])
    return {
        "in_even": x["w_in_even"][0], "out_even": x["w_out_even"][0], "pool": x["pool_w"][0],
        "in_odd": x["w_in_odd"][0], "out_odd": x["w_out_odd"][0], "rgig": rg,
        "glu": x["ssm_w_glu_2"][0], "up0": x["w_up_2"][0], "down0": x["w_down_2"][0],
        "up1": x["w_up_2"][1], "down1": x["w_down_2"][1], "gate0": x["w_ple_gate_2"][0],
        "gate1": x["w_ple_gate_2"][1], "proj0": x["w_ple_proj_2"][0], "proj1": x["w_ple_proj_2"][1],
        "wk": x["w_k_2"], "wv": x["w_v_2"], "wq": x["w_q_2"][0][:, cols], "wo": x["w_o_2"][0][cols, :],
    }


def unit_tiles(what):
    name, a, b = what
    if name == "pool":
        return None
    if name == "rgig":
        return None
    if name in ("proj0", "proj1"):
        return [(kc, 4 * b + n) for n in range(4) for kc in range(2)]
    if name == "out_odd4":
        return [(8 + kc, 2 * b + m) for m in range(2) for kc in range(4)]
    if name == "wv":
        return [(4 * b + kc, n) for kc in range(4) for n in range(2)]
    return [(8 * a + kc, b) for kc in range(8)]


def pack(order, mats):
    out = np.empty((len(order), 128, 8, 128), np.float32)
    for i, what in enumerate(order):
        name, a, b = what
        m = mats["out_odd" if name == "out_odd4" else name]
        if name == "pool":
            for g in range(2):
                for kc in range(2):
                    for n in range(2):
                        out[i, :, (g * 2 + kc) * 2 + n, :] = m[2 * b + g, kc * 128:kc * 128 + 128, n * 128:n * 128 + 128]
        elif name == "rgig":
            for h in range(4):
                out[i, :, 2 * h, :] = m[4 * b + h]
                out[i, :, 2 * h + 1, :] = m[12 + 4 * b + h]
        else:
            for j, (r, c) in enumerate(unit_tiles(what)):
                out[i, :, j, :] = m[r * 128:r * 128 + 128, c * 128:c * 128 + 128]
    return out.reshape(len(order), 128, 1024)


def vectors(x):
    cols = []

    def add(v, n):
        cols.append(np.asarray(v).reshape(n, 128).T)

    add(x["norm_even"][0], 8)
    cols.append(x["conv_a_w"][0].reshape(31, 8, 128).transpose(2, 1, 0).reshape(128, 248))
    for n in ("conv_a_b", "ln_a_g", "ln_a_b", "pool_b", "pool_scale", "norm_odd"):
        add(x[n][0], 8)
    cols.append(x["conv_c_w"][0].reshape(4, 12, 128).transpose(2, 1, 0).reshape(128, 48))
    for n in ("conv_c_b", "b_rg", "b_ig", "lru_lambda"):
        add(x[n][0], 12)
    add(x["final_norm"], 8)
    add(x["norm_mix_2"], 16)
    add(x["ssm_d_2"][0], 8)
    add(x["kv_norm_2"], 8)
    add(x["norm_mlp_2"], 16)
    add(x["norm_ple_2"], 16)
    add(x["norm_final_2"], 8)
    cols.append(np.repeat(x["attn_sinks_2"][0][None, :], 128, axis=0))
    return np.ascontiguousarray(np.concatenate(cols, axis=1))


def constants():
    c = np.zeros((128, NCC), np.float32)
    c[:, 0:128] = np.eye(128, dtype=np.float32)
    for base in (0, 64):
        for d in range(8):
            c[base + d + 8, CC["rot"] + base + d] = -1.0
            c[base + d, CC["rot"] + base + d + 8] = 1.0
    i = np.arange(128)[:, None]
    j = np.arange(256)[None, :]
    ok = (j <= i + 128) & (i + 128 - j < 128)
    c[:, CC["mask"]:CC["mask"] + 256] = np.where(ok, 0.0, -1e30)
    for g in range(4):
        w = 2 << g
        c[:, CC["cnt"] + 16 * g:CC["cnt"] + 16 * g + 16] = w / np.minimum(np.arange(1, 17), w)
    return c


def rope_tables():
    inv = np.float32(500000.0) ** (-np.arange(0, 16, 2, dtype=np.float32) / np.float32(16))
    ang = np.arange(T, dtype=np.float32)[None, :] * inv[:, None].astype(np.float32)
    r = np.zeros((128, 2, T), np.float32)
    r[:, 0, :] = 1.0
    for base in (0, 8, 64, 72):
        r[base:base + 8, 0, :] = np.cos(ang)
        r[base:base + 8, 1, :] = np.sin(ang)
    return r


def ssm_parameters(x):
    def gn(a):
        return a.reshape(32, 2, 64).transpose(1, 2, 0).reshape(128, 32)

    ldt = np.repeat(x["ssm_log_dt_2"][0][:, None], 64, axis=1)
    b = [x[n][0].reshape(32, 2, 64, 16).transpose(1, 2, 0, 3).reshape(128, 512) for n in ("ssm_b_re_2", "ssm_b_im_2")]
    c = [x[n][0].reshape(32, 2, 16, 64).transpose(1, 3, 0, 2).reshape(128, 512) for n in ("ssm_c_re_2", "ssm_c_im_2")]
    return np.ascontiguousarray(np.concatenate(
        [gn(x["ssm_lambda_re_2"][0]), gn(x["ssm_lambda_im_2"][0]), gn(ldt)] + b + c, axis=1))


def build(nc, order, arrays, stop=None):
    D = {n: nc.dram_tensor(f"in_{n}", a, F32, kind="ExternalInput").ap() for n, a in arrays.items()}
    D["out"] = nc.dram_tensor("out_0", (8, 128, T), F32, kind="ExternalOutput").ap()
    with ExitStack() as ctx:
        k = Builder(nc, ctx, order)
        program(nc, ctx, k, D, stop)
        if order is not None:
            with nc.Block() as block:
                k.emit(block)
    return k.used


def layout(x, order):
    t = lambda a: np.ascontiguousarray(a)
    return {
        "w": pack(order, matrices(x)),
        "xT": t(x["x"][0].T.reshape(8, 128, T)),
        "pT": t(x["p_2"][:, 0].transpose(0, 2, 1).reshape(2, 2, 128, T).transpose(0, 2, 1, 3)),
        "vecs": vectors(x),
        "consts": constants(),
        "rope": rope_tables(),
        "ssm": ssm_parameters(x),
    }


SHAPES = {"w": (1, 128, 1024), "xT": (8, 128, T), "pT": (2, 128, 2, T), "vecs": (128, NV), "consts": (128, NCC),
          "rope": (128, 2, T), "ssm": (128, NSC)}


def kernel(**inputs):
    import concourse.bacc as bacc
    from concourse.bass_utils import run_bass_kernel_spmd

    order = build(bacc.Bacc("TRN2", target_bir_lowering=False, num_devices=1), None, SHAPES)
    x = {n: np.asarray(a) for n, a in inputs.items()}
    arrays = layout(x, order)
    nc = bacc.Bacc("TRN2", target_bir_lowering=False, num_devices=1)
    build(nc, order, {n: a.shape for n, a in arrays.items()})
    r = run_bass_kernel_spmd(nc, [{f"in_{n}": a for n, a in arrays.items()}], core_ids=[0])
    out = r.results[0]["out_0"].reshape(1024, T)
    return np.ascontiguousarray(out.T).reshape(1, T, 1024)
```

```python
import math
from contextlib import ExitStack

import numpy as np
import concourse.bass as bass
from concourse import mybir

F32 = mybir.dt.float32
F32R = mybir.dt.float32r
ALU = mybir.AluOpType
ACT = mybir.ActivationFunctionType
AX = mybir.AxisListType

T = 512
NC8 = 8
PI = math.pi
TWO_PI_HI = 6.28125
TWO_PI_MID = float(np.float32(2 * PI - 6.28125))
TWO_PI_LO = float(np.float32(2 * PI - 6.28125 - TWO_PI_MID))
ROUND = 12582912.0

VECS = [
    ("norm_even", 8), ("conv_a_w", 31 * 8), ("conv_a_b", 8), ("ln_a_g", 8), ("ln_a_b", 8),
    ("pool_b", 8), ("pool_scale", 8), ("norm_odd", 8), ("conv_c_w", 4 * 12), ("conv_c_b", 12),
    ("b_rg", 12), ("b_ig", 12), ("lru_lambda", 12), ("final_norm", 8), ("norm_mix", 16),
    ("ssm_d", 8), ("kv_norm", 8), ("norm_mlp", 16), ("norm_ple", 16), ("norm_final", 8),
    ("sinks", 16),
]
VCOL = {}
_at = 0
for _n, _c in VECS:
    VCOL[_n] = _at
    _at += _c
NV = _at

CC = {"ident": 0, "rot": 128, "mask": 256, "cnt": 512, "sgn": 576}
NCC = 580
SC = {"lre": 0, "lim": 32, "ldt": 64, "br": 96, "bi": 608, "cr": 1120, "ci": 1632, "d4": 2144}
NSC = 2176


class Engine:

    def __init__(self, k, name):
        self.k, self.name, self.items, self.seen, self.sem, self.n = k, name, [], {}, None, 0

    def stage(self, name):
        self.sem, self.n = self.k.semaphore(f"{self.name}_{name}"), 0

    def wait(self, *tokens):
        for t in tokens:
            if isinstance(t, (list, tuple)) and not (len(t) == 2 and isinstance(t[1], int)):
                self.wait(*t)
                continue
            if t is None:
                continue
            sem, value = t
            if self.seen.get(sem, 0) < value:
                self.seen[sem] = value
                self.items.append(("wait", sem, value))

    def __call__(self, fn, *tokens, quiet=False):
        self.wait(*tokens)
        if quiet:
            self.items.append(("op", fn, None, 0))
            return None
        self.n += 1
        self.items.append(("op", fn, self.sem, 1))
        return (self.sem, self.n)

    @property
    def last(self):
        return (self.sem, self.n) if self.n else None


class Slot:

    def __init__(self, ap):
        self.ap, self.free = ap, []


class Ring:

    def __init__(self, aps):
        self.slots = [Slot(a) for a in aps]

    def take(self):
        return self.slots.pop(0)

    def give(self, s, *tokens):
        s.free = list(tokens)
        self.slots.append(s)


class Weave:

    def __init__(self, between=None):
        self.active, self.between = [], between

    def add(self, gen):
        self.active.append(gen)

    def step(self, rounds=1):
        for _ in range(rounds):
            for g in list(self.active):
                try:
                    next(g)
                except StopIteration:
                    self.active.remove(g)
            if self.between:
                self.between()

    def drain(self):
        while self.active:
            self.step()


class Split:

    def __init__(self, hi, lo):
        self.hi, self.lo = hi, lo
        self.free = []
        self.ready = {}


class Builder:
    NR, NS = 3, 3

    def __init__(self, nc, ctx, order):
        self.nc, self.ctx, self.dry = nc, ctx, order is None
        self.order = order or []
        self.used = []
        self.sems = {}
        self.pe, self.act, self.dve, self.pool, self.sp = (Engine(self, n) for n in ("pe", "act", "dve", "pool", "sp"))
        self.engines = (self.pe, self.act, self.dve, self.pool)
        self.bg = []
        self.dma_n = {}

    def semaphore(self, name):
        assert name not in self.sems
        self.sems[name] = self.ctx.enter_context(self.nc.semaphore(name))
        return name

    def stage(self, name):
        for e in self.engines:
            e.stage(name)

    def load(self, dst, src, *tokens, sem):
        self.sp.wait(*tokens)
        if sem not in self.sems:
            self.semaphore(sem)
            self.dma_n[sem] = 0
        self.dma_n[sem] += 16
        self.sp.items.append(("op", lambda e: e.dma_start(dst, src), sem, 16))
        return (sem, self.dma_n[sem])

    def fence(self):
        return [e.last for e in self.engines if e.last]

    def weights_init(self, raw, hi, lo, dram):
        self.raw, self.hi, self.lo, self.dram = raw, hi, lo, dram
        self.hi_tok, self.lo_tok, self.pe_tok, self.raw_tok = {}, {}, {}, {}
        self.next_dma = self.next_split = 0
        for _ in range(self.NR):
            self._dma()

    def _dma(self):
        i = self.next_dma
        if i >= len(self.order):
            return
        self.next_dma += 1
        j = i % self.NR
        w = [self.hi_tok[i - self.NR], self.lo_tok[i - self.NR]] if i >= self.NR else []
        self.raw_tok[i] = self.load(self.raw[:, j, :], self.dram[i, :, :], *w, sem=f"raw{j}")

    def _split(self):
        i = self.next_split
        if i >= len(self.order):
            return
        self.next_split += 1
        r, s = i % self.NR, i % self.NS
        done = self.pe_tok[i - self.NS] if i >= self.NS else None
        raw, hi, lo = self.raw[:, r, :], self.hi[:, s, :], self.lo[:, s, :]
        self.hi_tok[i] = self.act(lambda e: e.activation(hi, raw, ACT.Copy), self.raw_tok[i], done)
        self.lo_tok[i] = self.pool(
            lambda e: e.tensor_tensor(lo, raw, hi.bitcast(F32), ALU.subtract), self.hi_tok[i], done)
        self._dma()

    def weights(self, what):
        i = len(self.used)
        self.used.append(what)
        if self.dry:
            self.order.append(what)
            self.hi_tok[i] = self.lo_tok[i] = None
            return i
        assert self.order[i] == what
        while self.next_split < min(i + self.NS, len(self.order)):
            self._split()
        return i

    def tiles(self, i):
        s = i % self.NS
        return self.hi[:, s, :], self.lo[:, s, :]

    def unit_done(self, i, tok):
        self.pe_tok[i] = tok

    def mm3(self, out, wh, wl, xh, xl, start, stop, *tokens, last=False):
        self.pe.wait(*tokens)
        self.pe(lambda e: e.matmul(out, wh, xh, start=start, stop=False), quiet=True)
        self.pe(lambda e: e.matmul(out, wl, xh, start=False, stop=False), quiet=True)
        return self.pe(lambda e: e.matmul(out, wh, xl, start=False, stop=stop), quiet=not last)

    def linear(self, what, x, chunks, bank, wait_x=True):
        i = self.weights(what)
        wh, wl = self.tiles(i)
        tok = None
        self.pe.wait(bank.free, self.hi_tok[i], self.lo_tok[i])
        for n, c in enumerate(chunks):
            ws = slice(n * 128, n * 128 + 128)
            tok = self.mm3(bank.ap[:, :], wh[:, ws], wl[:, ws], x.hi[:, c, :], x.lo[:, c, :],
                           n == 0, n == len(chunks) - 1, x.ready[c], last=n == len(chunks) - 1)
        self.unit_done(i, tok)
        return tok

    def emit(self, block):
        def run(q, sems):
            def go(eng):
                for it in q.items:
                    if it[0] == "wait":
                        eng.wait_ge(sems[it[1]], it[2])
                    else:
                        ins = it[1](eng)
                        if it[2] is not None:
                            ins.then_inc(sems[it[2]], it[3])
            return go
        block.tensor(run(self.pe, self.sems))
        block.scalar(run(self.act, self.sems))
        block.vector(run(self.dve, self.sems))
        block.gpsimd(run(self.pool, self.sems))
        block.sync(run(self.sp, self.sems))


def program(nc, ctx, k, D, stop=None):
    pe, act, dve, pool = k.pe, k.act, k.dve, k.pool

    def sb(name, shape, dt=F32, c=ctx):
        return c.enter_context(nc.sbuf_tensor(name, shape, dt))

    H = sb("H", [128, 8, T])
    RAW = sb("RAW", [128, k.NR, 1024])
    WH = sb("WH", [128, k.NS, 1024], F32R)
    WL = sb("WL", [128, k.NS, 1024], F32R)
    VE = sb("VE", [128, NV])
    CO = sb("CO", [128, NCC])
    ONES = sb("ONES", [128, 128])
    NT = 9
    TMP = sb("TMP", [128, NT, 576])
    RS = sb("RS", [128, 2, T])
    SM = sb("SM", [128, 64])
    P0h = sb("P0h", [128, 8, T], F32R)
    P0l = sb("P0l", [128, 8, T], F32R)
    P0 = Split(P0h, P0l)
    banks = [ctx.enter_context(nc.psum_tensor(f"B{i}", [128, 512], F32)) for i in range(8)]
    BK = Ring(banks)
    TR = Ring([TMP[:, i, :] for i in range(NT)])
    ident = CO[:, 0:128]

    def vec(name, c):
        return VE[:, VCOL[name] + c:VCOL[name] + c + 1]

    k.stage("init")
    t_ve = k.load(VE[:, :], D["vecs"], sem="d_ve")
    t_h = [k.load(H[:, c, :], D["xT"][c], sem=f"d_h{c}") for c in range(8)]
    k.weights_init(RAW, WH, WL, D["w"])
    t_co = k.load(CO[:, :], D["consts"], sem="d_co")
    t_ones = dve(lambda e: e.memset(ONES[:, :], 1.0))
    t_mh = dve(lambda e: e.memset(SM[:, 0:4], -0.5))
    H_tok = list(t_h)
    H_rd = [[] for _ in range(8)]
    pe.wait(t_ones, t_co)
    act.wait(t_ve)
    dve.wait(t_ve, t_co)
    sm_free = [None]
    ACC = sb("ACC", [128, T])
    acc_free = [None]

    acc_n = [0]

    def sumsq(src, tok):
        acc_n[0] += 1
        if acc_n[0] == 1:
            t = act(lambda e: e.activation(ACC[:, :], src, ACT.Square), tok, acc_free[0])
            sumsq.tok = t
            return t
        s = TR.take()
        a = act(lambda e: e.activation(s.ap[:, 0:T], src, ACT.Square), tok, s.free)
        t = pool(lambda e: e.tensor_tensor(ACC[:, :], ACC[:, :], s.ap[:, 0:T], ALU.add), a, sumsq.tok)
        TR.give(s, t)
        sumsq.tok = t
        return a

    rs_i = [0]
    rs_free = [[], []]

    def stat_a(eps):
        assert acc_n[0] == 8
        acc_n[0] = 0
        b = BK.take()
        pe.wait(sumsq.tok, b.free)
        for j in range(4):
            t = pe(lambda e, j=j: e.matmul(b.ap[:, j:j + 1], ACC[:, j * 128:j * 128 + 128], ONES[:, 0:1],
                                           start=True, stop=True), quiet=j < 3)
        acc_free[0] = t
        d = dve(lambda e: e.tensor_scalar(SM[:, 4:8], b.ap[:, 0:4], 1.0 / 1024, eps, ALU.mult, ALU.add), t, sm_free[0])
        BK.give(b, d)
        return pool(lambda e: e.tensor_tensor(SM[:, 8:12], SM[:, 4:8], SM[:, 0:4], ALU.pow), d, t_mh, sm_free[0])

    def stat_b(tok):
        b = BK.take()
        pe.wait(tok, b.free)
        for j in range(4):
            t = pe(lambda e, j=j: e.matmul(b.ap[:, j * 128:j * 128 + 128], SM[:, 8 + j:9 + j].to_broadcast([128, 128]),
                                           ident, start=True, stop=True), quiet=j < 3)
        sm_free[0] = t
        i = rs_i[0] % 2
        rs_i[0] += 1
        a = act(lambda e: e.activation(RS[:, i, :], b.ap[:, :], ACT.Copy), t, rs_free[i])
        BK.give(b, a)
        rs_free[i] = []
        return RS[:, i, :], a, i

    def split_scaled(dst, c, src, g, tok):
        a = act(lambda e: e.activation(dst.hi[:, c, :], src, ACT.Copy, scale=g), tok, dst.free)
        d = dve(lambda e: e.scalar_tensor_tensor(dst.lo[:, c, :], src, g, dst.hi[:, c, :].bitcast(F32),
                                                 ALU.mult, ALU.subtract), a, tok, dst.free)
        dst.ready[c] = [a, d]
        return [a, d]

    def split(dst, c, src, tok):
        a = act(lambda e: e.activation(dst.hi[:, c, :], src, ACT.Copy), tok, dst.free)
        d = dve(lambda e: e.tensor_tensor(dst.lo[:, c, :], src, dst.hi[:, c, :].bitcast(F32), ALU.subtract),
                a, tok, dst.free)
        dst.ready[c] = [a, d]
        return [a, d]

    def norm_in(c, outs):
        r = [sumsq(H[:, c, :], H_tok[c])]
        for dst, name, off in outs:
            r += split_scaled(dst, c, H[:, c, :], vec(name, off + c), H_tok[c])
        H_rd[c] = r

    def add_to_h(c, src, toks):
        H_tok[c] = dve(lambda e: e.tensor_tensor(H[:, c, :], H[:, c, :], src, ALU.add), toks, H_tok[c], H_rd[c])
        return H_tok[c]

    def bg(n):
        for _ in range(n):
            if k.bg:
                k.bg.pop(0)()

    class Lag:

        def __init__(self, eps=1e-6):
            self.pend, self.n, self.eps, self.rs = [], 0, eps, None

        def put(self, evac):
            self.pend.append(evac)
            self.n += 1
            if self.n == 1:
                self.a = stat_a(self.eps)
            elif self.n == 2:
                self.rs, self.rt, self.ri = stat_b(self.a)
            if self.rs is not None:
                for f in self.pend:
                    f(self.rs, self.rt)
                self.pend = []

        def end(self, tok):
            rs_free[self.ri] = tok

    def scale_psum(dst, b, rs, rt, t, *w):
        return dve(lambda e: e.tensor_tensor(dst, b.ap[:, :], rs, ALU.mult), t, rt, *w)

    def done(name):
        if stop != name:
            return False
        for c in range(8):
            k.load(D["out"][c], H[:, c, :], H_tok[c], sem="d_out")
        k.sp.wait(("d_out", k.dma_n["d_out"]))
        return True

    k.stage("even")
    scope = ExitStack()
    E1 = Split(sb("P1h", [128, 8, T], F32R, scope), sb("P1l", [128, 8, T], F32R, scope))
    E2 = Split(sb("P2h", [128, 8, T], F32R, scope), sb("P2l", [128, 8, T], F32R, scope))
    UP = sb("UP", [128, 4, 30 + T], F32, scope)
    CV = sb("CV", [128, 8, T], F32, scope)
    PBS = sb("PBS", [128, 8], F32, scope)
    LS = sb("LS", [128, T], F32, scope)
    t_pad = pool(lambda e: e.memset(UP[:, :, 0:30], 0.0))
    t_pbs = dve(lambda e: e.tensor_tensor(PBS[:, :], VE[:, VCOL["pool_b"]:VCOL["pool_b"] + 8],
                                          VE[:, VCOL["pool_scale"]:VCOL["pool_scale"] + 8], ALU.mult))
    for c in range(8):
        norm_in(c, [(P0, "norm_even", 0)])
    UR = Ring([UP[:, i, :] for i in range(4)])
    rate = [1]
    W = Weave(lambda: bg(rate[0]))

    def bank():
        while not BK.slots:
            W.step()
        return BK.take()

    def temps(n):
        while len(TR.slots) < n:
            yield

    cv_tok = [None] * 8
    ls = {"t": None, "n": 0}
    us = {}

    def tap_dve(c, u, t_u, j):
        w = VE[:, VCOL["conv_a_w"] + c * 31 + j:VCOL["conv_a_w"] + c * 31 + j + 1]
        x = u.ap[:, j:j + T]
        cv_tok[c] = dve(lambda e: e.scalar_tensor_tensor(CV[:, c, :], x, w, CV[:, c, :], ALU.mult, ALU.add),
                        cv_tok[c], t_u)

    def tap_side(c, u, t_u, j, side):
        w = VE[:, VCOL["conv_a_w"] + c * 31 + j:VCOL["conv_a_w"] + c * 31 + j + 1]
        x = u.ap[:, j:j + T]
        if not side:
            s = side["sum"] = TR.take()
            side["t"] = act(lambda e: e.activation(s.ap[:, 0:T], x, ACT.Copy, scale=w), t_u, s.free)
            return
        s, m = side["sum"], TR.take()
        a = act(lambda e: e.activation(m.ap[:, 0:T], x, ACT.Copy, scale=w), t_u, m.free)
        side["t"] = pool(lambda e: e.tensor_tensor(s.ap[:, 0:T], s.ap[:, 0:T], m.ap[:, 0:T], ALU.add), a, side["t"])
        TR.give(m, side["t"])

    def conv_chain(c, u, t_u):
        side = {}

        def first():
            w = VE[:, VCOL["conv_a_w"] + c * 31:VCOL["conv_a_w"] + c * 31 + 1]
            cv_tok[c] = act(lambda e: e.activation(CV[:, c, :], u.ap[:, 0:T], ACT.Identity, bias=vec("conv_a_b", c),
                                                   scale=w), t_u)
        steps = [first]
        n_side = 4
        main = list(range(1, 31 - n_side))
        for i, j in enumerate(main):
            if i % 4 == 3 and i // 4 < n_side:
                steps.append(lambda j=j, i=i: (tap_side(c, u, t_u, 31 - n_side + i // 4, side), tap_dve(c, u, t_u, j)))
            else:
                steps.append(lambda j=j: tap_dve(c, u, t_u, j))

        def last():
            t = cv_tok[c]
            if side:
                s = side["sum"]
                cv_tok[c] = dve(lambda e: e.tensor_tensor(CV[:, c, :], CV[:, c, :], s.ap[:, 0:T], ALU.add),
                                cv_tok[c], side["t"])
                TR.give(s, cv_tok[c])
            UR.give(u, t, side.get("t"))
            ls["n"] += 1
            if ls["n"] == 2:
                o = [x for x in range(8) if cv_done[x]][0]
                ls["t"] = pool(lambda e: e.tensor_tensor(LS[:, :], CV[:, o, :], CV[:, c, :], ALU.add), cv_tok[o], cv_tok[c])
            elif ls["n"] > 2:
                ls["t"] = pool(lambda e: e.tensor_tensor(LS[:, :], LS[:, :], CV[:, c, :], ALU.add), cv_tok[c], ls["t"])
            cv_done[c] = True
        steps.append(last)
        return steps

    cv_done = [False] * 8

    def pair(c, bg_, t_g, bv, t_v, rs, rt):
        yield from temps(4)
        s, v = TR.take(), TR.take()
        d = scale_psum(s.ap[:, 0:T], bg_, rs, rt, t_g, s.free)
        BK.give(bg_, d)
        a = act(lambda e: e.activation(s.ap[:, 0:T], s.ap[:, 0:T], ACT.Sigmoid), d)
        yield
        d = scale_psum(v.ap[:, 0:T], bv, rs, rt, t_v, v.free)
        BK.give(bv, d)
        yield
        while not UR.slots:
            bg(4)
        u = UR.take()
        m = dve(lambda e: e.tensor_tensor(u.ap[:, 30:], v.ap[:, 0:T], s.ap[:, 0:T], ALU.mult), d, a, u.free, t_pad)
        TR.give(s, m)
        TR.give(v, m)
        us[c] = (u, m)
        if c % 2:
            x, y = (conv_chain(i, *us[i]) for i in (c - 1, c))
            for p, q in zip(x, y):
                k.bg += [p, q]

    def windows(c, v, tv):
        g = c // 2
        w = 2 << g
        cur, tok = v, tv
        for s in range(g + 1):
            sh = 1 << s
            yield from temps(1)
            nx = TR.take()
            a = pool(lambda e, cur=cur, nx=nx, sh=sh: e.tensor_tensor(
                nx.ap[:, sh:T], cur.ap[:, sh:T], cur.ap[:, 0:T - sh], ALU.add), tok, nx.free)
            b = pool(lambda e, cur=cur, nx=nx, sh=sh: e.tensor_copy(nx.ap[:, 0:sh], cur.ap[:, 0:sh]), tok, nx.free)
            if cur is not v:
                TR.give(cur, a, b)
            cur, tok = nx, [a, b]
        a = pool(lambda e, cur=cur: e.tensor_tensor(cur.ap[:, 0:16], cur.ap[:, 0:16],
                                                    CO[:, CC["cnt"] + 16 * g:CC["cnt"] + 16 * g + 16], ALU.mult), tok, t_co)
        yield
        yield
        d = dve(lambda e, cur=cur: e.scalar_tensor_tensor(v.ap[:, 0:T], cur.ap[:, 0:T], 1.0 / w, v.ap[:, 0:T],
                                                          ALU.mult, ALU.subtract), a, tok, tv)
        TR.give(cur, d)
        windows.d = d

    def bval(c, b, t):
        yield from temps(4)
        v = TR.take()
        d = scale_psum(v.ap[:, 0:T], b, lag.rs, lag.rt, t, v.free)
        BK.give(b, d)
        yield from windows(c, v, d)
        d = windows.d
        yield
        a = act(lambda e: e.activation(E2.hi[:, c, :], v.ap[:, 0:T], ACT.Copy), d, E2.free)
        yield
        x = dve(lambda e: e.tensor_tensor(E2.lo[:, c, :], v.ap[:, 0:T], E2.hi[:, c, :].bitcast(F32), ALU.subtract), a)
        E2.ready[c] = [a, x]
        TR.give(v, x)

    def silu_gate(b, t, s_ap, ts, dst, c, give=None):
        yield from temps(3)
        g, sg = TR.take(), TR.take()
        d = scale_psum(g.ap[:, 0:T], b, lag.rs, lag.rt, t, g.free)
        BK.give(b, d)
        a = act(lambda e: e.activation(sg.ap[:, 0:T], g.ap[:, 0:T], ACT.Sigmoid), d, sg.free)
        m = pool(lambda e: e.tensor_tensor(s_ap, g.ap[:, 0:T], s_ap, ALU.mult), d, ts)
        TR.give(g, a, m)
        yield
        yield
        m2 = dve(lambda e: e.tensor_tensor(sg.ap[:, 0:T], s_ap, sg.ap[:, 0:T], ALU.mult), a, m)
        if give:
            give(m2)
        yield
        a = act(lambda e: e.activation(dst.hi[:, c, :], sg.ap[:, 0:T], ACT.Copy), m2, dst.free)
        yield
        x = dve(lambda e: e.tensor_tensor(dst.lo[:, c, :], sg.ap[:, 0:T], dst.hi[:, c, :].bitcast(F32), ALU.subtract),
                a, dst.free)
        dst.ready[c] = [a, x]
        TR.give(sg, x)

    def agate(c, b, t):
        yield from temps(2)
        g = TR.take()
        d = scale_psum(AG[:, c, :], b, lag.rs, lag.rt, t)
        BK.give(b, d)
        a = act(lambda e: e.activation(g.ap[:, 0:T], AG[:, c, :], ACT.Sigmoid), d, g.free)
        yield
        yield
        ag_tok[c] = pool(lambda e: e.tensor_tensor(AG[:, c, :], AG[:, c, :], g.ap[:, 0:T], ALU.mult), a, d)
        TR.give(g, ag_tok[c])

    AG = sb("AG", [128, 8, T], F32, scope)
    ag_tok = {}
    yb = {}
    lag = Lag()

    def after(n=1):
        W.step(n)

    def unit_pair(c):
        b1 = bank()
        t1 = k.linear(("in_even", 0, 8 + c), P0, range(8), b1)
        if c == 0:
            sa = stat_a(1e-6)
        after()
        b2 = bank()
        t2 = k.linear(("in_even", 0, c), P0, range(8), b2)
        if c == 0:
            lag.rs, lag.rt, lag.ri = stat_b(sa)
        W.add(pair(c, b1, t1, b2, t2, lag.rs, lag.rt))
        after()

    def unit_bval(c):
        b = bank()
        t = k.linear(("in_even", 0, 24 + c), P0, range(8), b)
        W.add(bval(c, b, t))
        after()

    def unit_pool(h):
        while not all(4 * h + i in E2.ready for i in range(4)):
            W.step()
        while len(TR.slots) < 5:
            W.step()
        i = k.weights(("pool", 0, h))
        wh, wl = k.tiles(i)
        pe.wait(k.hi_tok[i], k.lo_tok[i])
        for g in range(2):
            for n in range(2):
                b = bank()
                pe.wait(b.free)
                for kc in range(2):
                    o = ((g * 2 + kc) * 2 + n) * 128
                    c = (h * 2 + g) * 2 + kc
                    t = k.mm3(b.ap[:, :], wh[:, o:o + 128], wl[:, o:o + 128], E2.hi[:, c, :], E2.lo[:, c, :],
                              kc == 0, kc == 1, E2.ready[c], last=kc == 1)
                c = (h * 2 + g) * 2 + n
                s = TR.take()
                a = act(lambda e, b=b, c=c, s=s: e.activation(
                    s.ap[:, 0:T], b.ap[:, :], ACT.Identity, bias=PBS[:, c:c + 1], scale=vec("pool_scale", c)),
                    t, t_pbs, s.free)
                BK.give(b, a)
                yb[c] = (s, a)
        k.unit_done(i, t)
        E2.last = t
        after()

    def unit_bgate(c):
        b = bank()
        t = k.linear(("in_even", 0, 32 + c), P0, range(8), b)
        s, a = yb[c]
        W.add(silu_gate(b, t, s.ap[:, 0:T], a, E1, c, lambda m: TR.give(s, m)))
        after()

    def unit_agate(c):
        b = bank()
        t = k.linear(("in_even", 0, 16 + c), P0, range(8), b)
        W.add(agate(c, b, t))
        after()
        P0.last = t

    def out_unit(what, base, n, src, outs, x0=0):
        b = bank()
        while not all(c in src.ready for c in range(x0, x0 + 8)):
            W.step()
        t = k.linear((what, base, n), src, range(x0, x0 + 8), b)
        BK.give(b, add_to_h(n, b.ap[:, :], t))
        if outs is not None:
            norm_in(n, outs)
        src.last = t
        after()

    fill = ([lambda c=c: unit_bval(c) for c in range(4)] + [lambda c=c: unit_agate(c) for c in range(2)]
            + [lambda: unit_pool(0)] + [lambda c=c: unit_bgate(c) for c in range(4)]
            + [lambda c=c: unit_bval(c) for c in range(4, 8)] + [lambda c=c: unit_agate(c) for c in range(2, 4)]
            + [lambda: unit_pool(1)] + [lambda c=c: unit_bgate(c) for c in range(4, 8)]
            + [lambda c=c: unit_agate(c) for c in range(4, 8)]
            + [lambda n=n: out_unit("out_even", 1, n, E1, None) for n in range(8)])
    unit_pair(0)
    unit_pair(1)
    rate[0] = 6
    at = 0
    for c in range(2, 8):
        while at < 4.5 * (c - 1):
            fill[at]()
            at += 1
        unit_pair(c)
    for f in fill[at:]:
        f()
    W.drain()
    bg(len(k.bg))
    b = BK.take()
    t = pe(lambda e, b=b: e.matmul(b.ap[:, :], ONES[:, :], LS[:, :], start=True, stop=True), ls["t"], b.free)
    mu = TR.take()
    a = act(lambda e, b=b: e.activation(mu.ap[:, 0:T], b.ap[:, :], ACT.Copy, scale=1.0 / 1024), t, mu.free)
    BK.give(b, a)
    cs = []
    for c in range(8):
        d = dve(lambda e, c=c: e.tensor_tensor(CV[:, c, :], CV[:, c, :], mu.ap[:, 0:T], ALU.subtract), a, ls["t"], cv_tok[c])
        cs.append(d)
        sumsq(CV[:, c, :], d)
    TR.give(mu, cs[-1])
    ln_rs, ln_t, ln_i = stat_b(stat_a(1e-5))

    def ln_chain(c):
        yield from temps(1)
        s = TR.take()
        d = dve(lambda e: e.tensor_tensor(CV[:, c, :], CV[:, c, :], ln_rs, ALU.mult), ln_t, cs[c], sumsq.tok)
        a = act(lambda e: e.activation(s.ap[:, 0:T], CV[:, c, :], ACT.Sigmoid, bias=vec("ln_a_b", c),
                                       scale=vec("ln_a_g", c)), d, s.free)
        yield
        a2 = pool(lambda e: e.tensor_scalar(CV[:, c, :], CV[:, c, :], vec("ln_a_g", c), vec("ln_a_b", c),
                                            ALU.mult, ALU.add), a, d)
        yield
        d = dve(lambda e: e.tensor_tensor(s.ap[:, 0:T], CV[:, c, :], s.ap[:, 0:T], ALU.mult), a2, a)
        yield
        d = dve(lambda e: e.tensor_tensor(s.ap[:, 0:T], AG[:, c, :], s.ap[:, 0:T], ALU.mult), d, ag_tok[c])
        yield
        a = act(lambda e: e.activation(E2.hi[:, c, :], s.ap[:, 0:T], ACT.Copy), d, E2.last)
        yield
        x = dve(lambda e: e.tensor_tensor(E2.lo[:, c, :], s.ap[:, 0:T], E2.hi[:, c, :].bitcast(F32), ALU.subtract),
                a, E2.last)
        E2.ready[c] = [a, x]
        TR.give(s, x)
    E2.ready = {}
    for c in range(8):
        W.add(ln_chain(c))
        W.step()
    W.drain()
    rs_free[ln_i] = [dve.last]
    P0.free = [P0.last]
    lag.end([dve.last])
    for n in range(8):
        out_unit("out_even", 0, n, E2, [(P0, "norm_odd", 0)])
    fence = k.fence()
    scope.close()
    if done("even"):
        return

    k.stage("odd")
    psc = ExitStack()
    SPT = sb("SPT", [128, NSC], F32, psc)
    PW = sb("PW", [128, 2, 5, 32], F32, psc)
    BB = sb("BB", [128, 2, 32, 16], F32, psc)
    A4 = sb("A4", [128, 2, 2, 32], F32, psc)
    SW = sb("SW", [128, 12, 32], F32, psc)
    SP4 = sb("SP4", [128, 2, 12], F32, psc)
    scope = ExitStack()
    Yh = sb("Yh", [128, 12, T], F32R, scope)
    Yl = sb("Yl", [128, 12, T], F32R, scope)
    Y = Split(Yh, Yl)
    Y.free = fence
    XP = sb("XP", [128, 2, 3 + T], F32, scope)
    GT = sb("GT", [128, 15, T], F32, scope)
    GR = Ring([GT[:, i, :] for i in range(15)])
    XR = Ring([XP[:, i, :] for i in range(2)])
    for s in GR.slots + XR.slots:
        s.free = fence
    D4 = SPT[:, SC["d4"]:SC["d4"] + 32]
    t_xp = pool(lambda e: e.memset(XP[:, :, 0:3], 0.0), fence)
    t_sp = k.load(SPT[:, :], D["ssm"], fence, sem="d_sp")
    lam = VE[:, VCOL["lru_lambda"]:VCOL["lru_lambda"] + 12]
    a = act(lambda e: e.activation(SP4[:, 0, :], lam, ACT.Abs), fence)
    a = act(lambda e: e.activation(SP4[:, 0, :], SP4[:, 0, :], ACT.Exp, scale=-1.0), a)
    a = act(lambda e: e.activation(SP4[:, 0, :], SP4[:, 0, :], ACT.Ln, bias=1.0), a)
    d = dve(lambda e: e.tensor_scalar(SP4[:, 1, :], lam, -1.0, 0.0, ALU.mult, ALU.max), fence)
    d = dve(lambda e: e.tensor_tensor(SP4[:, 0, :], SP4[:, 0, :], SP4[:, 1, :], ALU.add), a, d)
    d = dve(lambda e: e.tensor_scalar(SP4[:, 0, :], SP4[:, 0, :], 4.0, None, ALU.mult), d)
    t_sp4 = dve(lambda e: e.tensor_scalar(SP4[:, 1, :], SP4[:, 0, :], -2.0, None, ALU.mult), d)

    ch = {"t": [t_sp] + fence, "m": None}

    def small(eng, fn):
        def go():
            ch["t"] = eng(fn, ch["t"])
        k.bg.append(go)

    def sw(i):
        return SW[:, i, :]

    def spc(n):
        return SPT[:, SC[n]:SC[n] + 32]

    small(act, lambda e: e.activation(sw(0), spc("ldt"), ACT.Exp))
    small(dve, lambda e: e.tensor_tensor(sw(1), spc("lre"), sw(0), ALU.mult))
    small(act, lambda e: e.activation(sw(1), sw(1), ACT.Exp))
    small(dve, lambda e: e.tensor_tensor(sw(2), spc("lim"), sw(0), ALU.mult))
    for which, quarter in ((3, 0.0), (4, 0.25)):
        small(dve, lambda e, q=quarter: e.tensor_scalar(sw(5), sw(2), 1.0 / (2 * PI), q, ALU.mult, ALU.add))
        small(dve, lambda e: e.tensor_scalar(sw(5), sw(5), ROUND, None, ALU.add))
        small(dve, lambda e: e.tensor_scalar(sw(5), sw(5), ROUND, None, ALU.subtract))
        small(dve, lambda e: e.scalar_tensor_tensor(sw(6), sw(5), -TWO_PI_HI, sw(2), ALU.mult, ALU.add))
        small(dve, lambda e: e.scalar_tensor_tensor(sw(6), sw(5), -TWO_PI_MID, sw(6), ALU.mult, ALU.add))
        small(dve, lambda e: e.scalar_tensor_tensor(sw(6), sw(5), -TWO_PI_LO, sw(6), ALU.mult, ALU.add))
        small(dve, lambda e, q=quarter: e.tensor_scalar(sw(6), sw(6), 2 * PI * q, PI, ALU.add, ALU.min))
        small(dve, lambda e: e.tensor_scalar(sw(6), sw(6), -PI, None, ALU.max))
        small(act, lambda e, w=which: e.activation(sw(w), sw(6), ACT.Sin))
    small(dve, lambda e: e.memset(PW[:, 0, 0, :], 1.0))
    small(dve, lambda e: e.memset(PW[:, 1, 0, :], 0.0))
    small(dve, lambda e: e.tensor_tensor(PW[:, 0, 1, :], sw(1), sw(4), ALU.mult))
    small(dve, lambda e: e.tensor_tensor(PW[:, 1, 1, :], sw(1), sw(3), ALU.mult))

    def small_cmul(o, x, y, t):
        for i, (p, q) in enumerate(((0, 0), (1, 1), (0, 1), (1, 0))):
            small(dve, lambda e, i=i, p=p, q=q: e.tensor_tensor(t[i], x[p], y[q], ALU.mult))
        small(dve, lambda e: e.tensor_tensor(o[0], t[0], t[1], ALU.subtract))
        small(dve, lambda e: e.tensor_tensor(o[1], t[2], t[3], ALU.add))

    for n in (1, 2):
        small_cmul([PW[:, r, n + 1:2 * n + 1, :] for r in range(2)], [PW[:, r, 1:1 + n, :] for r in range(2)],
                   [PW[:, r, n:n + 1, :].to_broadcast([128, n, 32]) for r in range(2)],
                   [SW[:, 4 + 2 * i:4 + 2 * i + n, :] for i in range(4)])
    lre, lim = spc("lre"), spc("lim")
    small(dve, lambda e: e.tensor_tensor(sw(0), lre, lre, ALU.mult))
    small(dve, lambda e: e.tensor_tensor(sw(1), lim, lim, ALU.mult))
    small(dve, lambda e: e.tensor_tensor(sw(0), sw(0), sw(1), ALU.add))
    small(dve, lambda e: e.reciprocal(sw(0), sw(0)))
    small(dve, lambda e: e.tensor_scalar(sw(1), PW[:, 0, 1, :], 1.0, None, ALU.subtract))
    small(dve, lambda e: e.tensor_tensor(sw(2), sw(1), lre, ALU.mult))
    small(dve, lambda e: e.tensor_tensor(sw(3), PW[:, 1, 1, :], lim, ALU.mult))
    small(dve, lambda e: e.tensor_tensor(sw(4), PW[:, 1, 1, :], lre, ALU.mult))
    small(dve, lambda e: e.tensor_tensor(sw(5), sw(1), lim, ALU.mult))
    small(dve, lambda e: e.tensor_tensor(sw(2), sw(2), sw(3), ALU.add))
    small(dve, lambda e: e.tensor_tensor(sw(4), sw(4), sw(5), ALU.subtract))
    small(dve, lambda e: e.tensor_tensor(sw(2), sw(2), sw(0), ALU.mult))
    small(dve, lambda e: e.tensor_tensor(sw(4), sw(4), sw(0), ALU.mult))

    def v3(ap):
        return ap.rearrange("p (g h) -> p g h", h=16)

    def coef(i):
        return SW[:, i, :].unsqueeze(2).to_broadcast([128, 32, 16])

    br_, bi_ = (v3(SPT[:, SC[n]:SC[n] + 512]) for n in ("br", "bi"))

    def bbar():
        s = [TR.take() for _ in range(2)]
        w = ch["t"]
        for r, (x, y, op) in enumerate(((br_, bi_, ALU.subtract), (bi_, br_, ALU.add))):
            u0 = v3(s[0].ap[:, 0:512])
            u1 = v3(s[1].ap[:, 0:512])
            a = dve(lambda e, u0=u0, x=x: e.tensor_tensor(u0, coef(2), x, ALU.mult), w, s[0].free)
            b = dve(lambda e, u1=u1, y=y: e.tensor_tensor(u1, coef(4), y, ALU.mult), w, s[1].free)
            w = dve(lambda e, u0=u0, u1=u1, r=r, op=op: e.tensor_tensor(BB[:, r, :, :], u0, u1, op), a, b)
        TR.give(s[0], w)
        TR.give(s[1], w)
        ch["t"] = w
    k.bg.append(bbar)
    for i, (r, sg) in enumerate(((0, 1.0), (0, 1.0), (1, -1.0), (1, 1.0))):
        small(dve, lambda e, i=i, r=r, sg=sg: e.tensor_scalar(A4[:, i // 2, i % 2, :], PW[:, r, 4, :], sg, None, ALU.mult))

    lag = Lag()
    xcs, heads, rg_done = {}, {}, {}
    rate[0] = 1

    def xr_chain(h, b, t):
        while not (XR.slots and GR.slots):
            yield
        x, s = XR.take(), GR.take()
        d = scale_psum(x.ap[:, 3:], b, lag.rs, lag.rt, t, x.free, t_xp)
        BK.give(b, d)
        w = [VE[:, VCOL["conv_c_w"] + 4 * h + j:VCOL["conv_c_w"] + 4 * h + j + 1] for j in range(4)]
        a = act(lambda e: e.activation(s.ap, x.ap[:, 0:T], ACT.Identity, bias=vec("conv_c_b", h), scale=w[0]), d, s.free)
        yield
        for j in range(1, 4):
            a = dve(lambda e, j=j: e.scalar_tensor_tensor(s.ap, x.ap[:, j:j + T], w[j], s.ap, ALU.mult, ALU.add), a)
            yield
        XR.give(x, a)
        hi = act(lambda e: e.activation(Y.hi[:, h, :], s.ap, ACT.Copy), a, Y.free)
        yield
        lo = dve(lambda e: e.tensor_tensor(Y.lo[:, h, :], s.ap, Y.hi[:, h, :].bitcast(F32), ALU.subtract), hi, Y.free)
        Y.ready[h] = [hi, lo]
        xcs[h] = (s, a, [hi, lo])

    def unit_xr(h):
        b = bank()
        t = k.linear(("in_odd", 0, h), P0, range(8), b)
        if h == 0:
            lag.a = stat_a(1e-6)
            first.append((h, b, t))
            return
        if h == 1:
            lag.rs, lag.rt, lag.ri = stat_b(lag.a)
            W.add(xr_chain(*first[0]))
        W.add(xr_chain(h, b, t))
        after(2)
    first = []

    def head_chain(h, b0, p0, b1, p1):
        xc, tx, ts = xcs[h]
        t, ix = GR.take(), GR.take()
        a = act(lambda e: e.activation(t.ap, b0.ap[:, :], ACT.Sigmoid, bias=vec("b_rg", h)), p0, t.free)
        BK.give(b0, a)
        a2 = act(lambda e: e.activation(ix.ap, b1.ap[:, :], ACT.Sigmoid, bias=vec("b_ig", h)), p1, ix.free)
        BK.give(b1, a2)
        m = pool(lambda e: e.tensor_tensor(ix.ap, ix.ap, xc.ap, ALU.mult), a2, tx)
        yield
        e_ = xc
        q = act(lambda e: e.activation(e_.ap, t.ap, ACT.Exp, scale=SP4[:, 1, h:h + 1]), a, t_sp4, m, ts)
        q2 = act(lambda e: e.activation(t.ap, t.ap, ACT.Tanh, scale=SP4[:, 0, h:h + 1]), q)
        yield
        while not TR.slots:
            yield
        s = TR.take()
        r = act(lambda e: e.activation(s.ap[:, 0:T], t.ap, ACT.Sqrt), q2, s.free)
        yield
        n = dve(lambda e: e.scalar_tensor_tensor(t.ap, e_.ap, 1.0, t.ap, ALU.add, ALU.mult), r, q)
        yield
        r = dve(lambda e: e.scalar_tensor_tensor(s.ap[:, 0:T], e_.ap, 1.0, s.ap[:, 0:T], ALU.add, ALU.mult), r, q)
        GR.give(xc, r, n)
        n = pool(lambda e: e.tensor_scalar(t.ap, t.ap, -1.0, 1.0, ALU.mult, ALU.add), n)
        yield
        r = dve(lambda e: e.tensor_tensor(ix.ap, ix.ap, s.ap[:, 0:T], ALU.mult), r, m)
        TR.give(s, r)
        yield
        sc = dve(lambda e: e.tensor_tensor_scan(ix.ap, t.ap, ix.ap, 0.0, ALU.mult, ALU.add), n, r)
        GR.give(t, sc)
        heads[h] = (ix, sc)

    def unit_rgig(g):
        hs = range(4 * g, 4 * g + 4)
        while not (all(h in xcs for h in hs) and len(GR.slots) >= 8):
            W.step()
        i = k.weights(("rgig", 0, g))
        wh, wl = k.tiles(i)
        pe.wait(k.hi_tok[i], k.lo_tok[i])
        gens = []
        for h in hs:
            o = (h % 4) * 256
            bs = []
            for r in range(2):
                b = bank()
                pe.wait(b.free)
                ws = slice(o + 128 * r, o + 128 * r + 128)
                bs += [b, k.mm3(b.ap[:, :], wh[:, ws], wl[:, ws], Y.hi[:, h, :], Y.lo[:, h, :],
                                True, True, Y.ready[h], last=True)]
            gen = head_chain(h, *bs)
            next(gen)
            gens.append(gen)
        k.unit_done(i, bs[3])
        rg_done[g] = bs[3]
        for _ in range(2):
            for gen in gens:
                next(gen)
        for gen in gens:
            W.add(gen)
        after()

    def unit_gate(h):
        while h not in heads:
            W.step()
        b = bank()
        t = k.linear(("in_odd", 0, 12 + h), P0, range(8), b)
        ix, sc = heads[h]
        W.add(silu_gate(b, t, ix.ap, sc, Late(Y, [rg_done[h // 4]]), h, lambda m: GR.give(ix, m)))
        after(2)
        P0.last = t

    class Late:

        def __init__(self, y, free):
            self.hi, self.lo, self.ready, self.free = y.hi, y.lo, out_ready, free
    out_ready = {}
    for h in range(6):
        unit_xr(h)
    unit_rgig(0)
    for h in (6, 7):
        unit_xr(h)
    for h in range(4):
        unit_gate(h)
    unit_rgig(1)
    for h in range(8, 12):
        unit_xr(h)
    for h in range(4, 6):
        unit_gate(h)
    unit_rgig(2)
    for h in range(6, 12):
        unit_gate(h)
    P0.free = [P0.last]
    W.step(2)
    bg(len(k.bg))
    while not all(h in out_ready for h in range(8)):
        W.step()
    Y.ready = out_ready
    for n in range(8):
        out_unit("out_odd", 0, n, Y, None)
    W.drain()
    lag.end([dve.last])
    for n in range(4):
        i = k.weights(("out_odd4", 0, n))
        wh, wl = k.tiles(i)
        pe.wait(k.hi_tok[i], k.lo_tok[i])
        for m in range(2):
            b = bank()
            pe.wait(b.free)
            for kc in range(4):
                ws = slice((4 * m + kc) * 128, (4 * m + kc) * 128 + 128)
                t = k.mm3(b.ap[:, :], wh[:, ws], wl[:, ws], Y.hi[:, 8 + kc, :], Y.lo[:, 8 + kc, :],
                          kc == 0, kc == 3, Y.ready[8 + kc], last=kc == 3)
            c = 2 * n + m
            BK.give(b, add_to_h(c, b.ap[:, :], t))
            H_rd[c] = [sumsq(H[:, c, :], H_tok[c])]
        k.unit_done(i, t)
    fence = k.fence()
    scope.close()
    if done("odd"):
        psc.close()
        return

    k.stage("ssm")
    scope = ExitStack()
    U4 = sb("U4", [128, 32, 128], F32, scope)
    SS = sb("SS", [128, 129, 2, 32], F32, scope)
    BX = sb("BX", [128, 2, 32, 32], F32, scope)
    sub = ExitStack()
    U = sb("U", [128, 2, T], F32, sub)
    PX = sb("PX", [128, 2, 2, 4, 128], F32, sub)
    MT = sb("MT", [128, 2, 2, 4, 128], F32, sub)
    t_px = pool(lambda e: e.memset(PX[:, :, :, :, :], 0.0), fence)
    t_ss = pool(lambda e: e.memset(SS[:, 0, :, :], 0.0), fence)
    rs, rt, ri = stat_b(stat_a(1e-6))
    for c in range(8):
        H_tok[c] = dve(lambda e, c=c, rs=rs: e.scalar_tensor_tensor(H[:, c, :], H[:, c, :], vec("final_norm", c), rs,
                                                            ALU.mult, ALU.mult), rt, H_tok[c], H_rd[c])
        H_rd[c] = [sumsq(H[:, c, :], H_tok[c])]
    rs_free[ri] = [H_tok[7]]
    if done("fnorm"):
        sub.close()
        scope.close()
        psc.close()
        return

    px_free = [[], []]
    mt_free = [[], []]
    px_tok = {}

    def in_tables(q):
        z = q % 2
        t = [TR.take() for _ in range(4)]
        tv = [s.ap[:, 0:256].rearrange("p (g j h) -> p g j h", g=4, j=4) for s in t]

        def pw(r):
            return PW[:, r, 3::-1, 4 * q:4 * q + 4].rearrange("p m g -> p g m").unsqueeze(3).to_broadcast([128, 4, 4, 16])

        def b_(r):
            return BB[:, r, 4 * q:4 * q + 4, :].unsqueeze(2).to_broadcast([128, 4, 4, 16])
        tk = []
        for i, (x, y) in enumerate(((0, 0), (1, 1), (0, 1), (1, 0))):
            tk.append(pool(lambda e, i=i, x=x, y=y: e.tensor_tensor(tv[i], pw(x), b_(y), ALU.mult), t[i].free, ch["t"]))
        out = []
        for r, op in ((0, ALU.subtract), (1, ALU.add)):
            for par in range(2):
                ps = slice(64 * par, 64 * par + 64)
                o = PX[ps, z, r, :, :].rearrange("p g (j w h) -> p g j w h", j=4, w=2)[:, :, :, par, :]
                out.append(dve(lambda e, r=r, op=op, ps=ps, o=o: e.tensor_tensor(o, tv[2 * r][ps], tv[2 * r + 1][ps], op),
                               tk[2 * r], tk[2 * r + 1], px_free[z], t_px))
        for s in t:
            TR.give(s, out[-1])
        px_tok[q] = out

    def transposes(q):
        z = q % 2
        toks = []
        for r in range(2):
            b = BK.take()
            pe.wait(b.free, px_tok[q])
            for g in range(4):
                last = pe(lambda e, b=b, r=r, g=g: e.transpose(b.ap[:, g * 128:g * 128 + 128], PX[:, z, r, g, :], ident),
                          quiet=g < 3)
            a = act(lambda e, b=b, r=r: e.activation(MT[:, z, r, :, :].rearrange("p a b -> p (a b)"), b.ap[:, :],
                                                     ACT.Copy), last, mt_free[z])
            BK.give(b, a)
            toks.append(a)
        a = [pool(lambda e, r=r: e.tensor_copy(BX[:, r, 4 * q:4 * q + 4, :], PX[:, z, r, :, 96:128]), px_tok[q], fence)
             for r in range(2)]
        px_free[z] = [last, *a]
        return toks, a

    in_tables(0)
    in_tables(1)
    rs, rt, ri = stat_b(stat_a(1e-6))
    u_tok = []
    u4_tok = {}
    for c in range(8):
        u_tok.append(dve(lambda e, c=c, rs=rs: e.scalar_tensor_tensor(
            U[:, c % 2, :], H[:, c, :], vec("norm_mix", c), rs, ALU.mult, ALU.mult),
            rt, H_tok[c], u4_tok.get(c - 2), fence))
        H_rd[c] = H_rd[c] + [u_tok[c]]
        if c % 2 == 1:
            ts = []
            for j in range(4):
                for pr in range(4):
                    src = U[32 * pr:32 * pr + 32, :, j::4]
                    dst = U4[32 * j:32 * j + 32, 4 * (c - 1) + pr:4 * (c + 1):4, :]
                    if (4 * j + pr) % 3 == 2:
                        ts.append(act(lambda e, d=dst, s=src: e.activation(d, s, ACT.Copy), u_tok[c - 1:c + 1], fence))
                    else:
                        ts.append(dve(lambda e, d=dst, s=src: e.tensor_copy(d, s), u_tok[c - 1:c + 1], fence))
            u4_tok[c - 1] = u4_tok[c] = ts
    rs_free[ri] = [u_tok[7]]
    bx_tok = []
    v_tok = []
    for q in range(8):
        z = q % 2
        mt, a = transposes(q)
        bx_tok.append(a)
        for hp in range(2):
            b = BK.take()
            pe.wait(b.free, mt, u4_tok[q])
            for x in range(2):
                g = 2 * hp + x
                for r in range(2):
                    t = pe(lambda e, b=b, r=r, x=x, g=g, z=z, q=q: e.matmul(
                        b.ap[:, 256 * x + 128 * r:256 * x + 128 * r + 128], MT[:, z, r, g, :], U4[:, 4 * q + g, :],
                        start=True, stop=True), quiet=not (x == 1 and r == 1))
            o = SS[:, 1:129, :, 4 * q + 2 * hp:4 * q + 2 * hp + 2].rearrange("p c r x -> p x r c")
            a = act(lambda e, b=b, o=o: e.activation(o, b.ap[:, :].rearrange("p (x r c) -> p x r c", x=2, r=2), ACT.Copy),
                    t, fence)
            BK.give(b, a)
        v_tok.append(a)
        mt_free[z] = [t]
        if q + 2 < 8:
            in_tables(q + 2)
    fence2 = [pe.last, act.last, dve.last, pool.last]
    sub.close()
    sub = ExitStack()
    CA = sb("CA", [128, 2, 2, 4, 5, 32], F32, sub)
    TT = sb("TT", [128, 2, 4, 128], F32, sub)
    t_ca = pool(lambda e: e.memset(CA[:, :, :, :, :, :], 0.0), fence2)
    t_tt = pool(lambda e: e.memset(TT[:, :, :, :], 0.0), fence2)
    cr_, ci_ = (v3(SPT[:, SC[n]:SC[n] + 512]) for n in ("cr", "ci"))
    ca_free = [[], []]
    ca_tok, tt_tok = {}, {}

    def out_tables(q):
        z = q % 2
        t = [TR.take() for _ in range(4)]
        tv = [s.ap[:, 0:320].rearrange("p (g m h) -> p g m h", g=4, m=5) for s in t]

        def pw(r):
            return PW[:, r, :, 4 * q:4 * q + 4].rearrange("p m g -> p g m").unsqueeze(3).to_broadcast([128, 4, 5, 16])

        def c_(x):
            return x[:, 4 * q:4 * q + 4, :].unsqueeze(2).to_broadcast([128, 4, 5, 16])
        tk = []
        for i, (x, y) in enumerate(((cr_, 0), (ci_, 1), (cr_, 1), (ci_, 0))):
            tk.append(pool(lambda e, o=tv[i], x=c_(x), y=pw(y): e.tensor_tensor(o, x, y, ALU.mult), t[i].free, ch["t"]))
        n = dve(lambda e, x=t[2].ap[:, 0:320]: e.tensor_scalar(x, x, -1.0, None, ALU.mult), tk[2])
        out = []
        for r in range(2):
            for par in range(2):
                ps = slice(64 * par, 64 * par + 64)
                out.append(dve(lambda e, ps=ps, o=CA[ps, z, r, :, :, 16 * par:16 * par + 16], x=tv[2 * r], y=tv[2 * r + 1]:
                               e.tensor_tensor(o, x[ps], y[ps], ALU.subtract), tk, n, ca_free[z], t_ca))
        for s in t:
            TR.give(s, out[-1])
        ca_tok[q] = out

    def toeplitz(q):
        z = q % 2
        b = BK.take()
        pe.wait(b.free, ca_tok[q], bx_tok)
        for g in range(4):
            for r in range(2):
                t = pe(lambda e, b=b, g=g, r=r: e.matmul(
                    b.ap[0:32, 128 * g:128 * g + 128], BX[:, r, 4 * q + g, :],
                    CA[:, z, r, g, 0:4, :].rearrange("p m h -> p (m h)"), start=r == 0, stop=r == 1),
                    quiet=not (g == 3 and r == 1))
        bv = b.ap[0:32, :].rearrange("p (g n) -> p g n", g=4)
        ts = [act(lambda e, j=j: e.activation(TT[32 * j:32 * j + 32, z, :, 32 * j:128], bv[:, :, 0:128 - 32 * j],
                                              ACT.Copy), t, ca_free[z], t_tt) for j in range(4)]
        BK.give(b, ts[-1])
        for g in range(4):
            d4 = D4[:, 4 * q + g:4 * q + g + 1]
            ts.append(dve(lambda e, g=g, d4=d4: e.scalar_tensor_tensor(TT[:, z, g, :], ident, d4, TT[:, z, g, :],
                                                                      ALU.mult, ALU.add), ts[:4]))
        tt_tok[q] = ts[4:]

    out_tables(0)
    toeplitz(0)
    out_tables(1)
    toeplitz(1)
    tS = [v_tok[-1], t_ss]
    SC4 = TR.take()
    s1, s2 = SC4.ap[:, 0:64].rearrange("p (r x) -> p r x", r=2), SC4.ap[:, 64:128].rearrange("p (r x) -> p r x", r=2)
    w = SC4.free
    for c in range(2, 128):
        a = dve(lambda e, c=c: e.tensor_tensor(s1, SS[:, c - 1, :, :], A4[:, 0, :, :], ALU.mult), tS, w)
        b = dve(lambda e, c=c: e.tensor_tensor(s2, SS[:, c - 1, ::-1, :], A4[:, 1, :, :], ALU.mult), tS, w)
        a = dve(lambda e, c=c: e.tensor_tensor(s1, s1, SS[:, c, :, :], ALU.add), a)
        tS = dve(lambda e, c=c: e.tensor_tensor(SS[:, c, :, :], s1, s2, ALU.add), a, b)
        w = tS
    TR.give(SC4, tS)
    G = P0

    def gelu(q, y, g1, yt):
        Y_, G_ = y.ap[:, 0:T], g1.ap[:, 0:T]
        a = act(lambda e: e.activation(G_, Y_, ACT.Square), yt, g1.free)
        yield
        a = pool(lambda e: e.tensor_scalar(G_, G_, 0.044715, 1.0, ALU.mult, ALU.add), a)
        yield
        a = dve(lambda e: e.tensor_tensor(G_, G_, Y_, ALU.mult), a)
        yield
        a = act(lambda e: e.activation(G_, G_, ACT.Sigmoid, scale=2 * math.sqrt(2 / PI)), a)
        yield
        a = dve(lambda e: e.tensor_tensor(G_, G_, Y_, ALU.mult), a)
        TR.give(y, a)
        yield
        x = act(lambda e: e.activation(G.hi[:, q, :], G_, ACT.Copy), a, G.free)
        yield
        z = dve(lambda e: e.tensor_tensor(G.lo[:, q, :], G_, G.hi[:, q, :].bitcast(F32), ALU.subtract), x, G.free)
        G.ready[q] = [x, z]
        TR.give(g1, z)

    for q in range(8):
        z = q % 2
        b = BK.take()
        pe.wait(b.free, tS, tt_tok[q], u4_tok[q])
        for g in range(4):
            o = b.ap[:, 128 * g:128 * g + 128]
            pe(lambda e, o=o, z=z, g=g, q=q: e.matmul(o, TT[:, z, g, :], U4[:, 4 * q + g, :], start=True, stop=False),
               quiet=True)
            for r in range(2):
                t = pe(lambda e, o=o, z=z, g=g, q=q, r=r: e.matmul(
                    o, CA[:, z, r, g, 1:5, :].rearrange("p m h -> p (m h)"), SS[:, 0:128, r, 4 * q + g],
                    start=False, stop=r == 1), quiet=not (g == 3 and r == 1))
        ca_free[z] = [t]
        if q + 2 < 8:
            out_tables(q + 2)
            toeplitz(q + 2)
        while len(TR.slots) < 6:
            W.step()
        y, g1 = TR.take(), TR.take()
        yt = []
        for i in range(4):
            for pr in range(4):
                o, x = y.ap[32 * pr:32 * pr + 32, i:T:4], b.ap[32 * i:32 * i + 32, 128 * pr:128 * pr + 128]
                if i < 2:
                    yt.append(act(lambda e, o=o, x=x: e.activation(o, x, ACT.Copy), t, y.free))
                else:
                    yt.append(dve(lambda e, o=o, x=x: e.tensor_copy(o, x), t, y.free))
        BK.give(b, yt)
        W.add(gelu(q, y, g1, yt))
        W.step(2)
    W.drain()
    fence = k.fence()
    sub.close()
    scope.close()
    psc.close()
    if done("ssmx"):
        return
    scope = ExitStack()
    P1 = Split(sb("P1hb", [128, 8, T], F32R, scope), sb("P1lb", [128, 8, T], F32R, scope))
    P2 = Split(sb("P2hb", [128, 8, T], F32R, scope), sb("P2lb", [128, 8, T], F32R, scope))
    P1.free = P2.free = fence
    for n in range(8):
        b = BK.take()
        t = k.linear(("glu", 0, 8 + n), P0, range(8), b)
        s = TR.take()
        a = act(lambda e, b=b, s=s: e.activation(s.ap[:, 0:T], b.ap[:, :], ACT.Sigmoid), t, s.free)
        BK.give(b, a)
        b = BK.take()
        t = k.linear(("glu", 0, n), P0, range(8), b)
        d = dve(lambda e, b=b, s=s: e.tensor_tensor(s.ap[:, 0:T], s.ap[:, 0:T], b.ap[:, :], ALU.mult), t, a)
        BK.give(b, d)
        TR.give(s, add_to_h(n, s.ap[:, 0:T], d))
        norm_in(n, [(P1, "norm_mlp", 0)])
    P0.free = [t]
    if done("mix0"):
        scope.close()
        return

    def mlp(l, src, ha, hb, dst):
        bufs = [ha, hb]
        lag = Lag()

        def up(qt):
            dstq = bufs[qt % 2]
            for c in range(8):
                b = BK.take()
                t = k.linear((f"up{l}", 0, 8 * qt + c), src, range(8), b)

                def evac(rs, rt, b=b, t=t, c=c):
                    s = TR.take()
                    d = dve(lambda e: e.scalar_tensor_tensor(s.ap[:, 0:T], b.ap[:, :], 0.0, rs, ALU.max, ALU.mult),
                            t, rt, s.free)
                    BK.give(b, d)
                    a = act(lambda e: e.activation(dstq.hi[:, c, :], s.ap[:, 0:T], ACT.Square), d, dstq.free)
                    a2 = act(lambda e: e.activation(s.ap[:, 0:T], s.ap[:, 0:T], ACT.Square), a)
                    x = dve(lambda e: e.tensor_tensor(dstq.lo[:, c, :], s.ap[:, 0:T], dstq.hi[:, c, :].bitcast(F32),
                                                      ALU.subtract), a2, dstq.free)
                    TR.give(s, x)
                    dstq.ready[c] = [a, x]
                lag.put(evac)
            return t

        def down(qt):
            x = bufs[qt % 2]
            for n in range(8):
                b = BK.take()
                t = k.linear((f"down{l}", qt, n), x, range(8), b)
                BK.give(b, add_to_h(n, b.ap[:, :], t))
                if qt == 3:
                    norm_in(n, [(dst, "norm_ple", 8 * l)])
            x.free = [t]
        up(0)
        up(1)
        down(0)
        up(2)
        down(1)
        src.free = [up(3)]
        lag.end([dve.last])
        down(2)
        down(3)

    def proj(l, PJ, PT):
        for kc in range(2):
            s = TR.take()
            a = k.load(s.ap[:, 0:T], D["pT"][l][:, kc, :], s.free, sem=f"d_p{l}{kc}")
            TR.give(s, *split(PT, kc, s.ap[:, 0:T], a))
        toks = []
        for h in range(2):
            i = k.weights((f"proj{l}", 0, h))
            wh, wl = k.tiles(i)
            pe.wait(k.hi_tok[i], k.lo_tok[i])
            for n in range(4):
                b = BK.take()
                pe.wait(b.free)
                for kc in range(2):
                    ws = slice((n * 2 + kc) * 128, (n * 2 + kc) * 128 + 128)
                    t = k.mm3(b.ap[:, :], wh[:, ws], wl[:, ws], PT.hi[:, kc, :], PT.lo[:, kc, :],
                              kc == 0, kc == 1, PT.ready[kc], last=kc == 1)
                toks.append(act(lambda e, b=b, c=4 * h + n: e.activation(PJ[:, c, :], b.ap[:, :], ACT.Copy), t, PT.free))
                BK.give(b, toks[-1])
            k.unit_done(i, t)
        return toks

    def ple(l, src, PJ, tp, outs):
        lag = Lag()
        for n in range(8):
            b = BK.take()
            t = k.linear((f"gate{l}", 0, n), src, range(8), b)

            def evac(rs, rt, b=b, t=t, n=n):
                s = TR.take()
                d = scale_psum(s.ap[:, 0:T], b, rs, rt, t, s.free)
                BK.give(b, d)
                a = act(lambda e: e.activation(s.ap[:, 0:T], s.ap[:, 0:T], ACT.Sigmoid), d)
                d = pool(lambda e: e.tensor_tensor(s.ap[:, 0:T], s.ap[:, 0:T], PJ[:, n, :], ALU.mult), a, tp[n])
                TR.give(s, add_to_h(n, s.ap[:, 0:T], d))
                norm_in(n, outs)
            lag.put(evac)
        src.free = [t]
        lag.end([dve.last])

    PJ = sb("PJ", [128, 8, T], F32, scope)
    PT = Split(sb("PTh", [128, 2, T], F32R, scope), sb("PTl", [128, 2, T], F32R, scope))
    PT.free = fence
    tp = proj(0, PJ, PT)
    mlp(0, P1, P0, P2, P1)
    if done("mlp0"):
        scope.close()
        return
    ple(0, P1, PJ, tp, [(P0, "norm_mix", 8), (P2, "kv_norm", 0)])
    if done("ple0"):
        scope.close()
        return
    fence = k.fence()
    scope.close()

    k.stage("att")
    scope = ExitStack()
    P1 = Split(sb("P1hc", [128, 8, T], F32R, scope), sb("P1lc", [128, 8, T], F32R, scope))
    P2b = Split(sb("P2hc", [128, 8, T], F32R, scope), sb("P2lc", [128, 8, T], F32R, scope))
    P1.free = fence
    at = ExitStack()
    KT = sb("KT", [128, 2, T], F32, at)
    V = sb("V", [128, 4, 256], F32, at)
    Q = sb("Q", [128, 8, T], F32, at)
    RO = sb("RO", [128, 2, T], F32, at)
    AS = ACC[:, :].rearrange("p (n k) -> p n k", n=16)
    RK = sb("RK", [128, 4], F32, at)
    t_ro = k.load(RO[:, :, :], D["rope"], fence, sem="d_ro")
    rot = CO[:, CC["rot"]:CC["rot"] + 128]
    lag = Lag()
    pend = []

    def rope_out(dst, s, d):
        b = BK.take()
        t = pe(lambda e: e.matmul(b.ap[:, :], rot, s.ap[:, 0:T], start=True, stop=True), d, b.free)
        m = TR.take()
        x = dve(lambda e: e.tensor_tensor(m.ap[:, 0:T], b.ap[:, :], RO[:, 1, :], ALU.mult), t, m.free, t_ro)
        BK.give(b, x)
        y = pool(lambda e: e.tensor_tensor(s.ap[:, 0:T], s.ap[:, 0:T], RO[:, 0, :], ALU.mult), t, t_ro)
        r = dve(lambda e: e.tensor_tensor(dst, s.ap[:, 0:T], m.ap[:, 0:T], ALU.add), x, y, fence)
        TR.give(s, r)
        TR.give(m, r)
        return r

    rope_tok = {}

    def proj_rope(what, n, src, dst, key):
        b = BK.take()
        t = k.linear((what, 0, n), src, range(8), b)

        def evac(rs, rt):
            s = TR.take()
            d = scale_psum(s.ap[:, 0:T], b, rs, rt, t, s.free)
            BK.give(b, d)
            pend.append((dst, s, d, key))
        lag.put(evac)
        return t

    def ropes(keep):
        while len(pend) > keep:
            dst, s, d, key = pend.pop(0)
            rope_tok[key] = rope_out(dst, s, d)

    for n in range(2):
        proj_rope("wk", n, P2, KT[:, n, :], ("k", n))
    t_rk = dve(lambda e: e.tensor_copy(RK[:, :], SM[:, 8:12]), lag.a, fence)
    vb = [BK.take() for _ in range(4)]
    for hf in range(2):
        i = k.weights(("wv", 0, hf))
        wh, wl = k.tiles(i)
        pe.wait(k.hi_tok[i], k.lo_tok[i], [b.free for b in vb])
        for tb in range(4):
            for kc in range(4):
                c = 4 * hf + kc
                xh = P2.hi[:, c, 128 * tb:128 * tb + 128]
                xl = P2.lo[:, c, 128 * tb:128 * tb + 128]
                ws = slice(256 * kc, 256 * kc + 256)
                o = vb[tb].ap[:, 0:256]
                pe.wait(P2.ready[c])
                pe(lambda e, o=o, xh=xh, w=wh[:, ws], c=c: e.matmul(o, xh, w, start=c == 0, stop=False), quiet=True)
                pe(lambda e, o=o, xh=xh, w=wl[:, ws]: e.matmul(o, xh, w, start=False, stop=False), quiet=True)
                t = pe(lambda e, o=o, xl=xl, w=wh[:, ws], c=c: e.matmul(o, xl, w, start=False, stop=c == 7),
                       quiet=kc != 3)
            if hf == 1:
                a = act(lambda e, o=o, tb=tb: e.activation(V[:, tb, :], o, ACT.Copy, scale=RK[:, tb:tb + 1]), t, t_rk, fence)
                BK.give(vb[tb], a)
                rope_tok["v", tb] = a
        k.unit_done(i, t)
    ropes(0)
    for n in range(8):
        t = proj_rope("wq", n, P0, Q[:, n, :], ("q", n))
        ropes(1)
    ropes(0)
    P0.free = [t]
    lag.end([dve.last])
    mask = CO[:, CC["mask"]:CC["mask"] + 256]
    sink = VE[:, VCOL["sinks"]:VCOL["sinks"] + 16]
    o_parts = {}

    def scores(n):
        blk, kv = n // 4, n % 4
        k0, nk = (128, 128) if blk == 0 else (0, 256)
        p_ = slice(64 * (kv % 2), 64 * (kv % 2) + 64)
        ks = slice(128 * blk - 128 + k0, 128 * blk + 128)
        st = AS[:, n, :]
        out, mx = [], []
        for hp in range(2):
            b = BK.take()
            pe.wait(b.free, rope_tok["k", kv // 2])
            for j in range(2):
                c = 4 * (kv // 2) + 2 * hp + j
                t = pe((lambda b, j, c: lambda e: e.matmul(
                    b.ap[:, 256 * j:256 * j + nk], Q[p_, c, 128 * blk:128 * blk + 128], KT[p_, kv // 2, ks],
                    start=True, stop=True))(b, j, c), rope_tok["q", c], quiet=j == 0)
            s = TR.take()
            bv = b.ap[:, :].rearrange("p (a k) -> p a k", a=2)[:, :, 0:nk]
            sv = s.ap[:, 0:512].rearrange("p (a k) -> p a k", a=2)[:, :, 0:nk]
            mv = mask[:, k0:256].unsqueeze(1).to_broadcast([128, 2, nk])
            d = dve(lambda e, bv=bv, sv=sv: e.scalar_tensor_tensor(sv, bv, 0.125, mv, ALU.mult, ALU.add), t, s.free)
            BK.give(b, d)
            mx.append(dve(lambda e, sv=sv, hp=hp: e.tensor_reduce(st[:, 2 * hp:2 * hp + 2], sv, AX.X, ALU.max), d, acc_free[0]))
            out.append((s, sv))
        sk = sink[:, 4 * kv:4 * kv + 4]
        d = dve(lambda e: e.tensor_tensor(st[:, 0:4], st[:, 0:4], sk, ALU.max), mx)
        d1 = dve(lambda e: e.tensor_scalar(st[:, 4:8], st[:, 0:4], -1.0, None, ALU.mult), d)
        d2 = dve(lambda e: e.tensor_tensor(st[:, 8:12], sk, st[:, 0:4], ALU.subtract), d)
        ex = []
        for h in range(4):
            sv = out[h // 2][1][:, h % 2, :]
            ex.append(act(lambda e, sv=sv, h=h: e.activation(sv, sv, ACT.Exp, bias=st[:, 4 + h:5 + h],
                                                            accum_out=st[:, 12 + h:13 + h]), d1))
        a = act(lambda e: e.activation(st[:, 8:12], st[:, 8:12], ACT.Exp), d2)
        d = dve(lambda e: e.tensor_tensor(st[:, 16:20], st[:, 12:16], st[:, 8:12], ALU.add), a, ex)
        d = dve(lambda e: e.reciprocal(st[:, 16:20], st[:, 16:20]), d)
        w = []
        for h in range(4):
            sv = out[h // 2][1][:, h % 2, :]
            w.append(dve(lambda e, sv=sv, h=h: e.tensor_scalar(sv, sv, st[:, 16 + h:17 + h], None, ALU.mult), d, ex[h]))
        return out, w

    def attend(n, out, w):
        blk, kv = n // 4, n % 4
        halves = [1] if blk == 0 else [0, 1]
        wt = []
        for hf in halves:
            b = BK.take()
            pe.wait(b.free)
            for h in range(4):
                sv = out[h // 2][1][:, h % 2, 128 * (hf if blk else 0):128 * (hf if blk else 0) + 128]
                t = pe((lambda b, h, sv: lambda e: e.transpose(b.ap[:, 128 * h:128 * h + 128], sv, ident))(b, h, sv),
                       w[h], quiet=h < 3)
            s = TR.take()
            a = act((lambda b, s: lambda e: e.activation(s.ap[:, 0:512], b.ap[:, :], ACT.Copy))(b, s), t, s.free)
            BK.give(b, a)
            wt.append((s, a, blk - 1 + hf))
        for s, _ in out:
            TR.give(s, t)
        b = BK.take()
        pe.wait(b.free)
        p_ = slice(64 * (kv % 2), 64 * (kv % 2) + 64)
        for i, (s, a, vb_) in enumerate(wt):
            t = pe((lambda b, s, vb_, i: lambda e: e.matmul(b.ap[p_, :], V[:, vb_, 64 * kv:64 * kv + 64], s.ap[:, 0:512],
                                                          start=i == 0, stop=i == len(wt) - 1))(b, s, vb_, i),
                   a, rope_tok["v", vb_], quiet=i < len(wt) - 1)
        for s, _, _ in wt:
            TR.give(s, t)
        cs = slice(4 * (kv // 2), 4 * (kv // 2) + 4)
        ts = slice(128 * blk, 128 * blk + 128)
        bv = b.ap[p_, :].rearrange("p (c t) -> p c t", c=4)
        hi, lo = P1.hi[p_, cs, ts], P1.lo[p_, cs, ts]
        a = act(lambda e: e.activation(hi, bv, ACT.Copy), t, P1.free)
        d = dve(lambda e: e.tensor_tensor(lo, bv, hi.bitcast(F32), ALU.subtract), a, P1.free)
        BK.give(b, d)
        for c in range(4 * (kv // 2), 4 * (kv // 2) + 4):
            o_parts.setdefault(c, []).extend([a, d])

    prev = None
    for n in range(16):
        cur = (n, *scores(n))
        if prev:
            attend(*prev)
        prev = cur
    attend(*prev)
    for c in range(8):
        P1.ready[c] = o_parts[c]
    acc_free[0] = [dve.last, act.last]
    fence = k.fence()
    at.close()
    PJ = sb("PJb", [128, 8, T], F32, scope)
    PT = Split(sb("PThb", [128, 2, T], F32R, scope), sb("PTlb", [128, 2, T], F32R, scope))
    PT.free = fence
    P2b.free = fence
    for n in range(8):
        b = BK.take()
        t = k.linear(("wo", 0, n), P1, range(8), b)
        BK.give(b, add_to_h(n, b.ap[:, :], t))
        norm_in(n, [(P0, "norm_mlp", 8)])
    P1.free = [t]
    if done("mix1"):
        scope.close()
        return
    tp = proj(1, PJ, PT)
    mlp(1, P0, P1, P2b, P0)
    if done("mlp1"):
        scope.close()
        return
    ple(1, P0, PJ, tp, [])
    rs, rt, ri = stat_b(stat_a(1e-6))
    for c in range(8):
        s = TR.take()
        d = dve(lambda e, c=c, s=s, rs=rs: e.scalar_tensor_tensor(s.ap[:, 0:T], H[:, c, :], vec("norm_final", c), rs,
                                                          ALU.mult, ALU.mult), rt, H_tok[c], s.free)
        o = k.load(D["out"][c], s.ap[:, 0:T], d, sem="d_out")
    k.sp.wait(o)
    scope.close()


def matrices(x):
    heads = [(0, 4), (1, 5), (2, 6), (3, 7), (8, 12), (9, 13), (10, 14), (11, 15)]
    cols = np.concatenate([np.arange(64) + 64 * h for pair in heads for h in pair])
    rg = np.concatenate([x["w_rg"][0], x["w_ig"][0]])
    return {
        "in_even": x["w_in_even"][0], "out_even": x["w_out_even"][0], "pool": x["pool_w"][0],
        "in_odd": x["w_in_odd"][0], "out_odd": x["w_out_odd"][0], "rgig": rg,
        "glu": x["ssm_w_glu_2"][0], "up0": x["w_up_2"][0], "down0": x["w_down_2"][0],
        "up1": x["w_up_2"][1], "down1": x["w_down_2"][1], "gate0": x["w_ple_gate_2"][0],
        "gate1": x["w_ple_gate_2"][1], "proj0": x["w_ple_proj_2"][0], "proj1": x["w_ple_proj_2"][1],
        "wk": x["w_k_2"], "wv": x["w_v_2"], "wq": x["w_q_2"][0][:, cols], "wo": x["w_o_2"][0][cols, :],
    }


def unit_tiles(what):
    name, a, b = what
    if name == "pool":
        return None
    if name == "rgig":
        return None
    if name in ("proj0", "proj1"):
        return [(kc, 4 * b + n) for n in range(4) for kc in range(2)]
    if name == "out_odd4":
        return [(8 + kc, 2 * b + m) for m in range(2) for kc in range(4)]
    if name == "wv":
        return [(4 * b + kc, n) for kc in range(4) for n in range(2)]
    return [(8 * a + kc, b) for kc in range(8)]


def pack(order, mats):
    out = np.empty((len(order), 128, 8, 128), np.float32)
    for i, what in enumerate(order):
        name, a, b = what
        m = mats["out_odd" if name == "out_odd4" else name]
        if name == "pool":
            for g in range(2):
                for kc in range(2):
                    for n in range(2):
                        out[i, :, (g * 2 + kc) * 2 + n, :] = m[2 * b + g, kc * 128:kc * 128 + 128, n * 128:n * 128 + 128]
        elif name == "rgig":
            for h in range(4):
                out[i, :, 2 * h, :] = m[4 * b + h]
                out[i, :, 2 * h + 1, :] = m[12 + 4 * b + h]
        else:
            for j, (r, c) in enumerate(unit_tiles(what)):
                out[i, :, j, :] = m[r * 128:r * 128 + 128, c * 128:c * 128 + 128]
    return out.reshape(len(order), 128, 1024)


def vectors(x):
    cols = []

    def add(v, n):
        cols.append(np.asarray(v).reshape(n, 128).T)

    add(x["norm_even"][0], 8)
    cols.append(x["conv_a_w"][0].reshape(31, 8, 128).transpose(2, 1, 0).reshape(128, 248))
    for n in ("conv_a_b", "ln_a_g", "ln_a_b", "pool_b", "pool_scale", "norm_odd"):
        add(x[n][0], 8)
    cols.append(x["conv_c_w"][0].reshape(4, 12, 128).transpose(2, 1, 0).reshape(128, 48))
    for n in ("conv_c_b", "b_rg", "b_ig", "lru_lambda"):
        add(x[n][0], 12)
    add(x["final_norm"], 8)
    add(x["norm_mix_2"], 16)
    add(x["ssm_d_2"][0], 8)
    add(x["kv_norm_2"], 8)
    add(x["norm_mlp_2"], 16)
    add(x["norm_ple_2"], 16)
    add(x["norm_final_2"], 8)
    cols.append(np.repeat(x["attn_sinks_2"][0][None, :], 128, axis=0))
    return np.ascontiguousarray(np.concatenate(cols, axis=1))


def constants():
    c = np.zeros((128, NCC), np.float32)
    c[:, 0:128] = np.eye(128, dtype=np.float32)
    for base in (0, 64):
        for d in range(8):
            c[base + d + 8, CC["rot"] + base + d] = -1.0
            c[base + d, CC["rot"] + base + d + 8] = 1.0
    i = np.arange(128)[:, None]
    j = np.arange(256)[None, :]
    ok = (j <= i + 128) & (i + 128 - j < 128)
    c[:, CC["mask"]:CC["mask"] + 256] = np.where(ok, 0.0, -1e30)
    for g in range(4):
        w = 2 << g
        c[:, CC["cnt"] + 16 * g:CC["cnt"] + 16 * g + 16] = w / np.minimum(np.arange(1, 17), w)
    return c


def rope_tables():
    inv = np.float32(500000.0) ** (-np.arange(0, 16, 2, dtype=np.float32) / np.float32(16))
    ang = np.arange(T, dtype=np.float32)[None, :] * inv[:, None].astype(np.float32)
    r = np.zeros((128, 2, T), np.float32)
    r[:, 0, :] = 1.0
    for base in (0, 8, 64, 72):
        r[base:base + 8, 0, :] = np.cos(ang)
        r[base:base + 8, 1, :] = np.sin(ang)
    return r


def ssm_parameters(x):
    def gn(a):
        return a.reshape(32, 2, 64).transpose(1, 2, 0).reshape(128, 32)

    ldt = np.repeat(x["ssm_log_dt_2"][0][:, None], 64, axis=1)
    b = [x[n][0].reshape(32, 2, 64, 16).transpose(1, 2, 0, 3).reshape(128, 512) for n in ("ssm_b_re_2", "ssm_b_im_2")]
    c = [x[n][0].reshape(32, 2, 16, 64).transpose(1, 3, 0, 2).reshape(128, 512) for n in ("ssm_c_re_2", "ssm_c_im_2")]
    return np.ascontiguousarray(np.concatenate(
        [gn(x["ssm_lambda_re_2"][0]), gn(x["ssm_lambda_im_2"][0]), gn(ldt)] + b + c
        + [np.tile(x["ssm_d_2"][0].reshape(32, 32).T, (4, 1))], axis=1))


def build(nc, order, arrays, stop=None):
    D = {n: nc.dram_tensor(f"in_{n}", a, F32, kind="ExternalInput").ap() for n, a in arrays.items()}
    D["out"] = nc.dram_tensor("out_0", (8, 128, T), F32, kind="ExternalOutput").ap()
    with ExitStack() as ctx:
        k = Builder(nc, ctx, order)
        program(nc, ctx, k, D, stop)
        if order is not None:
            with nc.Block() as block:
                k.emit(block)
    return k.used


def layout(x, order):
    t = lambda a: np.ascontiguousarray(a)
    return {
        "w": pack(order, matrices(x)),
        "xT": t(x["x"][0].T.reshape(8, 128, T)),
        "pT": t(x["p_2"][:, 0].transpose(0, 2, 1).reshape(2, 2, 128, T).transpose(0, 2, 1, 3)),
        "vecs": vectors(x),
        "consts": constants(),
        "rope": rope_tables(),
        "ssm": ssm_parameters(x),
    }


SHAPES = {"w": (1, 128, 1024), "xT": (8, 128, T), "pT": (2, 128, 2, T), "vecs": (128, NV), "consts": (128, NCC),
          "rope": (128, 2, T), "ssm": (128, NSC)}


def kernel(**inputs):
    import concourse.bacc as bacc
    from concourse.bass_utils import run_bass_kernel_spmd

    order = build(bacc.Bacc("TRN2", target_bir_lowering=False, num_devices=1, dynamic_dma_scratch_size=1024), None, SHAPES)
    x = {n: np.asarray(a) for n, a in inputs.items()}
    arrays = layout(x, order)
    nc = bacc.Bacc("TRN2", target_bir_lowering=False, num_devices=1, dynamic_dma_scratch_size=1024)
    build(nc, order, {n: a.shape for n, a in arrays.items()})
    r = run_bass_kernel_spmd(nc, [{f"in_{n}": a for n, a in arrays.items()}], core_ids=[0])
    out = r.results[0]["out_0"].reshape(1024, T)
    return np.ascontiguousarray(out.T).reshape(1, T, 1024)
```

```python
import math
from contextlib import ExitStack

import numpy as np
import concourse.bass as bass
from concourse import mybir

F32 = mybir.dt.float32
F32R = mybir.dt.float32r
ALU = mybir.AluOpType
ACT = mybir.ActivationFunctionType
AX = mybir.AxisListType

T = 512
PI = math.pi
TWO_PI_HI = 6.28125
TWO_PI_MID = float(np.float32(2 * PI - 6.28125))
TWO_PI_LO = float(np.float32(2 * PI - 6.28125 - TWO_PI_MID))
ROUND = 12582912.0

VECS = [
    ("norm_even", 8), ("conv_a_w", 31 * 8), ("conv_a_b", 8), ("ln_a_g", 8), ("ln_a_b", 8),
    ("pool_b", 8), ("pool_scale", 8), ("norm_odd", 8), ("conv_c_w", 4 * 12), ("conv_c_b", 12),
    ("b_rg", 12), ("b_ig", 12), ("lru_lambda", 12), ("final_norm", 8), ("norm_mix", 16),
    ("ssm_d", 8), ("kv_norm", 8), ("norm_mlp", 16), ("norm_ple", 16), ("norm_final", 8),
    ("sinks", 16),
]
VCOL = {}
_at = 0
for _n, _c in VECS:
    VCOL[_n] = _at
    _at += _c
NV = _at

CC = {"ident": 0, "rot": 128, "mask": 256, "cnt": 512, "sgn": 576}
NCC = 580
SC = {"lre": 0, "lim": 32, "ldt": 64, "br": 96, "bi": 608, "cr": 1120, "ci": 1632, "d4": 2144}
NSC = 2176


class Engine:

    def __init__(self, k, name):
        self.k, self.name, self.items, self.seen, self.sem, self.n = k, name, [], {}, None, 0

    def stage(self, name):
        self.sem, self.n = self.k.semaphore(f"{self.name}_{name}"), 0

    def wait(self, *tokens):
        for t in tokens:
            if isinstance(t, (list, tuple)) and not (len(t) == 2 and isinstance(t[1], int)):
                self.wait(*t)
                continue
            if t is None:
                continue
            sem, value = t
            if self.seen.get(sem, 0) < value:
                self.seen[sem] = value
                self.items.append(("wait", sem, value))

    def __call__(self, fn, *tokens, quiet=False):
        self.wait(*tokens)
        if quiet:
            self.items.append(("op", fn, None, 0))
            return None
        self.n += 1
        self.items.append(("op", fn, self.sem, 1))
        return (self.sem, self.n)

    @property
    def last(self):
        return (self.sem, self.n) if self.n else None


class Slot:

    def __init__(self, ap):
        self.ap, self.free = ap, []


class Ring:

    def __init__(self, aps):
        self.slots = [Slot(a) for a in aps]

    def take(self):
        return self.slots.pop(0)

    def give(self, s, *tokens):
        s.free = list(tokens)
        self.slots.append(s)


class Weave:

    def __init__(self, between=None):
        self.active, self.between = [], between

    def add(self, gen):
        self.active.append(gen)

    def step(self, rounds=1):
        for _ in range(rounds):
            for g in list(self.active):
                try:
                    next(g)
                except StopIteration:
                    self.active.remove(g)
            if self.between:
                self.between()

    def drain(self):
        while self.active:
            self.step()


class Split:

    def __init__(self, hi, lo):
        self.hi, self.lo = hi, lo
        self.free = []
        self.ready = {}


class Builder:
    NR, NS = 3, 3

    def __init__(self, nc, ctx, order):
        self.nc, self.ctx, self.dry = nc, ctx, order is None
        self.order = order or []
        self.used = []
        self.sems = {}
        self.pe, self.act, self.dve, self.pool, self.sp = (Engine(self, n) for n in ("pe", "act", "dve", "pool", "sp"))
        self.engines = (self.pe, self.act, self.dve, self.pool)
        self.bg = []
        self.dma_n = {}

    def semaphore(self, name):
        assert name not in self.sems
        self.sems[name] = self.ctx.enter_context(self.nc.semaphore(name))
        return name

    def stage(self, name):
        for e in self.engines:
            e.stage(name)

    def load(self, dst, src, *tokens, sem):
        self.sp.wait(*tokens)
        if sem not in self.sems:
            self.semaphore(sem)
            self.dma_n[sem] = 0
        self.dma_n[sem] += 16
        self.sp.items.append(("op", lambda e: e.dma_start(dst, src), sem, 16))
        return (sem, self.dma_n[sem])

    def fence(self):
        return [e.last for e in self.engines if e.last]

    def weights_init(self, raw, hi, lo, dram):
        self.raw, self.hi, self.lo, self.dram = raw, hi, lo, dram
        self.hi_tok, self.lo_tok, self.pe_tok, self.raw_tok = {}, {}, {}, {}
        self.next_dma = self.next_split = 0

    def fetch(self):
        i = self.next_dma
        if self.dry or i >= len(self.order):
            return
        self.next_dma += 1
        j = i % self.NR
        w = [self.hi_tok[i - self.NR], self.lo_tok[i - self.NR]] if i >= self.NR else []
        self.raw_tok[i] = self.load(self.raw[:, j, :], self.dram[i, :, :], *w, sem=f"raw{j}")

    def prepare(self):
        i = self.next_split
        if self.dry or i >= len(self.order):
            return
        self.next_split += 1
        r, s = i % self.NR, i % self.NS
        done = self.pe_tok[i - self.NS] if i >= self.NS else None
        raw, hi, lo = self.raw[:, r, :], self.hi[:, s, :], self.lo[:, s, :]
        self.hi_tok[i] = self.act(lambda e: e.activation(hi, raw, ACT.Copy), self.raw_tok[i], done)
        self.lo_tok[i] = self.pool(
            lambda e: e.tensor_tensor(lo, raw, hi.bitcast(F32), ALU.subtract), self.hi_tok[i], done)
        self.fetch()

    def weights(self, what):
        i = len(self.used)
        self.used.append(what)
        if self.dry:
            self.order.append(what)
            self.hi_tok[i] = self.lo_tok[i] = None
            return i
        assert self.order[i] == what
        while self.next_split < min(i + self.NS, len(self.order)):
            self.prepare()
        return i

    def tiles(self, i):
        s = i % self.NS
        return self.hi[:, s, :], self.lo[:, s, :]

    def unit_done(self, i, tok):
        self.pe_tok[i] = tok

    def mm3(self, out, wh, wl, xh, xl, start, stop, *tokens, last=False):
        self.pe.wait(*tokens)
        self.pe(lambda e: e.matmul(out, wh, xh, start=start, stop=False), quiet=True)
        self.pe(lambda e: e.matmul(out, wl, xh, start=False, stop=False), quiet=True)
        return self.pe(lambda e: e.matmul(out, wh, xl, start=False, stop=stop), quiet=not last)

    def linear(self, what, x, chunks, bank):
        i = self.weights(what)
        wh, wl = self.tiles(i)
        tok = None
        self.pe.wait(bank.free, self.hi_tok[i], self.lo_tok[i])
        for n, c in enumerate(chunks):
            ws = slice(n * 128, n * 128 + 128)
            tok = self.mm3(bank.ap[:, :], wh[:, ws], wl[:, ws], x.hi[:, c, :], x.lo[:, c, :],
                           n == 0, n == len(chunks) - 1, x.ready[c], last=n == len(chunks) - 1)
        self.unit_done(i, tok)
        return tok

    def emit(self, block):
        def run(q, sems):
            def go(eng):
                for it in q.items:
                    if it[0] == "wait":
                        eng.wait_ge(sems[it[1]], it[2])
                    else:
                        ins = it[1](eng)
                        if it[2] is not None:
                            ins.then_inc(sems[it[2]], it[3])
            return go
        block.tensor(run(self.pe, self.sems))
        block.scalar(run(self.act, self.sems))
        block.vector(run(self.dve, self.sems))
        block.gpsimd(run(self.pool, self.sems))
        block.sync(run(self.sp, self.sems))


def program(nc, ctx, k, D):
    pe, act, dve, pool = k.pe, k.act, k.dve, k.pool

    def sb(name, shape, dt=F32, c=ctx):
        return c.enter_context(nc.sbuf_tensor(name, shape, dt))

    H = sb("H", [128, 8, T])
    RAW = sb("RAW", [128, k.NR, 1024])
    WH = sb("WH", [128, k.NS, 1024], F32R)
    WL = sb("WL", [128, k.NS, 1024], F32R)
    VE = sb("VE", [128, NV])
    CO = sb("CO", [128, NCC])
    ONES = sb("ONES", [128, 128])
    NT = 9
    TMP = sb("TMP", [128, NT, 576])
    RS = sb("RS", [128, 2, T])
    SM = sb("SM", [128, 64])
    SP4 = sb("SP4", [128, 2, 12])
    P0h = sb("P0h", [128, 8, T], F32R)
    P0l = sb("P0l", [128, 8, T], F32R)
    P0 = Split(P0h, P0l)
    banks = [ctx.enter_context(nc.psum_tensor(f"B{i}", [128, 512], F32)) for i in range(8)]
    BK = Ring(banks)
    TR = Ring([TMP[:, i, :] for i in range(NT)])
    ident = CO[:, 0:128]

    def vec(name, c):
        return VE[:, VCOL[name] + c:VCOL[name] + c + 1]

    k.stage("init")
    k.weights_init(RAW, WH, WL, D["w"])
    k.fetch()
    t_ve = k.load(VE[:, :], D["vecs"], sem="d_ve")
    t_h = []
    for c in range(8):
        t_h.append(k.load(H[:, c, :], D["xT"][c], sem=f"d_h{c}"))
        if c in (1, 5):
            k.fetch()
    t_co = k.load(CO[:, :], D["consts"], sem="d_co")
    t_ones = dve(lambda e: e.memset(ONES[:, :], 1.0))
    t_mh = dve(lambda e: e.memset(SM[:, 0:4], -0.5))
    H_tok = list(t_h)
    H_rd = [[] for _ in range(8)]
    pe.wait(t_ones)
    act.wait(t_ve)
    dve.wait(t_ve)
    sm_free = [None]
    ACC = sb("ACC", [128, T])
    acc_free = [None]

    acc_n = [0]
    acc2 = [None]

    acc2_tok = [None]

    def sumsq(src, tok, fast=False):
        acc_n[0] += 1
        if fast and acc_n[0] % 2 == 0:
            s = TR.take()
            a = act(lambda e: e.activation(s.ap[:, 0:T], src, ACT.Square), tok, s.free)
            if acc2[0] is None:
                acc2[0], acc2_tok[0] = s, a
                return a
            o = acc2[0]
            acc2_tok[0] = dve(lambda e: e.tensor_tensor(o.ap[:, 0:T], o.ap[:, 0:T], s.ap[:, 0:T], ALU.add), a, acc2_tok[0])
            TR.give(s, acc2_tok[0])
            return a
        if acc_n[0] == 1:
            t = act(lambda e: e.activation(ACC[:, :], src, ACT.Square), tok, acc_free[0])
            sumsq.tok = t
            return t
        s = TR.take()
        a = act(lambda e: e.activation(s.ap[:, 0:T], src, ACT.Square), tok, s.free)
        t = pool(lambda e: e.tensor_tensor(ACC[:, :], ACC[:, :], s.ap[:, 0:T], ALU.add), a, sumsq.tok)
        TR.give(s, t)
        sumsq.tok = t
        return a

    rs_i = [0]
    rs_free = [[], []]

    def stat_a(eps):
        while acc_n[0] < 8:
            assert W.active
            W.step()
        acc_n[0] = 0
        b = BK.take()
        sums = [ACC[:, :]]
        pe.wait(sumsq.tok, b.free)
        o = acc2[0]
        if o is not None:
            sums.append(o.ap[:, 0:T])
            pe.wait(acc2_tok[0])
        for j in range(4):
            for i, x in enumerate(sums):
                t = pe(lambda e, j=j, i=i, x=x: e.matmul(b.ap[:, j:j + 1], x[:, j * 128:j * 128 + 128], ONES[:, 0:1],
                                                         start=i == 0, stop=i == len(sums) - 1),
                       quiet=not (j == 3 and i == len(sums) - 1))
        acc_free[0] = t
        if o is not None:
            TR.give(o, t)
            acc2[0] = None
        d = dve(lambda e: e.tensor_scalar(SM[:, 4:8], b.ap[:, 0:4], 1.0 / 1024, eps, ALU.mult, ALU.add), t, sm_free[0])
        BK.give(b, d)
        return pool(lambda e: e.tensor_tensor(SM[:, 8:12], SM[:, 4:8], SM[:, 0:4], ALU.pow), d, t_mh, sm_free[0])

    def stat_b(tok):
        b = BK.take()
        pe.wait(tok, b.free, t_co)
        for j in range(4):
            t = pe(lambda e, j=j: e.matmul(b.ap[:, j * 128:j * 128 + 128], SM[:, 8 + j:9 + j].to_broadcast([128, 128]),
                                           ident, start=True, stop=True), quiet=j < 3)
        sm_free[0] = t
        i = rs_i[0] % 2
        rs_i[0] += 1
        a = act(lambda e: e.activation(RS[:, i, :], b.ap[:, :], ACT.Copy), t, rs_free[i])
        BK.give(b, a)
        rs_free[i] = []
        return RS[:, i, :], a, i

    def split_scaled(dst, c, src, g, tok):
        a = act(lambda e: e.activation(dst.hi[:, c, :], src, ACT.Copy, scale=g), tok, dst.free)
        d = dve(lambda e: e.scalar_tensor_tensor(dst.lo[:, c, :], src, g, dst.hi[:, c, :].bitcast(F32),
                                                 ALU.mult, ALU.subtract), a, tok, dst.free)
        dst.ready[c] = [a, d]
        return [a, d]

    def split(dst, c, src, tok):
        a = act(lambda e: e.activation(dst.hi[:, c, :], src, ACT.Copy), tok, dst.free)
        d = dve(lambda e: e.tensor_tensor(dst.lo[:, c, :], src, dst.hi[:, c, :].bitcast(F32), ALU.subtract),
                a, tok, dst.free)
        dst.ready[c] = [a, d]
        return [a, d]

    def norm_in(c, outs):
        H_rd[c] = []
        for dst, name, off in outs:
            H_rd[c] += split_scaled(dst, c, H[:, c, :], vec(name, off + c), H_tok[c])

        def square():
            if outs:
                yield
            H_rd[c].append(sumsq(H[:, c, :], H_tok[c], not outs))
        W.add(square())

    def add_to_h(c, src, toks):
        H_tok[c] = dve(lambda e: e.tensor_tensor(H[:, c, :], H[:, c, :], src, ALU.add), toks, H_tok[c], H_rd[c])
        return H_tok[c]

    def bg(n):
        for _ in range(n):
            if k.bg:
                k.bg.pop(0)()

    rate = [1]
    W = Weave(lambda: bg(rate[0]))

    class Lag:

        def __init__(self, eps=1e-6):
            self.pend, self.n, self.eps, self.rs = [], 0, eps, None

        def put(self, evac):
            self.pend.append(evac)
            self.n += 1
            if self.n == 1:
                self.a = stat_a(self.eps)
            elif self.n == 2:
                self.rs, self.rt, self.ri = stat_b(self.a)
            if self.rs is not None:
                for f in self.pend:
                    W.add(f(self.rs, self.rt))
                self.pend = []
            W.step()

        def end(self, tok):
            rs_free[self.ri] = tok

    def scale_psum(dst, b, rs, rt, t, *w):
        return dve(lambda e: e.tensor_tensor(dst, b.ap[:, :], rs, ALU.mult), t, rt, *w)

    k.stage("even")
    scope = ExitStack()
    E1 = Split(sb("E1h", [128, 8, T], F32R, scope), sb("E1l", [128, 8, T], F32R, scope))
    E2 = Split(sb("E2h", [128, 8, T], F32R, scope), sb("E2l", [128, 8, T], F32R, scope))
    UP = sb("UP", [128, 4, 30 + T], F32, scope)
    CV = sb("CV", [128, 8, T], F32, scope)
    PBS = sb("PBS", [128, 8], F32, scope)
    LS = sb("LS", [128, T], F32, scope)
    k.prepare()
    for c in range(8):
        H_rd[c] = split_scaled(P0, c, H[:, c, :], vec("norm_even", c), H_tok[c])
    t_pad = pool(lambda e: e.memset(UP[:, :, 0:30], 0.0))
    t_pbs = dve(lambda e: e.tensor_tensor(PBS[:, :], VE[:, VCOL["pool_b"]:VCOL["pool_b"] + 8],
                                          VE[:, VCOL["pool_scale"]:VCOL["pool_scale"] + 8], ALU.mult))
    UR = Ring([UP[:, i, :] for i in range(4)])

    def bank():
        while not BK.slots:
            W.step()
        return BK.take()

    def need(n):
        while len(TR.slots) < n:
            assert W.active
            W.step()

    def temps(n):
        while len(TR.slots) < n:
            yield

    cv_tok = [None] * 8
    ls = {"t": None, "n": 0}
    us = {}

    def tap_dve(c, u, t_u, j):
        w = VE[:, VCOL["conv_a_w"] + c * 31 + j:VCOL["conv_a_w"] + c * 31 + j + 1]
        x = u.ap[:, j:j + T]
        cv_tok[c] = dve(lambda e: e.scalar_tensor_tensor(CV[:, c, :], x, w, CV[:, c, :], ALU.mult, ALU.add),
                        cv_tok[c], t_u)

    def tap_side(c, u, t_u, j, side):
        w = VE[:, VCOL["conv_a_w"] + c * 31 + j:VCOL["conv_a_w"] + c * 31 + j + 1]
        x = u.ap[:, j:j + T]
        if not side:
            s = side["sum"] = TR.take()
            side["t"] = act(lambda e: e.activation(s.ap[:, 0:T], x, ACT.Copy, scale=w), t_u, s.free)
            return
        s, m = side["sum"], TR.take()
        a = act(lambda e: e.activation(m.ap[:, 0:T], x, ACT.Copy, scale=w), t_u, m.free)
        side["t"] = pool(lambda e: e.tensor_tensor(s.ap[:, 0:T], s.ap[:, 0:T], m.ap[:, 0:T], ALU.add), a, side["t"])
        TR.give(m, side["t"])

    def conv_chain(c, u, t_u):
        side = {}

        def first():
            w = VE[:, VCOL["conv_a_w"] + c * 31:VCOL["conv_a_w"] + c * 31 + 1]
            cv_tok[c] = act(lambda e: e.activation(CV[:, c, :], u.ap[:, 0:T], ACT.Identity, bias=vec("conv_a_b", c),
                                                   scale=w), t_u)
        steps = [first]
        n_side = 5
        main = list(range(1, 31 - n_side))
        for i, j in enumerate(main):
            if i % 4 == 3 and i // 4 < n_side:
                steps.append(lambda j=j, i=i: (tap_side(c, u, t_u, 31 - n_side + i // 4, side), tap_dve(c, u, t_u, j)))
            else:
                steps.append(lambda j=j: tap_dve(c, u, t_u, j))

        def last():
            t = cv_tok[c]
            if side:
                s = side["sum"]
                cv_tok[c] = dve(lambda e: e.tensor_tensor(CV[:, c, :], CV[:, c, :], s.ap[:, 0:T], ALU.add),
                                cv_tok[c], side["t"])
                TR.give(s, cv_tok[c])
            UR.give(u, t, side.get("t"))
            ls["n"] += 1
            if ls["n"] == 2:
                o = [x for x in range(8) if cv_done[x]][0]
                ls["t"] = pool(lambda e: e.tensor_tensor(LS[:, :], CV[:, o, :], CV[:, c, :], ALU.add), cv_tok[o], cv_tok[c])
            elif ls["n"] > 2:
                ls["t"] = pool(lambda e: e.tensor_tensor(LS[:, :], LS[:, :], CV[:, c, :], ALU.add), cv_tok[c], ls["t"])
            cv_done[c] = True
        steps.append(last)
        return steps

    cv_done = [False] * 8

    def pair(c, bg_, t_g, bv, t_v, rs, rt):
        yield from temps(4)
        s, v = TR.take(), TR.take()
        d = scale_psum(s.ap[:, 0:T], bg_, rs, rt, t_g, s.free)
        BK.give(bg_, d)
        a = act(lambda e: e.activation(s.ap[:, 0:T], s.ap[:, 0:T], ACT.Sigmoid), d)
        yield
        d = scale_psum(v.ap[:, 0:T], bv, rs, rt, t_v, v.free)
        BK.give(bv, d)
        yield
        while not UR.slots:
            bg(4)
        u = UR.take()
        m = dve(lambda e: e.tensor_tensor(u.ap[:, 30:], v.ap[:, 0:T], s.ap[:, 0:T], ALU.mult), d, a, u.free, t_pad)
        TR.give(s, m)
        TR.give(v, m)
        us[c] = (u, m)
        while c % 2 and c - 1 not in us:
            yield
        if c % 2:
            x, y = (conv_chain(i, *us[i]) for i in (c - 1, c))
            for p, q in zip(x, y):
                k.bg += [p, q]

    def windows(c, v, tv):
        g = c // 2
        w = 2 << g
        cur, tok = v, tv
        for s in range(g + 1):
            sh = 1 << s
            yield from temps(1)
            nx = TR.take()
            a = pool(lambda e, cur=cur, nx=nx, sh=sh: e.tensor_tensor(
                nx.ap[:, sh:T], cur.ap[:, sh:T], cur.ap[:, 0:T - sh], ALU.add), tok, nx.free)
            b = pool(lambda e, cur=cur, nx=nx, sh=sh: e.tensor_copy(nx.ap[:, 0:sh], cur.ap[:, 0:sh]), tok, nx.free)
            if cur is not v:
                TR.give(cur, a, b)
            cur, tok = nx, [a, b]
        a = pool(lambda e, cur=cur: e.tensor_tensor(cur.ap[:, 0:16], cur.ap[:, 0:16],
                                                    CO[:, CC["cnt"] + 16 * g:CC["cnt"] + 16 * g + 16], ALU.mult), tok, t_co)
        yield
        yield
        d = dve(lambda e, cur=cur: e.scalar_tensor_tensor(v.ap[:, 0:T], cur.ap[:, 0:T], 1.0 / w, v.ap[:, 0:T],
                                                          ALU.mult, ALU.subtract), a, tok, tv)
        TR.give(cur, d)
        windows.d = d

    def bval(c, b, t):
        yield from temps(4)
        v = TR.take()
        d = scale_psum(v.ap[:, 0:T], b, lag.rs, lag.rt, t, v.free)
        BK.give(b, d)
        yield from windows(c, v, d)
        d = windows.d
        yield
        a = act(lambda e: e.activation(E2.hi[:, c, :], v.ap[:, 0:T], ACT.Copy), d, E2.free)
        yield
        x = dve(lambda e: e.tensor_tensor(E2.lo[:, c, :], v.ap[:, 0:T], E2.hi[:, c, :].bitcast(F32), ALU.subtract), a)
        E2.ready[c] = [a, x]
        TR.give(v, x)

    def silu_gate(b, t, s_ap, ts, dst, c, give=None):
        yield from temps(3)
        g, sg = TR.take(), TR.take()
        d = scale_psum(g.ap[:, 0:T], b, lag.rs, lag.rt, t, g.free)
        BK.give(b, d)
        a = act(lambda e: e.activation(sg.ap[:, 0:T], g.ap[:, 0:T], ACT.Sigmoid), d, sg.free)
        m = pool(lambda e: e.tensor_tensor(s_ap, g.ap[:, 0:T], s_ap, ALU.mult), d, ts)
        TR.give(g, a, m)
        yield
        yield
        m2 = dve(lambda e: e.tensor_tensor(sg.ap[:, 0:T], s_ap, sg.ap[:, 0:T], ALU.mult), a, m)
        if give:
            give(m2)
        yield
        a = act(lambda e: e.activation(dst.hi[:, c, :], sg.ap[:, 0:T], ACT.Copy), m2, dst.free)
        yield
        x = dve(lambda e: e.tensor_tensor(dst.lo[:, c, :], sg.ap[:, 0:T], dst.hi[:, c, :].bitcast(F32), ALU.subtract),
                a, dst.free)
        dst.ready[c] = [a, x]
        TR.give(sg, x)

    def agate(c, b, t):
        yield from temps(2)
        g = TR.take()
        d = scale_psum(AG[:, c, :], b, lag.rs, lag.rt, t)
        BK.give(b, d)
        a = act(lambda e: e.activation(g.ap[:, 0:T], AG[:, c, :], ACT.Sigmoid), d, g.free)
        yield
        yield
        ag_tok[c] = pool(lambda e: e.tensor_tensor(AG[:, c, :], AG[:, c, :], g.ap[:, 0:T], ALU.mult), a, d)
        TR.give(g, ag_tok[c])

    AG = sb("AG", [128, 8, T], F32, scope)
    ag_tok = {}
    yb = {}
    lag = Lag()

    def after(n=1):
        W.step(n)

    early = []

    def unit_pair(c):
        b1 = bank()
        t1 = k.linear(("in_even", 0, 8 + c), P0, range(8), b1)
        if c == 0:
            for i in range(8):
                H_rd[i] = H_rd[i] + [sumsq(H[:, i, :], H_tok[i], True)]
        elif c == 1:
            lag.rs, lag.rt, lag.ri = stat_b(lag.a)
            W.add(pair(*early, lag.rs, lag.rt))
        after()
        b2 = bank()
        t2 = k.linear(("in_even", 0, c), P0, range(8), b2)
        if c == 0:
            lag.a = stat_a(1e-6)
            early.extend([c, b1, t1, b2, t2])
            return
        W.add(pair(c, b1, t1, b2, t2, lag.rs, lag.rt))
        after()

    def unit_bval(c):
        b = bank()
        t = k.linear(("in_even", 0, 24 + c), P0, range(8), b)
        W.add(bval(c, b, t))
        after()

    def unit_pool(h):
        while not all(4 * h + i in E2.ready for i in range(4)):
            W.step()
        while len(TR.slots) < 5:
            W.step()
        i = k.weights(("pool", 0, h))
        wh, wl = k.tiles(i)
        pe.wait(k.hi_tok[i], k.lo_tok[i])
        for g in range(2):
            for n in range(2):
                b = bank()
                pe.wait(b.free)
                for kc in range(2):
                    o = ((g * 2 + kc) * 2 + n) * 128
                    c = (h * 2 + g) * 2 + kc
                    t = k.mm3(b.ap[:, :], wh[:, o:o + 128], wl[:, o:o + 128], E2.hi[:, c, :], E2.lo[:, c, :],
                              kc == 0, kc == 1, E2.ready[c], last=kc == 1)
                c = (h * 2 + g) * 2 + n
                s = TR.take()
                a = act(lambda e, b=b, c=c, s=s: e.activation(
                    s.ap[:, 0:T], b.ap[:, :], ACT.Identity, bias=PBS[:, c:c + 1], scale=vec("pool_scale", c)),
                    t, t_pbs, s.free)
                BK.give(b, a)
                yb[c] = (s, a)
        k.unit_done(i, t)
        E2.last = t
        after()

    def unit_bgate(c):
        b = bank()
        t = k.linear(("in_even", 0, 32 + c), P0, range(8), b)
        s, a = yb[c]
        W.add(silu_gate(b, t, s.ap[:, 0:T], a, E1, c, lambda m: TR.give(s, m)))
        after()

    def unit_agate(c):
        b = bank()
        t = k.linear(("in_even", 0, 16 + c), P0, range(8), b)
        W.add(agate(c, b, t))
        after()
        P0.last = t

    def out_unit(what, base, n, src, outs, x0=0):
        b = bank()
        while not all(c in src.ready for c in range(x0, x0 + 8)):
            W.step()
        t = k.linear((what, base, n), src, range(x0, x0 + 8), b)
        BK.give(b, add_to_h(n, b.ap[:, :], t))
        if outs is not None:
            norm_in(n, outs)
        src.last = t
        after()

    fill = ([lambda c=c: unit_bval(c) for c in range(4)] + [lambda c=c: unit_agate(c) for c in range(2)]
            + [lambda: unit_pool(0)] + [lambda c=c: unit_bgate(c) for c in range(4)]
            + [lambda c=c: unit_bval(c) for c in range(4, 8)] + [lambda c=c: unit_agate(c) for c in range(2, 4)]
            + [lambda: unit_pool(1)] + [lambda c=c: unit_bgate(c) for c in range(4, 8)]
            + [lambda c=c: unit_agate(c) for c in range(4, 8)]
            + [lambda n=n: out_unit("out_even", 1, n, E1, None) for n in range(2)]
            + [lambda: (E2.ready.clear(), W.add(layer_norm()), W.step())]
            + [lambda n=n: out_unit("out_even", 1, n, E1, None) for n in range(2, 8)])
    def layer_norm():
        while len(us) < 8:
            yield
        bg(len(k.bg))
        b = bank()
        t = pe(lambda e, b=b: e.matmul(b.ap[:, :], ONES[:, :], LS[:, :], start=True, stop=True), ls["t"], b.free)
        need(1)
        mu = TR.take()
        a = act(lambda e, b=b: e.activation(mu.ap[:, 0:T], b.ap[:, :], ACT.Copy, scale=1.0 / 1024), t, mu.free)
        BK.give(b, a)
        yield
        for c in range(8):
            need(3)
            d = dve(lambda e, c=c: e.tensor_tensor(CV[:, c, :], CV[:, c, :], mu.ap[:, 0:T], ALU.subtract),
                    a, ls["t"], cv_tok[c])
            cs.append(d)
            sumsq(CV[:, c, :], d, True)
            if c == 3:
                yield
        TR.give(mu, cs[-1])
        yield
        sa = stat_a(1e-5)
        yield
        ln_rs, ln_t, ln_i = stat_b(sa)
        for c in range(8):
            W.add(ln_chain(c, ln_rs, ln_t))
            yield
            yield
        while len(E2.ready) < 8:
            yield
        rs_free[ln_i] = [dve.last]

    cs = []

    def ln_chain(c, ln_rs, ln_t):
        yield from temps(1)
        s = TR.take()
        d = dve(lambda e: e.tensor_tensor(CV[:, c, :], CV[:, c, :], ln_rs, ALU.mult), ln_t, cs[c], sumsq.tok)
        a = act(lambda e: e.activation(s.ap[:, 0:T], CV[:, c, :], ACT.Sigmoid, bias=vec("ln_a_b", c),
                                       scale=vec("ln_a_g", c)), d, s.free)
        yield
        a2 = pool(lambda e: e.tensor_scalar(CV[:, c, :], CV[:, c, :], vec("ln_a_g", c), vec("ln_a_b", c),
                                            ALU.mult, ALU.add), a, d)
        a2 = pool(lambda e: e.tensor_tensor(CV[:, c, :], CV[:, c, :], AG[:, c, :], ALU.mult), a2, ag_tok[c])
        yield
        yield
        d = dve(lambda e: e.tensor_tensor(s.ap[:, 0:T], CV[:, c, :], s.ap[:, 0:T], ALU.mult), a2, a)
        yield
        a = act(lambda e: e.activation(E2.hi[:, c, :], s.ap[:, 0:T], ACT.Copy), d, E2.last)
        yield
        x = dve(lambda e: e.tensor_tensor(E2.lo[:, c, :], s.ap[:, 0:T], E2.hi[:, c, :].bitcast(F32), ALU.subtract),
                a, E2.last)
        E2.ready[c] = [a, x]
        TR.give(s, x)

    unit_pair(0)
    unit_pair(1)
    lam = VE[:, VCOL["lru_lambda"]:VCOL["lru_lambda"] + 12]
    a = act(lambda e: e.activation(SP4[:, 0, :], lam, ACT.Abs))
    a = act(lambda e: e.activation(SP4[:, 0, :], SP4[:, 0, :], ACT.Exp, scale=-1.0), a)
    a = act(lambda e: e.activation(SP4[:, 0, :], SP4[:, 0, :], ACT.Ln, bias=1.0), a)
    d = dve(lambda e: e.tensor_scalar(SP4[:, 1, :], lam, -1.0, 0.0, ALU.mult, ALU.max))
    d = dve(lambda e: e.tensor_tensor(SP4[:, 0, :], SP4[:, 0, :], SP4[:, 1, :], ALU.add), a, d)
    d = dve(lambda e: e.tensor_scalar(SP4[:, 0, :], SP4[:, 0, :], 4.0, None, ALU.mult), d)
    t_sp4 = dve(lambda e: e.tensor_scalar(SP4[:, 1, :], SP4[:, 0, :], -2.0, None, ALU.mult), d)
    rate[0] = 6
    at = 0
    for c in range(2, 8):
        while at < 2.5 * (c - 1):
            fill[at]()
            at += 1
        unit_pair(c)
    for f in fill[at:]:
        f()
    while len(E2.ready) < 8:
        W.step()
    W.drain()
    P0.free = [P0.last]
    lag.end([dve.last])
    for n in range(8):
        out_unit("out_even", 0, n, E2, [(P0, "norm_odd", 0)])
    fence = k.fence()
    scope.close()

    k.stage("odd")
    psc = ExitStack()
    SPT = sb("SPT", [128, NSC], F32, psc)
    PW = sb("PW", [128, 2, 5, 32], F32, psc)
    BB = sb("BB", [128, 2, 32, 16], F32, psc)
    AP = sb("AP", [128, 3, 2, 2, 32], F32, psc)
    SW = sb("SW", [128, 12, 32], F32, psc)
    scope = ExitStack()
    Yh = sb("Yh", [128, 12, T], F32R, scope)
    Yl = sb("Yl", [128, 12, T], F32R, scope)
    Y = Split(Yh, Yl)
    Y.free = fence
    XP = sb("XP", [128, 2, 3 + T], F32, scope)
    GT = sb("GT", [128, 15, T], F32, scope)
    GR = Ring([GT[:, i, :] for i in range(15)])
    XR = Ring([XP[:, i, :] for i in range(2)])
    for s in GR.slots + XR.slots:
        s.free = fence
    D4 = SPT[:, SC["d4"]:SC["d4"] + 32]
    t_xp = pool(lambda e: e.memset(XP[:, :, 0:3], 0.0), fence)
    t_sp = k.load(SPT[:, :], D["ssm"], fence, sem="d_sp")
    ch = {"t": [t_sp] + fence, "m": None}

    def small(eng, fn):
        def go():
            ch["t"] = eng(fn, ch["t"])
        k.bg.append(go)

    def sw(i):
        return SW[:, i, :]

    def spc(n):
        return SPT[:, SC[n]:SC[n] + 32]

    small(act, lambda e: e.activation(sw(0), spc("ldt"), ACT.Exp))
    small(dve, lambda e: e.tensor_tensor(sw(1), spc("lre"), sw(0), ALU.mult))
    small(act, lambda e: e.activation(sw(1), sw(1), ACT.Exp))
    small(dve, lambda e: e.tensor_tensor(sw(2), spc("lim"), sw(0), ALU.mult))
    for which, quarter in ((3, 0.0), (4, 0.25)):
        small(dve, lambda e, q=quarter: e.tensor_scalar(sw(5), sw(2), 1.0 / (2 * PI), q, ALU.mult, ALU.add))
        small(dve, lambda e: e.tensor_scalar(sw(5), sw(5), ROUND, None, ALU.add))
        small(dve, lambda e: e.tensor_scalar(sw(5), sw(5), ROUND, None, ALU.subtract))
        small(dve, lambda e: e.scalar_tensor_tensor(sw(6), sw(5), -TWO_PI_HI, sw(2), ALU.mult, ALU.add))
        small(dve, lambda e: e.scalar_tensor_tensor(sw(6), sw(5), -TWO_PI_MID, sw(6), ALU.mult, ALU.add))
        small(dve, lambda e: e.scalar_tensor_tensor(sw(6), sw(5), -TWO_PI_LO, sw(6), ALU.mult, ALU.add))
        small(dve, lambda e, q=quarter: e.tensor_scalar(sw(6), sw(6), 2 * PI * q, PI, ALU.add, ALU.min))
        small(dve, lambda e: e.tensor_scalar(sw(6), sw(6), -PI, None, ALU.max))
        small(act, lambda e, w=which: e.activation(sw(w), sw(6), ACT.Sin))
    small(dve, lambda e: e.memset(PW[:, 0, 0, :], 1.0))
    small(dve, lambda e: e.memset(PW[:, 1, 0, :], 0.0))
    small(dve, lambda e: e.tensor_tensor(PW[:, 0, 1, :], sw(1), sw(4), ALU.mult))
    small(dve, lambda e: e.tensor_tensor(PW[:, 1, 1, :], sw(1), sw(3), ALU.mult))

    def small_cmul(o, x, y, t):
        for i, (p, q) in enumerate(((0, 0), (1, 1), (0, 1), (1, 0))):
            small(dve, lambda e, i=i, p=p, q=q: e.tensor_tensor(t[i], x[p], y[q], ALU.mult))
        small(dve, lambda e: e.tensor_tensor(o[0], t[0], t[1], ALU.subtract))
        small(dve, lambda e: e.tensor_tensor(o[1], t[2], t[3], ALU.add))

    for n in (1, 2):
        small_cmul([PW[:, r, n + 1:2 * n + 1, :] for r in range(2)], [PW[:, r, 1:1 + n, :] for r in range(2)],
                   [PW[:, r, n:n + 1, :].to_broadcast([128, n, 32]) for r in range(2)],
                   [SW[:, 4 + 2 * i:4 + 2 * i + n, :] for i in range(4)])
    lre, lim = spc("lre"), spc("lim")
    small(dve, lambda e: e.tensor_tensor(sw(0), lre, lre, ALU.mult))
    small(dve, lambda e: e.tensor_tensor(sw(1), lim, lim, ALU.mult))
    small(dve, lambda e: e.tensor_tensor(sw(0), sw(0), sw(1), ALU.add))
    small(dve, lambda e: e.reciprocal(sw(0), sw(0)))
    small(dve, lambda e: e.tensor_scalar(sw(1), PW[:, 0, 1, :], 1.0, None, ALU.subtract))
    small(dve, lambda e: e.tensor_tensor(sw(2), sw(1), lre, ALU.mult))
    small(dve, lambda e: e.tensor_tensor(sw(3), PW[:, 1, 1, :], lim, ALU.mult))
    small(dve, lambda e: e.tensor_tensor(sw(4), PW[:, 1, 1, :], lre, ALU.mult))
    small(dve, lambda e: e.tensor_tensor(sw(5), sw(1), lim, ALU.mult))
    small(dve, lambda e: e.tensor_tensor(sw(2), sw(2), sw(3), ALU.add))
    small(dve, lambda e: e.tensor_tensor(sw(4), sw(4), sw(5), ALU.subtract))
    small(dve, lambda e: e.tensor_tensor(sw(2), sw(2), sw(0), ALU.mult))
    small(dve, lambda e: e.tensor_tensor(sw(4), sw(4), sw(0), ALU.mult))

    def v3(ap):
        return ap.rearrange("p (g h) -> p g h", h=16)

    def coef(i):
        return SW[:, i, :].unsqueeze(2).to_broadcast([128, 32, 16])

    br_, bi_ = (v3(SPT[:, SC[n]:SC[n] + 512]) for n in ("br", "bi"))

    def bbar():
        s = [TR.take() for _ in range(2)]
        w = ch["t"]
        for r, (x, y, op) in enumerate(((br_, bi_, ALU.subtract), (bi_, br_, ALU.add))):
            u0 = v3(s[0].ap[:, 0:512])
            u1 = v3(s[1].ap[:, 0:512])
            a = dve(lambda e, u0=u0, x=x: e.tensor_tensor(u0, coef(2), x, ALU.mult), w, s[0].free)
            b = dve(lambda e, u1=u1, y=y: e.tensor_tensor(u1, coef(4), y, ALU.mult), w, s[1].free)
            w = dve(lambda e, u0=u0, u1=u1, r=r, op=op: e.tensor_tensor(BB[:, r, :, :], u0, u1, op), a, b)
        TR.give(s[0], w)
        TR.give(s[1], w)
        ch["t"] = w
    k.bg.append(bbar)
    for v in range(3):
        if v == 0:
            small(dve, lambda e: e.tensor_copy(AP[:, 0, 0, 0, :], PW[:, 0, 4, :]))
            small(dve, lambda e: e.tensor_copy(AP[:, 0, 1, 1, :], PW[:, 1, 4, :]))
        else:
            x = [AP[:, v - 1, 0, 0, :], AP[:, v - 1, 1, 1, :]]
            small_cmul([AP[:, v, 0, 0, :], AP[:, v, 1, 1, :]], x, x, [sw(4 + i) for i in range(4)])
        small(dve, lambda e, v=v: e.tensor_copy(AP[:, v, 0, 1, :], AP[:, v, 0, 0, :]))
        small(dve, lambda e, v=v: e.tensor_scalar(AP[:, v, 1, 0, :], AP[:, v, 1, 1, :], -1.0, None, ALU.mult))

    lag = Lag()
    xcs, heads, rg_done = {}, {}, {}
    rate[0] = 1

    def xr_chain(h, b, t):
        while not (XR.slots and GR.slots):
            yield
        x, s = XR.take(), GR.take()
        d = scale_psum(x.ap[:, 3:], b, lag.rs, lag.rt, t, x.free, t_xp)
        BK.give(b, d)
        w = [VE[:, VCOL["conv_c_w"] + 4 * h + j:VCOL["conv_c_w"] + 4 * h + j + 1] for j in range(4)]
        a = act(lambda e: e.activation(s.ap, x.ap[:, 0:T], ACT.Identity, bias=vec("conv_c_b", h), scale=w[0]), d, s.free)
        yield
        for j in range(1, 4):
            a = dve(lambda e, j=j: e.scalar_tensor_tensor(s.ap, x.ap[:, j:j + T], w[j], s.ap, ALU.mult, ALU.add), a)
            yield
        XR.give(x, a)
        hi = act(lambda e: e.activation(Y.hi[:, h, :], s.ap, ACT.Copy), a, Y.free)
        yield
        lo = dve(lambda e: e.tensor_tensor(Y.lo[:, h, :], s.ap, Y.hi[:, h, :].bitcast(F32), ALU.subtract), hi, Y.free)
        Y.ready[h] = [hi, lo]
        xcs[h] = (s, a, [hi, lo])

    def unit_xr(h):
        b = bank()
        t = k.linear(("in_odd", 0, h), P0, range(8), b)
        if h == 0:
            lag.a = stat_a(1e-6)
            first.append((h, b, t))
            return
        if h == 1:
            lag.rs, lag.rt, lag.ri = stat_b(lag.a)
            W.add(xr_chain(*first[0]))
        W.add(xr_chain(h, b, t))
        after(2)
    first = []

    def head_chain(h, b0, p0, b1, p1):
        xc, tx, ts = xcs[h]
        t, ix = GR.take(), GR.take()
        a = act(lambda e: e.activation(t.ap, b0.ap[:, :], ACT.Sigmoid, bias=vec("b_rg", h)), p0, t.free)
        BK.give(b0, a)
        a2 = act(lambda e: e.activation(ix.ap, b1.ap[:, :], ACT.Sigmoid, bias=vec("b_ig", h)), p1, ix.free)
        BK.give(b1, a2)
        m = pool(lambda e: e.tensor_tensor(ix.ap, ix.ap, xc.ap, ALU.mult), a2, tx)
        yield
        e_ = xc
        q = act(lambda e: e.activation(e_.ap, t.ap, ACT.Exp, scale=SP4[:, 1, h:h + 1]), a, t_sp4, m, ts)
        q2 = act(lambda e: e.activation(t.ap, t.ap, ACT.Tanh, scale=SP4[:, 0, h:h + 1]), q)
        yield
        while not TR.slots:
            yield
        s = TR.take()
        r = act(lambda e: e.activation(s.ap[:, 0:T], t.ap, ACT.Sqrt), q2, s.free)
        yield
        n = dve(lambda e: e.scalar_tensor_tensor(t.ap, e_.ap, 1.0, t.ap, ALU.add, ALU.mult), r, q)
        yield
        r = dve(lambda e: e.scalar_tensor_tensor(s.ap[:, 0:T], e_.ap, 1.0, s.ap[:, 0:T], ALU.add, ALU.mult), r, q)
        GR.give(xc, r, n)
        n = pool(lambda e: e.tensor_scalar(t.ap, t.ap, -1.0, 1.0, ALU.mult, ALU.add), n)
        yield
        r = dve(lambda e: e.tensor_tensor(ix.ap, ix.ap, s.ap[:, 0:T], ALU.mult), r, m)
        TR.give(s, r)
        yield
        sc = dve(lambda e: e.tensor_tensor_scan(ix.ap, t.ap, ix.ap, 0.0, ALU.mult, ALU.add), n, r)
        GR.give(t, sc)
        heads[h] = (ix, sc)

    def unit_rgig(g):
        hs = range(4 * g, 4 * g + 4)
        while not (all(h in xcs for h in hs) and len(GR.slots) >= 8):
            W.step()
        i = k.weights(("rgig", 0, g))
        wh, wl = k.tiles(i)
        pe.wait(k.hi_tok[i], k.lo_tok[i])
        gens = []
        for h in hs:
            o = (h % 4) * 256
            bs = []
            for r in range(2):
                b = bank()
                pe.wait(b.free)
                ws = slice(o + 128 * r, o + 128 * r + 128)
                bs += [b, k.mm3(b.ap[:, :], wh[:, ws], wl[:, ws], Y.hi[:, h, :], Y.lo[:, h, :],
                                True, True, Y.ready[h], last=True)]
            gen = head_chain(h, *bs)
            next(gen)
            gens.append(gen)
        k.unit_done(i, bs[3])
        rg_done[g] = bs[3]
        k.prepare()
        for gen in gens:
            W.add(gen)
        after()

    def unit_gate(h):
        while h not in heads:
            W.step()
        b = bank()
        t = k.linear(("in_odd", 0, 12 + h), P0, range(8), b)
        ix, sc = heads[h]
        W.add(silu_gate(b, t, ix.ap, sc, Late(Y, [rg_done[h // 4]]), h, lambda m: GR.give(ix, m)))
        after(2)
        P0.last = t

    class Late:

        def __init__(self, y, free):
            self.hi, self.lo, self.ready, self.free = y.hi, y.lo, out_ready, free
    out_ready = {}
    for h in range(6):
        unit_xr(h)
    unit_rgig(0)
    for h in (6, 7, 8):
        unit_xr(h)
    for h in (0, 1, 2):
        unit_gate(h)
    unit_rgig(1)
    unit_gate(3)
    for h in (9, 10, 11):
        unit_xr(h)
    for h in (4, 5):
        unit_gate(h)
    unit_rgig(2)
    for h in range(6, 12):
        unit_gate(h)
    P0.free = [P0.last]
    W.step(2)
    bg(len(k.bg))
    while not all(h in out_ready for h in range(8)):
        W.step()
    Y.ready = out_ready
    for n in range(8):
        out_unit("out_odd", 0, n, Y, None)
    W.drain()
    lag.end([dve.last])
    for n in range(4):
        i = k.weights(("out_odd4", 0, n))
        wh, wl = k.tiles(i)
        pe.wait(k.hi_tok[i], k.lo_tok[i])
        for m in range(2):
            b = bank()
            pe.wait(b.free)
            for kc in range(4):
                ws = slice((4 * m + kc) * 128, (4 * m + kc) * 128 + 128)
                t = k.mm3(b.ap[:, :], wh[:, ws], wl[:, ws], Y.hi[:, 8 + kc, :], Y.lo[:, 8 + kc, :],
                          kc == 0, kc == 3, Y.ready[8 + kc], last=kc == 3)
            c = 2 * n + m
            BK.give(b, add_to_h(c, b.ap[:, :], t))
            H_rd[c] = [sumsq(H[:, c, :], H_tok[c], True)]
        k.unit_done(i, t)
    fence = k.fence()
    scope.close()

    k.stage("ssm")
    scope = ExitStack()
    U4 = sb("U4", [128, 32, 128], F32, scope)
    SS = sb("SS", [128, 129, 2, 32], F32, scope)
    BX = sb("BX", [128, 2, 32, 32], F32, scope)
    sub = ExitStack()
    U = sb("U", [128, 2, T], F32, sub)
    PX = sb("PX", [128, 2, 2, 4, 128], F32, sub)
    MT = sb("MT", [128, 2, 2, 4, 128], F32, sub)
    sa = stat_a(1e-6)
    t_px = pool(lambda e: e.memset(PX[:, :, :, :, :], 0.0), fence)
    t_ss = pool(lambda e: e.memset(SS[:, 0, :, :], 0.0), fence)
    px_free = [[], []]
    mt_free = [[], []]
    px_tok = {}

    px_mul = {}

    def in_products(q):
        t = [TR.take() for _ in range(4)]
        tv = [s.ap[:, 0:256].rearrange("p (g j h) -> p g j h", g=4, j=4) for s in t]

        def pw(r):
            return PW[:, r, 3::-1, 4 * q:4 * q + 4].rearrange("p m g -> p g m").unsqueeze(3).to_broadcast([128, 4, 4, 16])

        def b_(r):
            return BB[:, r, 4 * q:4 * q + 4, :].unsqueeze(2).to_broadcast([128, 4, 4, 16])
        tk = []
        for i, (x, y) in enumerate(((0, 0), (1, 1), (0, 1), (1, 0))):
            tk.append(pool(
                lambda e, i=i, x=x, y=y: e.tensor_tensor(tv[i], pw(x), b_(y), ALU.mult), t[i].free, ch["t"]))
        px_mul[q] = (t, tv, tk)

    def in_sums(q):
        z = q % 2
        t, tv, tk = px_mul[q]
        out = []
        for r, op in ((0, ALU.subtract), (1, ALU.add)):
            for par in range(2):
                ps = slice(64 * par, 64 * par + 64)
                o = PX[ps, z, r, :, :].rearrange("p g (j w h) -> p g j w h", j=4, w=2)[:, :, :, par, :]
                out.append(dve(lambda e, r=r, op=op, ps=ps, o=o: e.tensor_tensor(o, tv[2 * r][ps], tv[2 * r + 1][ps], op),
                               tk[2 * r], tk[2 * r + 1], px_free[z], t_px))
        for s in t:
            TR.give(s, out[-1])
        px_tok[q] = out

    def transposes(q):
        z = q % 2
        toks = []
        for r in range(2):
            b = BK.take()
            pe.wait(b.free, px_tok[q])
            for g in range(4):
                last = pe(lambda e, b=b, r=r, g=g: e.transpose(b.ap[:, g * 128:g * 128 + 128], PX[:, z, r, g, :], ident),
                          quiet=g < 3)
            a = act(lambda e, b=b, r=r: e.activation(MT[:, z, r, :, :].rearrange("p a b -> p (a b)"), b.ap[:, :],
                                                     ACT.Copy), last, mt_free[z])
            BK.give(b, a)
            toks.append(a)
        a = [act(lambda e, r=r: e.activation(BX[:, r, 4 * q:4 * q + 4, :], PX[:, z, r, :, 96:128], ACT.Copy), px_tok[q],
                 fence) for r in range(2)]
        px_free[z] = [last, *a]
        return toks, a

    in_products(0)
    rs, rt, ri = stat_b(sa)
    for c in range(8):
        H_tok[c] = dve(lambda e, c=c, rs=rs: e.scalar_tensor_tensor(H[:, c, :], H[:, c, :], vec("final_norm", c), rs,
                                                            ALU.mult, ALU.mult), rt, H_tok[c], H_rd[c])
        H_rd[c] = [sumsq(H[:, c, :], H_tok[c], True)]
    rs_free[ri] = [H_tok[7]]

    in_products(1)
    sa = stat_a(1e-6)
    in_sums(0)
    in_sums(1)
    rs, rt, ri = stat_b(sa)
    u_tok = []
    u4_tok = {}
    def chunk_u(c):
        u_tok.append(dve(lambda e, c=c, rs=rs: e.scalar_tensor_tensor(
            U[:, c % 2, :], H[:, c, :], vec("norm_mix", c), rs, ALU.mult, ALU.mult),
            rt, H_tok[c], u4_tok.get(c - 2), fence))
        H_rd[c] = H_rd[c] + [u_tok[c]]
        if c % 2 == 1:
            ts = []
            for j in range(4):
                for pr in range(4):
                    src = U[32 * pr:32 * pr + 32, :, j::4]
                    dst = U4[32 * j:32 * j + 32, 4 * (c - 1) + pr:4 * (c + 1):4, :]
                    if pr % 2:
                        ts.append(act(lambda e, d=dst, s=src: e.activation(d, s, ACT.Copy), u_tok[c - 1:c + 1], fence))
                    else:
                        ts.append(dve(lambda e, d=dst, s=src: e.tensor_copy(d, s), u_tok[c - 1:c + 1], fence))
            u4_tok[c - 1] = u4_tok[c] = ts
    bx_tok = []
    v_tok = []

    def combine(q, v, d0, n, s0, t, step, im=pool):
        xs = slice(4 * q, 4 * q + 4)

        def at(c0, r):
            return SS[:, c0:c0 + (n - 1) * step + 1:step, r, xs]

        def co(i, r):
            return AP[:, v, i, r, xs].unsqueeze(1).to_broadcast([128, n, 4])
        s = TR.take()
        out = []
        for r, eng in ((0, dve), (1, im)):
            o = s.ap[:, 256 * r:256 * r + 4 * n].rearrange("p (c x) -> p c x", x=4)
            for i in range(2):
                a = eng(lambda e, o=o, r=r, i=i: e.tensor_tensor(o, at(s0, r ^ i), co(i, r), ALU.mult), t,
                        s.free, ch["t"], out[-1:] if i else None)
                a = eng(lambda e, o=o, r=r: e.tensor_tensor(at(d0, r), at(d0, r), o, ALU.add), a)
                out.append(a)
        TR.give(s, out)
        return out
    up_tok = []

    def up(q):
        t = combine(q, 0, 2, 64, 1, v_tok[q], 2)
        up_tok.append(combine(q, 1, 4, 32, 2, t, 4, dve))

    ahead = transposes(0)
    chunk_u(0)
    chunk_u(1)
    for q in range(8):
        z = q % 2
        mt, a = ahead
        if q < 7:
            ahead = transposes(q + 1)
        bx_tok.append(a)
        for hp in range(2):
            b = BK.take()
            pe.wait(b.free, mt, u4_tok[q])
            for x in range(2):
                g = 2 * hp + x
                for r in range(2):
                    t = pe(lambda e, b=b, r=r, x=x, g=g, z=z, q=q: e.matmul(
                        b.ap[:, 256 * x + 128 * r:256 * x + 128 * r + 128], MT[:, z, r, g, :], U4[:, 4 * q + g, :],
                        start=True, stop=True), quiet=not (x == 1 and r == 1))
            o = SS[:, 1:129, :, 4 * q + 2 * hp:4 * q + 2 * hp + 2].rearrange("p c r x -> p x r c")
            a = act(lambda e, b=b, o=o: e.activation(o, b.ap[:, :].rearrange("p (x r c) -> p x r c", x=2, r=2), ACT.Copy),
                    t, fence)
            BK.give(b, a)
        v_tok.append(a)
        mt_free[z] = [t]
        if q + 2 < 8:
            in_products(q + 2)
            in_sums(q + 2)
        if q % 2 == 0 and q < 6:
            chunk_u(q + 2)
            chunk_u(q + 3)
        fence2 = [pe.last, act.last, dve.last]
        if q:
            up(q - 1)
    up(7)
    rs_free[ri] = [u_tok[7]]
    sub.close()
    sub = ExitStack()
    CA = sb("CA", [128, 3, 2, 4, 5, 32], F32, sub)
    TT = sb("TT", [128, 3, 4, 128], F32, sub)
    t_ca = act(lambda e: e.activation(CA[:, :, :, :, :, :].rearrange("p a b c d e -> p (a b c d e)"),
                                      ONES[:, 0:1].to_broadcast([128, 3 * 2 * 4 * 5 * 32]), ACT.Copy, scale=0.0), fence2)
    t_tt = act(lambda e: e.activation(TT[:, :, :, :].rearrange("p a b c -> p (a b c)"),
                                      ONES[:, 0:1].to_broadcast([128, 3 * 4 * 128]), ACT.Copy, scale=0.0), fence2)
    cr_, ci_, ncr_ = (v3(SPT[:, SC[n]:SC[n] + 512]) for n in ("cr", "ci", "br"))
    t_ncr = dve(lambda e: e.tensor_scalar(SPT[:, SC["br"]:SC["br"] + 512], SPT[:, SC["cr"]:SC["cr"] + 512], -1.0, None,
                                          ALU.mult), ch["t"])
    ca_free = [[], [], []]
    ca_tok, tt_tok = {}, {}

    tab = {}

    def table_products(q):
        need(4)
        t = [TR.take() for _ in range(4)]
        tv = [s.ap[:, 0:320].rearrange("p (g m h) -> p g m h", g=4, m=5) for s in t]

        def pw(r):
            return PW[:, r, :, 4 * q:4 * q + 4].rearrange("p m g -> p g m").unsqueeze(3).to_broadcast([128, 4, 5, 16])

        def c_(x):
            return x[:, 4 * q:4 * q + 4, :].unsqueeze(2).to_broadcast([128, 4, 5, 16])
        tk = []
        for i, (x, y) in enumerate(((cr_, 0), (ci_, 1), (ncr_, 1), (ci_, 0))):
            tk.append(pool(lambda e, o=tv[i], x=c_(x), y=pw(y): e.tensor_tensor(o, x, y, ALU.mult), t[i].free, ch["t"],
                           t_ncr))
        tab[q] = (t, tv, tk)

    def table_sums(q):
        z = q % 3
        t, tv, tk = tab[q]
        out = []
        for r in range(2):
            for par in range(2):
                ps = slice(64 * par, 64 * par + 64)
                out.append(dve(lambda e, ps=ps, o=CA[ps, z, r, :, :, 16 * par:16 * par + 16], x=tv[2 * r], y=tv[2 * r + 1]:
                               e.tensor_tensor(o, x[ps], y[ps], ALU.subtract), tk, ca_free[z], t_ca))
        for s in t:
            TR.give(s, out[-1])
        ca_tok[q] = out

    def toeplitz(q):
        z = q % 3
        b = BK.take()
        pe.wait(b.free, ca_tok[q], bx_tok)
        for g in range(4):
            for r in range(2):
                t = pe(lambda e, b=b, g=g, r=r: e.matmul(
                    b.ap[0:32, 128 * g:128 * g + 128], BX[:, r, 4 * q + g, :],
                    CA[:, z, r, g, 0:4, :].rearrange("p m h -> p (m h)"), start=r == 0, stop=r == 1),
                    quiet=not (g == 3 and r == 1))
        bv = b.ap[0:32, :].rearrange("p (g n) -> p g n", g=4)
        ts = [act(lambda e, j=j: e.activation(TT[32 * j:32 * j + 32, z, :, 32 * j:128], bv[:, :, 0:128 - 32 * j],
                                              ACT.Copy), t, ca_free[z], t_tt) for j in range(4)]
        BK.give(b, ts[-1])
        tt_tok[q] = ts

    def diagonal(q):
        z = q % 3
        ts = tt_tok[q]
        tt_tok[q] = []
        for g in range(4):
            d4 = D4[:, 4 * q + g:4 * q + g + 1]
            tt_tok[q].append(dve(lambda e, g=g, d4=d4: e.scalar_tensor_tensor(
                TT[:, z, g, :], ident, d4, TT[:, z, g, :], ALU.mult, ALU.add), ts))

    table_products(0)
    table_products(1)
    tS = [up_tok, t_ss]
    SC4 = TR.take()
    s1, s2 = SC4.ap[:, 0:64].rearrange("p (r x) -> p r x", r=2), SC4.ap[:, 64:128].rearrange("p (r x) -> p r x", r=2)
    w = SC4.free
    for c in range(8, 128, 4):
        a = dve(lambda e, c=c: e.tensor_tensor(s1, SS[:, c - 4, :, :], AP[:, 2, 0, :, :], ALU.mult), tS, w)
        b = dve(lambda e, c=c: e.tensor_tensor(s2, SS[:, c - 4, ::-1, :], AP[:, 2, 1, :, :], ALU.mult), tS, w)
        a = dve(lambda e, c=c: e.tensor_tensor(s1, s1, SS[:, c, :, :], ALU.add), a)
        tS = dve(lambda e, c=c: e.tensor_tensor(SS[:, c, :, :], s1, s2, ALU.add), a, b)
        w = tS
        if c == 24:
            table_sums(0)
            toeplitz(0)
            table_products(2)
        elif c == 56:
            diagonal(0)
            table_sums(1)
    TR.give(SC4, tS)
    G = P0

    def gelu(q, y, g1, yt):
        Y_, G_ = y.ap[:, 0:T], g1.ap[:, 0:T]
        a = act(lambda e: e.activation(G_, Y_, ACT.Square, scale=math.sqrt(0.044715)), yt, g1.free)
        yield
        a = dve(lambda e: e.scalar_tensor_tensor(G_, G_, 1.0, Y_, ALU.add, ALU.mult), a)
        yield
        a = act(lambda e: e.activation(G_, G_, ACT.Sigmoid, scale=2 * math.sqrt(2 / PI)), a)
        yield
        a = dve(lambda e: e.tensor_tensor(G_, G_, Y_, ALU.mult), a)
        TR.give(y, a)
        yield
        x = act(lambda e: e.activation(G.hi[:, q, :], G_, ACT.Copy), a, G.free)
        yield
        z = dve(lambda e: e.tensor_tensor(G.lo[:, q, :], G_, G.hi[:, q, :].bitcast(F32), ALU.subtract), x, G.free)
        G.ready[q] = [x, z]
        TR.give(g1, z)

    def down1(q):
        if q < 8:
            down_tok[q] = combine(q, 1, 6, 31, 4, tS, 4, dve if q % 2 else pool)

    def down0(q):
        if q < 8:
            down_tok[q] = combine(q, 0, 3, 63, 2, down_tok[q], 2)

    down_tok = {}
    down1(0)
    down0(0)
    down1(1)
    down0(1)
    down1(2)
    for q in range(8):
        if q < 6:
            table_sums(q + 2)
        need(2)
        down0(q + 2)
        down1(q + 3)
        if q < 5:
            table_products(q + 3)
        if q < 7:
            toeplitz(q + 1)
            diagonal(q + 1)
        z = q % 3
        b = BK.take()
        pe.wait(b.free, down_tok[q], tt_tok[q], u4_tok[q])
        for g in range(4):
            o = b.ap[:, 128 * g:128 * g + 128]
            pe(lambda e, o=o, z=z, g=g, q=q: e.matmul(o, TT[:, z, g, :], U4[:, 4 * q + g, :], start=True, stop=False),
               quiet=True)
            for r in range(2):
                t = pe(lambda e, o=o, z=z, g=g, q=q, r=r: e.matmul(
                    o, CA[:, z, r, g, 1:5, :].rearrange("p m h -> p (m h)"), SS[:, 0:128, r, 4 * q + g],
                    start=False, stop=r == 1), quiet=not (g == 3 and r == 1))
        ca_free[z] = [t]
        need(2)
        y, g1 = TR.take(), TR.take()
        yt = []
        for i in range(4):
            for pr in range(4):
                o, x = y.ap[32 * pr:32 * pr + 32, i:T:4], b.ap[32 * i:32 * i + 32, 128 * pr:128 * pr + 128]
                yt.append(act(lambda e, o=o, x=x: e.activation(o, x, ACT.Copy), t, y.free))
        BK.give(b, yt)
        W.step()
        W.add(gelu(q, y, g1, yt))
        W.step(2)
    W.drain()
    fence = k.fence()
    sub.close()
    scope.close()
    psc.close()
    scope = ExitStack()
    P1 = Split(sb("P1h", [128, 8, T], F32R, scope), sb("P1l", [128, 8, T], F32R, scope))
    PJ = sb("PJ", [128, 8, T], F32, scope)
    KT = sb("KT", [128, 2, T], F32, scope)
    V = sb("V", [128, 4, 256], F32, scope)
    RO = sb("RO", [128, 2, T], F32, scope)
    RK = sb("RK", [128, 4], F32, scope)
    sub = ExitStack()
    P2 = Split(sb("P2h", [128, 8, T], F32R, sub), sb("P2l", [128, 8, T], F32R, sub))
    P1.free = P2.free = fence
    PT = Split(P2.hi[:, 0:2, :], P2.lo[:, 0:2, :])
    PT.free = P2.free

    def load_p(l, PT):
        for kc in range(2):
            s = TR.take()
            a = k.load(s.ap[:, 0:T], D["pT"][l][:, kc, :], s.free, sem=f"d_p{l}{kc}")
            TR.give(s, *split(PT, kc, s.ap[:, 0:T], a))

    load_p(0, PT)
    for n in range(8):
        b = bank()
        t = k.linear(("glu", 0, 8 + n), P0, range(8), b)
        s = TR.take()
        a = act(lambda e, b=b, s=s: e.activation(s.ap[:, 0:T], b.ap[:, :], ACT.Sigmoid), t, s.free)
        BK.give(b, a)
        b = bank()
        t = k.linear(("glu", 0, n), P0, range(8), b)
        d = dve(lambda e, b=b, s=s: e.tensor_tensor(s.ap[:, 0:T], s.ap[:, 0:T], b.ap[:, :], ALU.mult), t, a)
        BK.give(b, d)
        TR.give(s, add_to_h(n, s.ap[:, 0:T], d))
        norm_in(n, [(P1, "norm_mlp", 0)])
        W.step()
    P0.free = [t]

    def mlp(l, src, ha, hb, dst):
        bufs = [ha, hb]
        lag = Lag()

        def up(qt):
            dstq = bufs[qt % 2]
            for c in range(8):
                b = bank()
                t = k.linear((f"up{l}", 0, 8 * qt + c), src, range(8), b)

                def evac(rs, rt, b=b, t=t, c=c):
                    yield from temps(1)
                    s = TR.take()
                    d = dve(lambda e: e.scalar_tensor_tensor(s.ap[:, 0:T], b.ap[:, :], 0.0, rs, ALU.max, ALU.mult),
                            t, rt, s.free)
                    BK.give(b, d)
                    a = act(lambda e: e.activation(dstq.hi[:, c, :], s.ap[:, 0:T], ACT.Square), d, dstq.free)
                    a2 = act(lambda e: e.activation(s.ap[:, 0:T], s.ap[:, 0:T], ACT.Square), a)
                    yield
                    x = dve(lambda e: e.tensor_tensor(dstq.lo[:, c, :], s.ap[:, 0:T], dstq.hi[:, c, :].bitcast(F32),
                                                      ALU.subtract), a2, dstq.free)
                    TR.give(s, x)
                    dstq.ready[c] = [a, x]
                lag.put(evac)
            return t

        def down(qt):
            x = bufs[qt % 2]
            W.drain()
            for n in range(8):
                b = bank()
                t = k.linear((f"down{l}", qt, n), x, range(8), b)
                BK.give(b, add_to_h(n, b.ap[:, :], t))
                if qt == 3:
                    norm_in(n, [(dst, "norm_ple", 8 * l)])
                W.step()
            x.free = [t]
        up(0)
        up(1)
        down(0)
        up(2)
        down(1)
        src.free = [up(3)]
        W.drain()
        lag.end([dve.last])
        down(2)
        down(3)

    t_proj = [None]
    pj_tok = {0: [], 1: []}

    def proj_unit(l, h, PJ, PT, free):
        toks = pj_tok[l]
        i = k.weights((f"proj{l}", 0, h))
        wh, wl = k.tiles(i)
        pe.wait(k.hi_tok[i], k.lo_tok[i])
        for n in range(4):
            b = bank()
            pe.wait(b.free)
            for kc in range(2):
                ws = slice((n * 2 + kc) * 128, (n * 2 + kc) * 128 + 128)
                t = k.mm3(b.ap[:, :], wh[:, ws], wl[:, ws], PT.hi[:, kc, :], PT.lo[:, kc, :],
                          kc == 0, kc == 1, PT.ready[kc], last=kc == 1)
            toks.append(act(lambda e, b=b, c=4 * h + n: e.activation(PJ[:, c, :], b.ap[:, :], ACT.Copy), t, free))
            BK.give(b, toks[-1])
        k.unit_done(i, t)
        t_proj[0] = t
        return toks

    def ple(l, src, PJ, tp, outs):
        lag = Lag()
        for n in range(8):
            b = bank()
            t = k.linear((f"gate{l}", 0, n), src, range(8), b)

            def evac(rs, rt, b=b, t=t, n=n):
                yield from temps(1)
                s = TR.take()
                d = scale_psum(s.ap[:, 0:T], b, rs, rt, t, s.free)
                BK.give(b, d)
                a = act(lambda e: e.activation(s.ap[:, 0:T], s.ap[:, 0:T], ACT.Sigmoid), d)
                yield
                d = dve(lambda e: e.tensor_tensor(s.ap[:, 0:T], s.ap[:, 0:T], PJ[:, n, :], ALU.mult), a, tp[n])
                TR.give(s, add_to_h(n, s.ap[:, 0:T], d))
                norm_in(n, outs)
            lag.put(evac)
        src.free = [t]
        W.drain()
        lag.end([dve.last])

    for h in range(2):
        tp = proj_unit(0, h, PJ, PT, fence)
    P2.free = [t_proj[0]]
    mlp(0, P1, P0, P2, P1)
    ple(0, P1, PJ, tp, [(P2, "kv_norm", 0), (P0, "norm_mix", 8)])

    fence = k.fence()
    k.stage("att")
    AS = ACC[:, :].rearrange("p (n k) -> p n k", n=16)
    t_ro = k.load(RO[:, :, :], D["rope"], fence, sem="d_ro")
    rot = CO[:, CC["rot"]:CC["rot"] + 128]
    lag = Lag()
    rope_tok = {}

    def rope(b, t, dst, key, free):
        yield from temps(2)
        s, m = TR.take(), TR.take()
        d = scale_psum(s.ap[:, 0:T], b, lag.rs, lag.rt, t, s.free)
        BK.give(b, d)
        yield
        while not BK.slots:
            yield
        b = BK.take()
        t = pe(lambda e, b=b: e.matmul(b.ap[:, :], rot, s.ap[:, 0:T], start=True, stop=True), d, b.free)
        x = dve(lambda e, b=b: e.tensor_tensor(m.ap[:, 0:T], b.ap[:, :], RO[:, 1, :], ALU.mult), t, m.free, t_ro)
        BK.give(b, x)
        y = pool(lambda e: e.tensor_tensor(s.ap[:, 0:T], s.ap[:, 0:T], RO[:, 0, :], ALU.mult), t, t_ro)
        yield
        r = dve(lambda e: e.tensor_tensor(dst, s.ap[:, 0:T], m.ap[:, 0:T], ALU.add), x, y, free)
        TR.give(s, r)
        TR.give(m, r)
        rope_tok[key] = r

    b0, b1 = bank(), bank()
    t0 = k.linear(("wk", 0, 0), P2, range(8), b0)
    sa = stat_a(1e-6)
    t1 = k.linear(("wk", 0, 1), P2, range(8), b1)
    lag.rs, lag.rt, lag.ri = stat_b(sa)
    t_rk = dve(lambda e: e.tensor_copy(RK[:, :], SM[:, 8:12]), sa, fence)
    W.add(rope(b0, t0, KT[:, 0, :], ("k", 0), fence))
    W.add(rope(b1, t1, KT[:, 1, :], ("k", 1), fence))
    after()
    vb = [bank() for _ in range(4)]
    for hf in range(2):
        i = k.weights(("wv", 0, hf))
        wh, wl = k.tiles(i)
        pe.wait(k.hi_tok[i], k.lo_tok[i], [b.free for b in vb])
        for tb in range(4):
            for kc in range(4):
                c = 4 * hf + kc
                xh = P2.hi[:, c, 128 * tb:128 * tb + 128]
                xl = P2.lo[:, c, 128 * tb:128 * tb + 128]
                ws = slice(256 * kc, 256 * kc + 256)
                o = vb[tb].ap[:, 0:256]
                pe.wait(P2.ready[c])
                pe(lambda e, o=o, xh=xh, w=wh[:, ws], c=c: e.matmul(o, xh, w, start=c == 0, stop=False), quiet=True)
                pe(lambda e, o=o, xh=xh, w=wl[:, ws]: e.matmul(o, xh, w, start=False, stop=False), quiet=True)
                t = pe(lambda e, o=o, xl=xl, w=wh[:, ws], c=c: e.matmul(o, xl, w, start=False, stop=c == 7),
                       quiet=kc != 3)
            if hf == 1:
                a = act(lambda e, o=o, tb=tb: e.activation(V[:, tb, :], o, ACT.Copy, scale=RK[:, tb:tb + 1]), t, t_rk, fence)
                BK.give(vb[tb], a)
                rope_tok["v", tb] = a
        k.unit_done(i, t)
        after()
    P2.free = [t]
    sub.close()
    sub = ExitStack()
    Q = sb("Q", [128, 8, T], F32, sub)

    def unit_q(n):
        b = bank()
        t = k.linear(("wq", 0, n), P0, range(8), b)
        W.add(rope(b, t, Q[:, n, :], ("q", n), P2.free))
        after()
        P0.free = [t]

    mask = CO[:, CC["mask"]:CC["mask"] + 256]
    sink = VE[:, VCOL["sinks"]:VCOL["sinks"] + 16]
    o_parts = {}

    def heads4(n):
        kv, blk = n // 4, n % 4
        k0, nk = (128, 128) if blk == 0 else (0, 256)
        p_ = slice(64 * (kv % 2), 64 * (kv % 2) + 64)
        ks = slice(128 * blk - 128 + k0, 128 * blk + 128)
        st = AS[:, n, :]
        out, mx, bs = [], [], []
        for hp in range(2):
            b = bank()
            pe.wait(b.free, rope_tok["k", kv // 2])
            for j in range(2):
                c = 4 * (kv // 2) + 2 * hp + j
                t = pe(lambda e, b=b, j=j, c=c: e.matmul(
                    b.ap[:, 256 * j:256 * j + nk], Q[p_, c, 128 * blk:128 * blk + 128], KT[p_, kv // 2, ks],
                    start=True, stop=True), rope_tok["q", c], quiet=j == 0)
            bs.append((b, t))
        for b, t in bs:
            yield
            need(1)
            s = TR.take()
            bv = b.ap[:, :].rearrange("p (a k) -> p a k", a=2)[:, :, 0:nk]
            sv = s.ap[:, 0:512].rearrange("p (a k) -> p a k", a=2)[:, :, 0:nk]
            mv = mask[:, k0:256].unsqueeze(1).to_broadcast([128, 2, nk])
            d = dve(lambda e, bv=bv, sv=sv, mv=mv: e.scalar_tensor_tensor(sv, bv, 0.125, mv, ALU.mult, ALU.add), t, s.free)
            BK.give(b, d)
            hp = len(out)
            mx.append(dve(lambda e, sv=sv, hp=hp: e.tensor_reduce(st[:, 2 * hp:2 * hp + 2], sv, AX.X, ALU.max), d,
                          acc_free[0]))
            out.append((s, sv))
        sk = sink[:, 4 * kv:4 * kv + 4]
        d = dve(lambda e: e.tensor_tensor(st[:, 0:4], st[:, 0:4], sk, ALU.max), mx)
        d1 = dve(lambda e: e.tensor_scalar(st[:, 4:8], st[:, 0:4], -1.0, None, ALU.mult), d)
        d2 = dve(lambda e: e.tensor_tensor(st[:, 8:12], sk, st[:, 0:4], ALU.subtract), d)
        ex = []
        hv = [out[h // 2][1][:, h % 2, :] for h in range(4)]
        for h in range(4):
            ex.append(act(lambda e, sv=hv[h], h=h: e.activation(sv, sv, ACT.Exp, bias=st[:, 4 + h:5 + h],
                                                                accum_out=st[:, 12 + h:13 + h]), d1))
        a = act(lambda e: e.activation(st[:, 8:12], st[:, 8:12], ACT.Exp), d2)
        yield
        d = dve(lambda e: e.tensor_tensor(st[:, 16:20], st[:, 12:16], st[:, 8:12], ALU.add), a, ex)
        d = dve(lambda e: e.reciprocal(st[:, 16:20], st[:, 16:20]), d)
        w = [pool(lambda e, sv=hv[h], h=h: e.tensor_scalar(sv, sv, st[:, 16 + h:17 + h], 1.0, ALU.mult, ALU.mult), d, ex[h])
             for h in range(4)]
        yield
        wt = []
        for hf in ([1] if blk == 0 else [0, 1]):
            need(1)
            b, s = bank(), TR.take()
            pe.wait(b.free)
            for h in range(4):
                sv = hv[h][:, 128 * (hf if blk else 0):128 * (hf if blk else 0) + 128]
                t = pe(lambda e, b=b, h=h, sv=sv: e.transpose(b.ap[:, 128 * h:128 * h + 128], sv, ident), w[h],
                       quiet=h < 3)
            a = act(lambda e, b=b, s=s: e.activation(s.ap[:, 0:512], b.ap[:, :], ACT.Copy), t, s.free)
            BK.give(b, a)
            wt.append((s, a, blk - 1 + hf))
        for s, _ in out:
            TR.give(s, t)
        yield
        b = bank()
        pe.wait(b.free)
        for i, (s, a, vb_) in enumerate(wt):
            t = pe(lambda e, s=s, vb_=vb_, i=i: e.matmul(b.ap[p_, :], V[:, vb_, 64 * kv:64 * kv + 64], s.ap[:, 0:512],
                                                         start=i == 0, stop=i == len(wt) - 1),
                   a, rope_tok["v", vb_], quiet=i < len(wt) - 1)
        for s, _, _ in wt:
            TR.give(s, t)
        cs = slice(4 * (kv // 2), 4 * (kv // 2) + 4)
        ts = slice(128 * blk, 128 * blk + 128)
        bv = b.ap[p_, :].rearrange("p (c t) -> p c t", c=4)
        hi, lo = P1.hi[p_, cs, ts], P1.lo[p_, cs, ts]
        yield
        a = act(lambda e: e.activation(hi, bv, ACT.Copy), t, P1.free)
        yield
        d = dve(lambda e: e.tensor_tensor(lo, bv, hi.bitcast(F32), ALU.subtract), a, P1.free)
        BK.give(b, d)
        for c in range(4 * (kv // 2), 4 * (kv // 2) + 4):
            o_parts.setdefault(c, []).extend([a, d])
        yield

    for n in range(5):
        unit_q(n)
    while ("q", 3) not in rope_tok:
        W.step()
    gens = [heads4(n) for n in range(16)]

    def go(n):
        if 0 <= n < 16:
            next(gens[n])

    go(0)
    for n in range(18):
        if n + 1 == 8:
            while ("q", 7) not in rope_tok:
                W.step()
        go(n + 1)
        go(n - 2)
        go(n - 2)
        go(n)
        go(n - 1)
        go(n)
        if n in (0, 2, 4):
            unit_q(5 + n // 2)
        if n == 6:
            lag.end([dve.last])
            PT = Split(P0.hi[:, 0:2, :], P0.lo[:, 0:2, :])
            PT.free = P0.free
            load_p(1, PT)
        if n in (9, 12):
            tp = proj_unit(1, (n - 9) // 3, PJ, PT, fence)
        go(n - 1)
        go(n - 2)
        W.step()
    W.drain()
    P0.free = [t_proj[0]]
    for c in range(8):
        P1.ready[c] = o_parts[c]
    acc_free[0] = [dve.last, act.last]
    sub.close()
    P2c = Split(sb("P2hc", [128, 8, T], F32R, scope), sb("P2lc", [128, 8, T], F32R, scope))
    P2c.free = k.fence()
    for n in range(8):
        b = BK.take()
        t = k.linear(("wo", 0, n), P1, range(8), b)
        BK.give(b, add_to_h(n, b.ap[:, :], t))
        norm_in(n, [(P0, "norm_mlp", 8)])
        W.step()
    P1.free = [t]
    mlp(1, P0, P1, P2c, P0)
    ple(1, P0, PJ, tp, [])
    rs, rt, ri = stat_b(stat_a(1e-6))
    for c in range(8):
        s = TR.take()
        d = dve(lambda e, c=c, s=s, rs=rs: e.scalar_tensor_tensor(s.ap[:, 0:T], H[:, c, :], vec("norm_final", c), rs,
                                                          ALU.mult, ALU.mult), rt, H_tok[c], s.free)
        o = k.load(D["out"][c], s.ap[:, 0:T], d, sem="d_out")
    k.sp.wait(o)
    scope.close()


def matrices(x):
    heads = [(0, 4), (1, 5), (2, 6), (3, 7), (8, 12), (9, 13), (10, 14), (11, 15)]
    cols = np.concatenate([np.arange(64) + 64 * h for pair in heads for h in pair])
    rg = np.concatenate([x["w_rg"][0], x["w_ig"][0]])
    return {
        "in_even": x["w_in_even"][0], "out_even": x["w_out_even"][0], "pool": x["pool_w"][0],
        "in_odd": x["w_in_odd"][0], "out_odd": x["w_out_odd"][0], "rgig": rg,
        "glu": x["ssm_w_glu_2"][0], "up0": x["w_up_2"][0], "down0": x["w_down_2"][0],
        "up1": x["w_up_2"][1], "down1": x["w_down_2"][1], "gate0": x["w_ple_gate_2"][0],
        "gate1": x["w_ple_gate_2"][1], "proj0": x["w_ple_proj_2"][0], "proj1": x["w_ple_proj_2"][1],
        "wk": x["w_k_2"], "wv": x["w_v_2"], "wq": x["w_q_2"][0][:, cols], "wo": x["w_o_2"][0][cols, :],
    }


def unit_tiles(what):
    name, a, b = what
    if name == "pool":
        return None
    if name == "rgig":
        return None
    if name in ("proj0", "proj1"):
        return [(kc, 4 * b + n) for n in range(4) for kc in range(2)]
    if name == "out_odd4":
        return [(8 + kc, 2 * b + m) for m in range(2) for kc in range(4)]
    if name == "wv":
        return [(4 * b + kc, n) for kc in range(4) for n in range(2)]
    return [(8 * a + kc, b) for kc in range(8)]


def pack(order, mats):
    out = np.empty((len(order), 128, 8, 128), np.float32)
    for i, what in enumerate(order):
        name, a, b = what
        m = mats["out_odd" if name == "out_odd4" else name]
        if name == "pool":
            for g in range(2):
                for kc in range(2):
                    for n in range(2):
                        out[i, :, (g * 2 + kc) * 2 + n, :] = m[2 * b + g, kc * 128:kc * 128 + 128, n * 128:n * 128 + 128]
        elif name == "rgig":
            for h in range(4):
                out[i, :, 2 * h, :] = m[4 * b + h]
                out[i, :, 2 * h + 1, :] = m[12 + 4 * b + h]
        else:
            for j, (r, c) in enumerate(unit_tiles(what)):
                out[i, :, j, :] = m[r * 128:r * 128 + 128, c * 128:c * 128 + 128]
    return out.reshape(len(order), 128, 1024)


def vectors(x):
    cols = []

    def add(v, n):
        cols.append(np.asarray(v).reshape(n, 128).T)

    add(x["norm_even"][0], 8)
    cols.append(x["conv_a_w"][0].reshape(31, 8, 128).transpose(2, 1, 0).reshape(128, 248))
    for n in ("conv_a_b", "ln_a_g", "ln_a_b", "pool_b", "pool_scale", "norm_odd"):
        add(x[n][0], 8)
    cols.append(x["conv_c_w"][0].reshape(4, 12, 128).transpose(2, 1, 0).reshape(128, 48))
    for n in ("conv_c_b", "b_rg", "b_ig", "lru_lambda"):
        add(x[n][0], 12)
    add(x["final_norm"], 8)
    add(x["norm_mix_2"], 16)
    add(x["ssm_d_2"][0], 8)
    add(x["kv_norm_2"], 8)
    add(x["norm_mlp_2"], 16)
    add(x["norm_ple_2"], 16)
    add(x["norm_final_2"], 8)
    cols.append(np.repeat(x["attn_sinks_2"][0][None, :], 128, axis=0))
    return np.ascontiguousarray(np.concatenate(cols, axis=1))


def constants():
    c = np.zeros((128, NCC), np.float32)
    c[:, 0:128] = np.eye(128, dtype=np.float32)
    for base in (0, 64):
        for d in range(8):
            c[base + d + 8, CC["rot"] + base + d] = -1.0
            c[base + d, CC["rot"] + base + d + 8] = 1.0
    i = np.arange(128)[:, None]
    j = np.arange(256)[None, :]
    ok = (j <= i + 128) & (i + 128 - j < 128)
    c[:, CC["mask"]:CC["mask"] + 256] = np.where(ok, 0.0, -1e30)
    for g in range(4):
        w = 2 << g
        c[:, CC["cnt"] + 16 * g:CC["cnt"] + 16 * g + 16] = w / np.minimum(np.arange(1, 17), w)
    return c


def rope_tables():
    inv = np.float32(500000.0) ** (-np.arange(0, 16, 2, dtype=np.float32) / np.float32(16))
    ang = np.arange(T, dtype=np.float32)[None, :] * inv[:, None].astype(np.float32)
    r = np.zeros((128, 2, T), np.float32)
    r[:, 0, :] = 1.0
    for base in (0, 8, 64, 72):
        r[base:base + 8, 0, :] = np.cos(ang)
        r[base:base + 8, 1, :] = np.sin(ang)
    return r


def ssm_parameters(x):
    def gn(a):
        return a.reshape(32, 2, 64).transpose(1, 2, 0).reshape(128, 32)

    ldt = np.repeat(x["ssm_log_dt_2"][0][:, None], 64, axis=1)
    b = [x[n][0].reshape(32, 2, 64, 16).transpose(1, 2, 0, 3).reshape(128, 512) for n in ("ssm_b_re_2", "ssm_b_im_2")]
    c = [x[n][0].reshape(32, 2, 16, 64).transpose(1, 3, 0, 2).reshape(128, 512) for n in ("ssm_c_re_2", "ssm_c_im_2")]
    return np.ascontiguousarray(np.concatenate(
        [gn(x["ssm_lambda_re_2"][0]), gn(x["ssm_lambda_im_2"][0]), gn(ldt)] + b + c
        + [np.tile(x["ssm_d_2"][0].reshape(32, 32).T, (4, 1))], axis=1))


def build(nc, order, arrays):
    D = {n: nc.dram_tensor(f"in_{n}", a, F32, kind="ExternalInput").ap() for n, a in arrays.items()}
    D["out"] = nc.dram_tensor("out_0", (8, 128, T), F32, kind="ExternalOutput").ap()
    with ExitStack() as ctx:
        k = Builder(nc, ctx, order)
        program(nc, ctx, k, D)
        if order is not None:
            with nc.Block() as block:
                k.emit(block)
    return k.used


def layout(x, order):
    t = lambda a: np.ascontiguousarray(a)
    return {
        "w": pack(order, matrices(x)),
        "xT": t(x["x"][0].T.reshape(8, 128, T)),
        "pT": t(x["p_2"][:, 0].transpose(0, 2, 1).reshape(2, 2, 128, T).transpose(0, 2, 1, 3)),
        "vecs": vectors(x),
        "consts": constants(),
        "rope": rope_tables(),
        "ssm": ssm_parameters(x),
    }


SHAPES = {"w": (1, 128, 1024), "xT": (8, 128, T), "pT": (2, 128, 2, T), "vecs": (128, NV), "consts": (128, NCC),
          "rope": (128, 2, T), "ssm": (128, NSC)}


def kernel(**inputs):
    import concourse.bacc as bacc
    from concourse.bass_utils import run_bass_kernel_spmd

    order = build(bacc.Bacc("TRN2", target_bir_lowering=False, num_devices=1, dynamic_dma_scratch_size=1024), None, SHAPES)
    x = {n: np.asarray(a) for n, a in inputs.items()}
    arrays = layout(x, order)
    nc = bacc.Bacc("TRN2", target_bir_lowering=False, num_devices=1, dynamic_dma_scratch_size=1024)
    build(nc, order, {n: a.shape for n, a in arrays.items()})
    r = run_bass_kernel_spmd(nc, [{f"in_{n}": a for n, a in arrays.items()}], core_ids=[0])
    out = r.results[0]["out_0"].reshape(1024, T)
    return np.ascontiguousarray(out.T).reshape(1, T, 1024)
```
